# Optimizing a Trainium2 kernel written in Bass

```python
import math
import jax, jax.numpy as jnp
from jax import lax
import numpy as np

D_MODEL = 1024
BATCH = 1
SEQ = 256
DEPTH = 2
DEC_BATCH = 8
DEC_SEQ = 8
PAST_LEN = 2048
PAGE_SIZE = 128

BRANCH_W = D_MODEL // 2
H_A = 4
DH_A = BRANCH_W // H_A
H_B = 4
DH_B = BRANCH_W // H_B
H_C = 4
DH_C = BRANCH_W // H_C
W_D = BRANCH_W
CONV_W = 3
N_BRANCH = 4
D_FF = 4 * D_MODEL
CHUNK = 64
ROPE_BASE = 10000.0
LN_EPS = 1e-5
NEG_BIG = -1e30
GATE_CLAMP = 1.0 - 1e-6
ALPHA = (2 * DEPTH) ** 0.25
BETA = (8 * DEPTH) ** -0.25
SPLIT_SIZES = (BRANCH_W,) * 4 + (H_A, H_A) + (BRANCH_W,) * 4 + (BRANCH_W,) * 4 + (BRANCH_W,) * 3
P_IN = 15 * BRANCH_W + 2 * H_A

kernel_name = 'hybrid_mlstm_ret_hgrn2_conv_step'

def _split_cols(z):
    parts, off = [], 0
    for s in SPLIT_SIZES:
        parts.append(z[..., off:off + s])
        off += s
    return parts

def _layer_norm(x, g, b):
    xf = x.astype(jnp.float32)
    mu = jnp.mean(xf, -1, keepdims=True)
    xc = xf - mu
    var = jnp.mean(jnp.square(xc), -1, keepdims=True)
    return xc * lax.rsqrt(var + LN_EPS) * g + b

def _head_rms(h, w):
    hn = h * lax.rsqrt(jnp.mean(jnp.square(h), -1, keepdims=True) + LN_EPS)
    return hn.reshape(h.shape[:2] + (-1,)) * w

def _head_ln(h, w):
    hc = h - jnp.mean(h, -1, keepdims=True)
    hn = hc * lax.rsqrt(jnp.mean(jnp.square(hc), -1, keepdims=True) + LN_EPS)
    return hn.reshape(h.shape[:2] + (-1,)) * w

def _rope(x, pos):
    half = x.shape[-1] // 2
    inv = ROPE_BASE ** (-jnp.arange(half, dtype=jnp.float32) / half)
    ang = pos[:, None] * inv[None, :]
    cos = jnp.cos(ang)[None, :, None, :]
    sin = jnp.sin(ang)[None, :, None, :]
    x1, x2 = x[..., :half], x[..., half:]
    return jnp.concatenate([x1 * cos - x2 * sin, x1 * sin + x2 * cos], -1)

def _to_chunks(a, c):
    b, t = a.shape[:2]
    return jnp.moveaxis(a.reshape((b, t // c, c) + a.shape[2:]), 1, 0)

def _from_chunks(a):
    nc, b, c = a.shape[:3]
    return jnp.moveaxis(a, 0, 1).reshape((b, nc * c) + a.shape[3:])

def _mlstm_chunked(q, k, v, ig, lf, C0, n0, m0):
    c = math.gcd(q.shape[1], CHUNK)
    xs = tuple(_to_chunks(a, c) for a in (q, k, v, ig, lf))
    causal = jnp.tril(jnp.ones((c, c), bool))

    def step(carry, inp):
        C, n, m = carry
        qc, kc, vc, ic, fc = inp
        b = jnp.swapaxes(jnp.cumsum(fc, axis=1), 1, 2)
        ic = jnp.swapaxes(ic, 1, 2)
        a = b + m[..., None]
        D = b[..., :, None] - b[..., None, :] + ic[..., None, :]
        D = jnp.where(causal, D, NEG_BIG)
        m_t = jnp.maximum(a, jnp.max(D, -1))
        w_inter = jnp.exp(a - m_t)
        s = jnp.einsum('bthd,bshd->bhts', qc, kc) * jnp.exp(D - m_t[..., None])
        num = (jnp.einsum('bhts,bshd->bthd', s, vc)
               + jnp.einsum('bthk,bhkv->bthv', qc, C) * jnp.swapaxes(w_inter, 1, 2)[..., None])
        den = jnp.sum(s, -1) + jnp.einsum('bthk,bhk->bht', qc, n) * w_inter
        den = jnp.swapaxes(jnp.maximum(jnp.abs(den), jnp.exp(-m_t)), 1, 2)
        h = num / den[..., None]
        bL = b[..., -1]
        g_last = bL[..., None] - b + ic
        m_new = jnp.maximum(bL + m, jnp.max(g_last, -1))
        w_s = jnp.exp(g_last - m_new[..., None])
        dec = jnp.exp(bL + m - m_new)
        C_new = dec[..., None, None] * C + jnp.einsum('bhs,bshk,bshv->bhkv', w_s, kc, vc)
        n_new = dec[..., None] * n + jnp.einsum('bhs,bshk->bhk', w_s, kc)
        return (C_new, n_new, m_new), h

    (C, n, m), hs = lax.scan(step, (C0, n0, m0), xs)
    return _from_chunks(hs), C, n, m

def _retention_chunked(q, k, v, log_gamma, S0):
    c = math.gcd(q.shape[1], CHUNK)
    xs = tuple(_to_chunks(a, c) for a in (q, k, v))
    idx = jnp.arange(c, dtype=jnp.float32)
    rel = idx[:, None] - idx[None, :]
    dec = jnp.where(rel >= 0, jnp.exp(log_gamma[:, None, None] * jnp.maximum(rel, 0.0)), 0.0)
    inter = jnp.swapaxes(jnp.exp(log_gamma[:, None] * (idx + 1.0)[None, :]), 0, 1)[None, :, :, None]
    to_end = jnp.exp(log_gamma[:, None] * (c - 1.0 - idx)[None, :])
    chunk_dec = jnp.exp(log_gamma * c)[None, :, None, None]

    def step(S, inp):
        qc, kc, vc = inp
        s = jnp.einsum('bthd,bshd->bhts', qc, kc) * dec
        o = jnp.einsum('bhts,bshv->bthv', s, vc) + jnp.einsum('bthk,bhkv->bthv', qc, S) * inter
        S_new = chunk_dec * S + jnp.einsum('hs,bshk,bshv->bhkv', to_end, kc, vc)
        return S_new, o

    S, os_ = lax.scan(step, S0, xs)
    return _from_chunks(os_), S

def _gla_chunked(q, k, v, g, S0):
    c = math.gcd(q.shape[1], CHUNK)
    xs = tuple(_to_chunks(a, c) for a in (q, k, v, g))
    causal = jnp.tril(jnp.ones((c, c), bool))[None, :, :, None, None]

    def step(S, inp):
        qc, kc, vc, gc = inp
        Bc = jnp.cumsum(gc, axis=1)
        diff = jnp.where(causal, Bc[:, :, None] - Bc[:, None, :], 0.0)
        wdec = jnp.where(causal, jnp.exp(diff), 0.0)
        A = jnp.einsum('bthk,bshk,btshk->bhts', qc, kc, wdec)
        o = jnp.einsum('bhts,bshv->bthv', A, vc) + jnp.einsum('bthk,bhkv->bthv', qc * jnp.exp(Bc), S)
        BL = Bc[:, -1]
        S_new = jnp.exp(BL)[..., None] * S + jnp.einsum('bshk,bshv->bhkv', kc * jnp.exp(BL[:, None] - Bc), vc)
        return S_new, o

    S, os_ = lax.scan(step, S0, xs)
    return _from_chunks(os_), S

def _short_conv(u, buf, w):
    t = u.shape[1]
    full = jnp.concatenate([buf.astype(u.dtype), u], axis=1)
    y = full[:, 0:t] * w[0]
    for j in range(1, CONV_W):
        y = y + full[:, j:j + t] * w[j]
    return y, full[:, -(CONV_W - 1):]

def _layer(x, pos, st, p, lb):
    (w_in, b_gate_a, norm_a, norm_b, norm_c, conv_w, w_branch, w_gate, b_gate,
     w_out, ln1_g, ln1_b, ln2_g, ln2_b, w_up, w_down) = p
    C0, n0, m0, Sr0, Sh0, buf0 = st
    f32 = jnp.float32
    bsz, t, _ = x.shape
    z = jnp.einsum('btd,dp->btp', x, w_in).astype(f32)
    (q_a, k_a, v_a, o_a, i_a, f_a, q_b, k_b, v_b, g_b,
     q_c, f_c, i_c, g_c, x_d, bg_d, cg_d) = _split_cols(z)
    heads = lambda a, h: a.reshape(bsz, t, h, -1)
    ig = i_a + b_gate_a[:H_A]
    lf = jax.nn.log_sigmoid(f_a + b_gate_a[H_A:])
    hA, C1, n1, m1 = _mlstm_chunked(heads(q_a, H_A), heads(k_a, H_A) * DH_A ** -0.5, heads(v_a, H_A),
                                    ig, lf, C0, n0, m0)
    yA = jax.nn.sigmoid(o_a) * _head_rms(hA, norm_a)
    log_gamma = jnp.log(1.0 - 2.0 ** (-5.0 - jnp.arange(H_B, dtype=f32)))
    qb = _rope(heads(q_b, H_B), pos)
    kb = _rope(heads(k_b, H_B), pos) * DH_B ** -0.5
    hB, Sr1 = _retention_chunked(qb, kb, heads(v_b, H_B), log_gamma, Sr0)
    yB = jax.nn.silu(g_b) * _head_ln(hB, norm_b)
    lbh = lb.reshape(H_C, DH_C)
    fc = heads(f_c, H_C)
    kc = (1.0 - lbh) * jax.nn.sigmoid(-fc)
    log_f = jnp.log1p(-jnp.minimum(kc, GATE_CLAMP))
    hC, Sh1 = _gla_chunked(jax.nn.silu(heads(q_c, H_C)), kc, heads(i_c, H_C), log_f, Sh0)
    yC = jax.nn.silu(g_c) * _head_rms(hC, norm_c)
    yconv, buf1 = _short_conv(cg_d * x_d, buf0, conv_w)
    yD = bg_d * yconv
    branches = jnp.stack([yA, yB, yC, yD], axis=2)
    proj = jnp.einsum('btnw,nwd->btnd', branches, w_branch)
    gates = jax.nn.sigmoid(jnp.einsum('btd,de->bte', x, w_gate) + b_gate).reshape(bsz, t, N_BRANCH, D_MODEL)
    mix = jnp.einsum('btd,de->bte', jnp.sum(gates * proj, axis=2), w_out)
    h = _layer_norm(ALPHA * x + mix, ln1_g, ln1_b)
    ff = jnp.einsum('btf,fd->btd', jnp.square(jax.nn.relu(jnp.einsum('btd,df->btf', h, w_up))), w_down)
    out = _layer_norm(ALPHA * h + ff, ln2_g, ln2_b).astype(x.dtype)
    return out, (C1, n1, m1, Sr1, Sh1, buf1)

def _trunk(x, pos, states, params, lb_all):
    outs = ([], [], [], [], [], [])
    for l in range(DEPTH):
        x, new = _layer(x, pos, tuple(s[l] for s in states), tuple(p[l] for p in params), lb_all[l])
        for lst, s in zip(outs, new):
            lst.append(s)
    return x, tuple(jnp.stack(lst) for lst in outs)

def setup_inputs(seed: int = 0) -> dict:
    key = jax.random.key(seed)
    ks = jax.random.split(key, 32)
    f32 = jnp.float32
    nrm = lambda k, s: jax.random.normal(k, s, f32)
    return {
        'x_prompt': nrm(ks[0], (BATCH, SEQ, D_MODEL)),
        'x_sample': nrm(ks[1], (DEC_BATCH, DEC_SEQ, D_MODEL)),
        'state_mlstm_C': 0.5 * nrm(ks[2], (DEPTH, DEC_BATCH, H_A, DH_A, DH_A)),
        'state_mlstm_n': 0.5 * nrm(ks[3], (DEPTH, DEC_BATCH, H_A, DH_A)),
        'state_mlstm_m': 2.0 + nrm(ks[4], (DEPTH, DEC_BATCH, H_A)),
        'state_ret': nrm(ks[5], (DEPTH, DEC_BATCH, H_B, DH_B, DH_B)),
        'state_hgrn': 0.5 * nrm(ks[6], (DEPTH, DEC_BATCH, H_C, DH_C, DH_C)),
        'state_conv': nrm(ks[7], (DEPTH, DEC_BATCH, CONV_W - 1, W_D)),
        'w_in': nrm(ks[8], (DEPTH, D_MODEL, P_IN)) * D_MODEL ** -0.5,
        'b_mlstm_gate': jnp.concatenate([0.1 * nrm(ks[9], (DEPTH, H_A)),
                                         jnp.linspace(3.0, 6.0, H_A, dtype=f32)[None, :] + 0.1 * nrm(ks[10], (DEPTH, H_A))], axis=-1),
        'norm_a': 1.0 + 0.05 * nrm(ks[11], (DEPTH, BRANCH_W)),
        'norm_b': 1.0 + 0.05 * nrm(ks[12], (DEPTH, BRANCH_W)),
        'norm_c': 1.0 + 0.05 * nrm(ks[13], (DEPTH, BRANCH_W)),
        'lb_c': 0.5 * nrm(ks[14], (DEPTH, H_C * DH_C)),
        'conv_w': nrm(ks[15], (DEPTH, CONV_W, W_D)) * CONV_W ** -0.5,
        'w_branch': nrm(ks[16], (DEPTH, N_BRANCH, BRANCH_W, D_MODEL)) * (BRANCH_W ** -0.5 * BETA),
        'w_gate': nrm(ks[17], (DEPTH, D_MODEL, N_BRANCH * D_MODEL)) * D_MODEL ** -0.5,
        'b_gate': 0.1 * nrm(ks[18], (DEPTH, N_BRANCH * D_MODEL)),
        'w_out': nrm(ks[19], (DEPTH, D_MODEL, D_MODEL)) * (D_MODEL ** -0.5 * BETA),
        'ln1_g': 1.0 + 0.05 * nrm(ks[20], (DEPTH, D_MODEL)),
        'ln1_b': 0.02 * nrm(ks[21], (DEPTH, D_MODEL)),
        'ln2_g': 1.0 + 0.05 * nrm(ks[22], (DEPTH, D_MODEL)),
        'ln2_b': 0.02 * nrm(ks[23], (DEPTH, D_MODEL)),
        'w_up': nrm(ks[24], (DEPTH, D_MODEL, D_FF)) * D_MODEL ** -0.5,
        'w_down': nrm(ks[25], (DEPTH, D_FF, D_MODEL)) * (D_FF ** -0.5 * BETA),
    }

def reference(x_prompt, x_sample, state_mlstm_C, state_mlstm_n, state_mlstm_m, state_ret, state_hgrn,
              state_conv, w_in, b_mlstm_gate, norm_a, norm_b, norm_c, lb_c, conv_w, w_branch, w_gate,
              b_gate, w_out, ln1_g, ln1_b, ln2_g, ln2_b, w_up, w_down):
    f32 = jnp.float32
    params = (w_in, b_mlstm_gate, norm_a, norm_b, norm_c, conv_w, w_branch, w_gate, b_gate,
              w_out, ln1_g, ln1_b, ln2_g, ln2_b, w_up, w_down)
    lb_sm = jax.nn.softmax(lb_c.astype(f32), axis=0)
    lb_all = jnp.cumsum(lb_sm, axis=0) - lb_sm[0]
    bp, tp = x_prompt.shape[:2]
    init = (jnp.zeros((DEPTH, bp, H_A, DH_A, DH_A), f32), jnp.zeros((DEPTH, bp, H_A, DH_A), f32),
            jnp.zeros((DEPTH, bp, H_A), f32), jnp.zeros((DEPTH, bp, H_B, DH_B, DH_B), f32),
            jnp.zeros((DEPTH, bp, H_C, DH_C, DH_C), f32), jnp.zeros((DEPTH, bp, CONV_W - 1, W_D), f32))
    pos_p = jnp.arange(tp, dtype=f32)
    y_prompt, p_states = _trunk(x_prompt, pos_p, init, params, lb_all)
    p_mlstm_C, p_mlstm_n, p_mlstm_m, p_ret, p_hgrn, p_conv = p_states
    ts = x_sample.shape[1]
    pos_s = PAST_LEN + jnp.arange(ts, dtype=f32)
    carried = (state_mlstm_C.astype(f32), state_mlstm_n.astype(f32), state_mlstm_m.astype(f32),
               state_ret.astype(f32), state_hgrn.astype(f32), state_conv.astype(f32))
    y_sample, s_states = _trunk(x_sample, pos_s, carried, params, lb_all)
    s_mlstm_C, s_mlstm_n, s_mlstm_m, s_ret, s_hgrn, s_conv = s_states
    return (y_prompt, y_sample, p_mlstm_C, p_mlstm_n, p_mlstm_m, p_ret, p_hgrn, p_conv,
            s_mlstm_C, s_mlstm_n, s_mlstm_m, s_ret, s_hgrn, s_conv)


_drawn_inputs = setup_inputs


def setup_inputs(seed=0):
    import zlib

    import numpy as np

    out = dict(_drawn_inputs(seed))
    spreads = {}
    factors = {'norm_a': 8.0, 'norm_b': 8.0, 'norm_c': 8.0, 'b_gate': 7.052}
    for name, (base, spread) in spreads.items():
        noise = np.random.default_rng([zlib.crc32(name.encode()), seed]).standard_normal(out[name].shape)
        drawn = base * np.exp(spread * noise) if base else spread * noise
        out[name] = __import__('jax').numpy.asarray(drawn.astype(out[name].dtype))
    for name, factor in factors.items():
        out[name] = (out[name] * factor).astype(out[name].dtype)
    return out
```

```python
from contextlib import ExitStack

import concourse.bass as bass
from concourse import mybir

ALU = mybir.AluOpType
ACT = mybir.ActivationFunctionType
F32 = mybir.dt.float32
F32R = mybir.dt.float32r
BF16 = mybir.dt.bfloat16
U32 = mybir.dt.uint32

P = 128
DEPTH, SEQ, NB, DS = 2, 256, 8, 8
NS = NB * DS
T = SEQ + NS
H = 4
DM = 1024
KD = DM // P
KF = 4 * KD
ALPHA = (2 * DEPTH) ** 0.25
KSCALE = float(P) ** -0.5
EPS = 1e-5
CLAMP = 1.0 - 1e-6
NEG = -1e30
SP4 = 448
TILES = ((0, P), (P, P), (SEQ, NS))
RING = 3
BANKS = 3
LEVELS = (4, 8, 16, 32, 64)

PN, PCW, PBG, PLN, PLB, PIF = 0, 12, 24, 56, 88, 92
NPAR = 100


def const_layout():
    at, off = {}, 0
    for name, n in (("ident", P), ("perm", P), ("tri", P), ("trib", P), ("diag", P), ("lv4", P), ("lv8", P),
                    ("lv16", P), ("lv32", P), ("lv64", P), ("dtab", H * 320), ("inter", H * NS),
                    ("toend", H * 2), ("seqmask", NB), ("vmask", H * NB), ("cos", T), ("sin", T),
                    ("scan", T), ("sel", H * P)):
        at[name] = (off, n)
        off += n
    return at, off


CONST_AT, NCONST = const_layout()


def slots_of_layer():
    s = []
    for kind in ("vC", "fC", "qC", "gC", "vA", "qA", "kA", "oA", "cD", "xD", "bD"):
        s += [("in", kind, h) for h in range(H)]

    def mixed(n):
        for half in range(2):
            for m in range(4):
                s.append(("gate", n, 4 * half + m))
            for m in range(2):
                s.append(("br", n, 4 * half + 2 * m))

    mixed("C")
    for kind in ("vB", "qB", "kB", "gB"):
        s += [("in", kind, h) for h in range(H)]
    mixed("A")
    mixed("B")
    mixed("D")
    s += [("out", m, 0) for m in range(KD)]
    s += [("up", m, 0) for m in range(KF)]
    s += [("down", m, q) for m in range(KD) for q in range(4)]
    return s


SLOTS = slots_of_layer()
NSLOT = len(SLOTS)
IN_COL = {"qA": 0, "kA": 512, "vA": 1024, "oA": 1536, "qB": 2056, "kB": 2568, "vB": 3080, "gB": 3592,
          "qC": 4104, "fC": 4616, "vC": 5128, "gC": 5640, "xD": 6152, "bD": 6664, "cD": 7176}
GATE_COL = 2048
BRANCH = {"A": 0, "B": 1, "C": 2, "D": 3}
Y_PAIR = {"C": 0, "A": 1, "B": 0, "D": 1}
MIXERS = "CAB"


def tiles_of_layer():
    t = []
    for kind, a, b in SLOTS:
        if kind == "br":
            t += [("br", a, b), ("br", a, b + 1)]
        elif kind != "down" or b == 3:
            t.append((kind, a, b))
    return t


def frees(tile):
    kind, a, _ = tile
    return "act" if kind == "in" and a in ("vC", "vA", "vB", "qA", "kA", "qB", "kB", "cD", "bD") else "dve"


LTILES = tiles_of_layer()
NTILE = len(LTILES)


def freed(engine, n):
    full, rest = divmod(n, NTILE)
    per = sum(frees(t) == engine for t in LTILES)
    return full * per + sum(frees(t) == engine for t in LTILES[:rest])


PHASES = {"vt": ("pe", "act"), "c_log": ("dve", "act", "dve"), "c_first": ("dve", "act", "dve"),
          "c_level": ("pe", "dve", "act", "dve"), "c_last": ("pe", "dve", "act", "dve"),
          "a_gate": ("pe", "dve", "act", "dve"), "a_cum": ("pe", "dve"), "a_row": ("pe", "dve", "act"),
          "a_score": ("pe", "act", "dve"), "b_rope": ("pe", "dve"), "b_score": ("pe", "dve"),
          "num": ("pe", "act", "dve", "act"), "b_mean": ("pe", "dve", "act"), "fin": ("pe", "act", "dve"),
          "conv": ("dve",)}
COST = {"vt": .3, "c_log": 2.6, "c_first": 3, "c_level": 1.9, "c_last": 2.5, "a_gate": .9, "a_cum": .2,
        "a_row": 1.6, "a_score": 1.0, "b_rope": .9, "b_score": .6, "num": 1.2, "b_mean": .5, "fin": 1.8,
        "conv": 1.3}


def schedule_of_layer():
    index = {s: i for i, s in enumerate(SLOTS)}
    last = lambda kind: index[("in", kind, H - 1)]
    chain = [("c_log", "C", 0, last("fC") + 1), ("c_first", "C", 0, last("qC") + 1)]
    chain += [("c_level", "C", i, 0) for i in range(len(LEVELS) + 1)] + [("c_last", "C", 0, last("gC") + 1)]
    for h in range(H):
        chain += [("num", "C", h, 0), ("fin", "C", h, 0)]
    chain += [("a_gate", "A", 0, last("oA") + 1), ("a_cum", "A", 0, 0), ("a_row", "A", 0, 0)]
    for h in range(H):
        chain += [("a_score", "A", h, 0), ("num", "A", h, 0), ("fin", "A", h, 0)]
    for h in range(H):
        chain += [("b_rope", "B", h, last("kB") + 1), ("b_score", "B", h, 0), ("num", "B", h, 0),
                  ("b_mean", "B", h, 0), ("fin", "B", h, last("gB") + 1)]
    chain += [("conv", "D", c, index[("br", "A", 6)] + 1) for c in range(H)]
    before = {index[("gate", n, 0)]: n for n in "CABD"}
    out, credit = [], 1.0
    for i, slot in enumerate(SLOTS):
        if i in before:
            while any(c[1] == before[i] for c in chain):
                out.append(("mix", *chain.pop(0)[:3]))
        out.append(("slot", i))
        back = SLOTS[i - 1] if i else ("", "", 0)
        if back[0] == "in" and back[1][0] == "v":
            out.append(("mix", "vt", back[1][1], back[2]))
            credit -= COST["vt"]
        credit = min(credit + 1, 1.0)
        while chain and chain[0][3] <= i and credit > 0:
            stage = chain.pop(0)
            out.append(("mix", *stage[:3]))
            credit -= COST[stage[0]]
            if PHASES[stage[0]][0] == "pe":
                break
    assert not chain
    return out


SCHEDULE = schedule_of_layer()


def phase_counts():
    done = {"pe": 0, "act": 0, "dve": 0}
    table = []
    last = None
    for item in SCHEDULE:
        if item[0] == "slot":
            table.append(None)
            continue
        rows = []
        for engine in PHASES[item[1]]:
            done[engine] += 1
            rows.append((engine, last, done[engine]))
            last = (engine, done[engine])
        table.append(rows)
    return table, done, last


PHASE_TABLE, PHASES_PER_LAYER, LAST_PHASE = phase_counts()


def mixer_end(n):
    return max(rows[-1][2] for item, rows in zip(SCHEDULE, PHASE_TABLE)
               if item[0] == "mix" and item[2] == n and item[1] in ("fin", "conv"))


def tiles_in(i):
    kind, _, b = SLOTS[i]
    return 2 if kind == "br" else int(kind != "down" or b == 3)


def slot_of_tile():
    return [i for i in range(NSLOT) for _ in range(tiles_in(i))]


TILE_SLOT = slot_of_tile()


def ends_norm(i):
    return {("out", KD - 1, 0): 0, ("down", KD - 1, 3): 1}.get(SLOTS[i])
HEADS_PER_LAYER = 3 * H


def trunk(nc, w, x, cst, par, ifw, st, n0, m0, cb, y_out, sp_out, ss_out, n_out, m_out, c_out):
    with ExitStack() as ctx:
        def sb(name, shape, dt=F32, where=ctx):
            return where.enter_context(nc.sbuf_tensor(name, shape, dt))

        def sem(name):
            return ctx.enter_context(nc.semaphore(name))

        xh = sb("xh", [P, KD, T], F32R)
        xl = sb("xl", [P, KD, T], F32R)
        raw = sb("raw", [P, RING, KD, P])
        whi = sb("whi", [P, RING, KD, P], F32R)
        wlo = sb("wlo", [P, RING, KD, P], F32R)
        with ExitStack() as early:
            zc = sb("zc", [P, 4, H, T], F32, early)
            vc = sb("vc", [P, H, 3, P], F32, early)
            za = sb("za", [P, 3, H, T], F32, early)
            va = sb("va", [P, H, 3, P], F32, early)
            ud = sb("ud", [P, H, SEQ + 2 + NB * (DS + 2)], F32, early)
            bd = sb("bd", [P, H, T], F32, early)
            yh = sb("yh", [P, 2, H, T], F32R, early)
            yl = sb("yl", [P, 2, H, T], F32R, early)
            vf = sb("vf", [P, 2, T], F32, early)
        ah = sb("ah", [P, KF, T], F32R)
        al = sb("al", [P, KF, T], F32R)
        pt = sb("pt", [P, H, SP4])
        mix = sb("mix", [P, KD, T])
        z12 = mix[:, :, :].rearrange("p (a h) t -> p a h t", a=2)
        gt = zc[:, 2, :, :]
        s0 = sb("s0", [P, 2, NB, P])
        ee = sb("ee", [P, SP4])
        vm = sb("vm", [NS, NB, P])
        kt = sb("kt", [P, 3, P])
        vw = sb("vw", [P, 2, P])
        pst = sb("pst", [P, 2, P])
        hh = sb("hh", [P, T])
        sq = sb("sq", [P, T])
        rs = sb("rs", [P, T])
        tt = sb("tt", [P, BANKS, T])
        qw = sb("qw", [P, H, NS])
        qn = sb("qn", [P, NS])
        dec = sb("dec", [P, H, NB])
        con = sb("con", [P, NCONST])
        ones = sb("ones", [P, 2, P])
        negb = sb("negb", [P, SP4], BF16)
        idb = sb("idb", [P, P], BF16)
        prm = sb("prm", [P, DEPTH, NPAR])
        nbg = sb("nbg", [P, DEPTH, KF])
        oml = sb("oml", [P, DEPTH, H])
        gw = sb("gw", [P, DEPTH, KD, 2 * H])
        n0s = sb("n0s", [P, DEPTH, H, NB])
        nou = sb("nou", [P, H, 1 + NB])
        m0s = sb("m0s", [H, DEPTH, NB])
        row = sb("row", [H, 2, T])
        wi = sb("wi", [H, NS])
        mou = sb("mou", [H, 1 + NB])
        cbs = sb("cbs", [P, DEPTH, H, NB, 2])
        cou = sb("cou", [P, H, 1 + NB, 2])
        iff = sb("iff", [P, 3, 2 * H])
        gb = sb("gb", [P, 3, 2 * H])
        af = sb("af", [P, 3, H])
        eps = sb("eps", [P, 1])
        gps = [ctx.enter_context(nc.psum_tensor(f"gps{i}", [P, 512], F32)) for i in range(BANKS)]
        xp = [ctx.enter_context(nc.psum_tensor(f"xp{i}", [P, 512], F32)) for i in range(5)]

        def c_(name, rows=P):
            off, n = CONST_AT[name]
            return con[0:rows, off:off + n]

        ident = c_("ident")

        const_in, x_in, small_in = sem("const_in"), sem("x_in"), sem("small_in")
        raw_in = [sem(f"raw_in{i}") for i in range(RING)]
        hi_done, lo_done, slot_done = sem("hi_done"), sem("lo_done"), sem("slot_done")
        tile_free = {"act": sem("tile_free_act"), "dve": sem("tile_free_dve")}
        act_half = sem("act_half")
        mix_done = {e: sem(f"mix_done_{e}") for e in ("pe", "act", "dve")}
        setup_dve, setup_act, setup_lb, setup_pool = sem("setup_dve"), sem("setup_act"), sem("setup_lb"), sem("setup_pool")
        x_hi, x_lo = sem("x_hi"), sem("x_lo")
        dve_chain, act_chain = sem("dve_chain"), sem("act_chain")
        mix_split = sem("mix_split")
        ln_mean, ln_center, ln_sq, ln_sqsum = sem("ln_mean"), sem("ln_center"), sem("ln_sq"), sem("ln_sqsum")
        ln_rstd, ln_scaled, y_ready = sem("ln_rstd"), sem("ln_scaled"), sem("y_ready")
        s_out, small_out, y_sent = sem("s_out"), sem("small_out"), sem("y_sent")
        s_in = [sem("s_in0"), sem("s_in1")]
        block = ctx.enter_context(nc.Block())

        def q_of(n, h):
            return (za if n == "A" else zc)[:, 0, h, :]

        def k_of(n, h):
            return (za if n == "A" else zc)[:, 1, h, :]

        def v_of(n, h, tile):
            rows = TILES[tile][1]
            return (va if n == "A" else vc)[0:rows, h, tile, :]

        def state_of(n, h):
            return H * MIXERS.index(n) + h

        def blocks(ap, lo, hi, m):
            return ap[:, :, lo:hi].rearrange("p h (b two m) -> p h b two m", two=2, m=m)

        def per_seq(ap):
            return ap.rearrange("p (b t) -> p b t", t=DS)

        def sample_u(h):
            return ud[:, h, SEQ + 2:SEQ + 2 + NB * (DS + 2)].rearrange("p (b t) -> p b t", t=DS + 2)

        def follow(eng, layer, before):
            if before is not None:
                eng.wait_ge(mix_done[before[0]], layer * PHASES_PER_LAYER[before[0]] + before[1])
            elif layer:
                eng.wait_ge(mix_done[LAST_PHASE[0]], layer * PHASES_PER_LAYER[LAST_PHASE[0]])

        def settled(eng, layer, tile, i):
            n = layer * NTILE + tile - tiles_in(i)
            for e in ("act", "dve"):
                if freed(e, n):
                    eng.wait_ge(tile_free[e], freed(e, n))

        @block.sync
        def _(sp):
            sp.dma_start(mix[:, :, :], x).then_inc(x_in, 16)
            sp.dma_start(raw[:, 0, :, :], w[0, 0]).then_inc(raw_in[0], 16)
            sp.dma_start(con[:, :], cst[:, 0:NCONST]).then_inc(const_in, 16)
            sp.dma_start(ee[:, :], cst[:, NCONST:NCONST + SP4]).then_inc(const_in, 16)
            sp.dma_start(prm[:, :, :], par).then_inc(const_in, 16)
            sp.dma_start(raw[:, 1, :, :], w[0, 1]).then_inc(raw_in[1], 16)
            sp.dma_start(raw[:, 2, :, :], w[0, 2]).then_inc(raw_in[2], 16)
            for dst, src in ((gw[:, :, :, :], ifw), (n0s[:, :, :, :], n0), (m0s[:, :, :], m0),
                             (cbs[:, :, :, :, :], cb)):
                sp.dma_start(dst, src).then_inc(small_in, 16)
            for j in range(2):
                sp.dma_start(s0[:, j, :, :], st[0, j]).then_inc(s_in[j], 16)
            sent = 0
            for layer in range(DEPTH):
                reload = None
                for item, rows in zip(SCHEDULE, PHASE_TABLE):
                    if item[0] == "slot":
                        c = layer * NSLOT + item[1] + RING
                        if c < DEPTH * NSLOT:
                            sp.wait_ge(lo_done, c - RING + 1)
                            sp.dma_start(raw[:, c % RING, :, :], w[c // NSLOT, c % NSLOT]).then_inc(raw_in[c % RING], 16)
                        if reload is not None:
                            j = layer * HEADS_PER_LAYER + reload
                            reload = None
                            if j < DEPTH * HEADS_PER_LAYER:
                                sp.wait_ge(s_out, 32 * (j - 1))
                                sp.dma_start(s0[:, j % 2, :, :],
                                             st[j // HEADS_PER_LAYER, j % HEADS_PER_LAYER]).then_inc(s_in[j % 2], 16)
                        continue
                    _, stage, n, h = item
                    if stage == "fin":
                        k = layer * PHASES_PER_LAYER["dve"] + rows[-1][2]
                        sp.wait_ge(mix_done["dve"], k)
                        j = state_of(n, h)
                        sp.dma_start(ss_out[layer, j], s0[:, j % 2, :, :]).then_inc(s_out, 16)
                        sp.dma_start(sp_out[layer, j], pst[:, j % 2, :]).then_inc(s_out, 16)
                        reload = j + 2
                        if n == "A" and h == H - 1:
                            sp.dma_start(n_out[layer], nou[:, :, :]).then_inc(small_out, 16)
                            sp.dma_start(m_out[layer], mou[:, :]).then_inc(small_out, 16)
                    if stage == "conv" and h == H - 1:
                        sp.wait_ge(mix_done["dve"], layer * PHASES_PER_LAYER["dve"] + rows[-1][2])
                        sp.dma_start(c_out[layer], cou[:, :, :, :]).then_inc(small_out, 16)
            for m in range(KD):
                sp.wait_ge(y_ready, m + 1)
                sp.dma_start(y_out[:, m, :], mix[:, m, :]).then_inc(y_sent, 16)
            sp.wait_ge(y_sent, 16 * KD)
            sp.wait_ge(s_out, 32 * DEPTH * HEADS_PER_LAYER)
            sp.wait_ge(small_out, 16 * 3 * DEPTH)

        @block.gpsimd
        def _(pool):
            nc.gpsimd.memset(ones[:, 0, :], 1.0)
            nc.gpsimd.memset(ones[:, 1, :], 1.0 / P)
            nc.gpsimd.memset(pt[:, :, :], 0.0)
            nc.gpsimd.memset(iff[:, :, :], 0.0).then_inc(setup_pool, 1)
            for c in range(DEPTH * NSLOT):
                pool.wait_ge(hi_done, c + 1)
                nc.gpsimd.tensor_tensor(wlo[:, c % RING, :, :], raw[:, c % RING, :, :],
                                        whi[:, c % RING, :, :].bitcast(F32), ALU.subtract).then_inc(lo_done, 1)

        @block.scalar
        def _(act):
            nc.scalar.preload_act_table_set("natural_log_exp_and_others")
            chain = [0]

            def link(ins):
                chain[0] += 1
                ins.then_inc(act_chain, 1)
                act.wait_ge(act_chain, chain[0])

            act.wait_ge(x_in, 16)
            for k in range(KD):
                nc.scalar.activation(xh[:, k, :], mix[:, k, :], ACT.Copy).then_inc(x_hi, 1)
            act.wait_ge(setup_lb, 1)
            nc.scalar.activation(oml[:, 1, :], oml[:, 0, :], ACT.Exp).then_inc(setup_act, 1)

            def split_hi(c):
                if c >= DEPTH * NSLOT:
                    return
                act.wait_ge(raw_in[c % RING], 16 * (c // RING + 1))
                if c >= RING:
                    act.wait_ge(slot_done, c - RING + 1)
                nc.scalar.activation(whi[:, c % RING, :, :], raw[:, c % RING, :, :], ACT.Copy).then_inc(hi_done, 1)

            def evict(layer, i):
                g = layer * NTILE + i
                kind, a, b = LTILES[i]
                ps = gps[g % BANKS][:, 0:T]
                t = tt[:, g % BANKS, :]
                if kind in ("br", "out", "down") or a == "xD":
                    return
                act.wait_ge(slot_done, layer * NSLOT + TILE_SLOT[i] + 1)
                free, half = tile_free["act"], act_half
                if kind == "up":
                    nc.scalar.activation(t, ps, ACT.Relu).then_inc(half, 1)
                elif kind == "gate":
                    j = KD * BRANCH[a] + b
                    nc.scalar.activation(t, ps, ACT.Exp, scale=-1.0, bias=nbg[:, layer, j:j + 1]).then_inc(half, 1)
                elif a[0] == "v":
                    nc.scalar.activation(vf[:, b % 2, :], ps, ACT.Copy).then_inc(free, 1)
                elif a in ("qA", "kA", "qB", "kB"):
                    dst = (q_of if a[0] == "q" else k_of)(a[1], b)
                    nc.scalar.activation(dst, ps, ACT.Copy, scale=KSCALE if a[0] == "k" else 1.0).then_inc(free, 1)
                elif a in ("cD", "bD"):
                    nc.scalar.activation(bd[:, b, :], ps, ACT.Copy).then_inc(free, 1)
                else:
                    nc.scalar.activation(t, ps, ACT.Exp, scale=1.0 if a == "fC" else -1.0).then_inc(half, 1)

            def phase(stage, n, h, k, layer, done):
                if stage == "vt":
                    v = va if n == "A" else vc
                    nc.scalar.activation(v[:, h, 0:2, :], xp[4][:, 0:2 * P].rearrange("p (a c) -> p a c", a=2), ACT.Copy)
                    done(nc.scalar.activation(v[0:NS, h, 2, :], xp[4][0:NS, 2 * P:3 * P], ACT.Copy))
                elif stage == "c_log":
                    done(nc.scalar.activation(z12[:, 0, :, :], z12[:, 0, :, :], ACT.Ln, scale=-1.0, bias=1.0))
                elif stage == "c_first":
                    nc.scalar.activation(z12[:, 1, :, :], z12[:, 0, :, :], ACT.Exp, scale=-1.0)
                    done(nc.scalar.activation(z12[:, 0, :, :], z12[:, 0, :, :], ACT.Exp))
                elif stage == "c_level":
                    hi = T if LEVELS[h:] and LEVELS[h] == DS // 2 else SEQ
                    done(nc.scalar.activation(z12[:, 0, :, 0:hi], z12[:, 0, :, 0:hi], ACT.Exp))
                elif stage == "c_last":
                    nc.scalar.activation(z12[:, 0, :, :], z12[:, 0, :, :], ACT.Exp)
                    nc.scalar.activation(qw[:, :, :], zc[:, 2, :, SEQ:T], ACT.Exp)
                    done(nc.scalar.activation(dec[:, :, :], zc[:, 2, :, SEQ + DS - 1:T:DS], ACT.Exp))
                elif stage == "a_gate":
                    link(nc.scalar.activation(af[:, :, :], iff[:, :, H:2 * H], ACT.Abs))
                    link(nc.scalar.activation(af[:, :, :], af[:, :, :], ACT.Exp, scale=-1.0))
                    done(nc.scalar.activation(af[:, :, :], af[:, :, :], ACT.Ln, bias=1.0))
                elif stage == "a_row":
                    nc.scalar.activation(row[:, 0, :], row[:, 0, :], ACT.Exp, scale=-1.0)
                    done(nc.scalar.activation(wi[:, :], wi[:, :], ACT.Exp))
                elif stage == "a_score":
                    nc.scalar.activation(ee[:, 0:256], xp[0][:, 0:256], ACT.Exp, bias=gb[:, 0, h:h + 1])
                    nc.scalar.activation(ee[:, 256:384], xp[0][:, 256:384], ACT.Exp, bias=gb[:, 1, h:h + 1])
                    done(nc.scalar.activation(ee[0:NS, 384:SP4], xp[0][0:NS, 384:SP4], ACT.Exp, bias=gb[0:NS, 2, h:h + 1]))
                elif stage == "num" and k == 1:
                    nc.scalar.activation(kt[:, 0:2, :], xp[0][:, 0:2 * P].rearrange("p (a c) -> p a c", a=2), ACT.Copy)
                    nc.scalar.activation(kt[0:NS, 2, :], xp[0][0:NS, 2 * P:3 * P], ACT.Copy)
                    if n == "A":
                        done(nc.scalar.activation(rs[:, :], xp[4][:, 0:T], ACT.Abs))
                    else:
                        done(nc.scalar.activation(hh[:, :], xp[3][:, 0:T], ACT.Copy))
                elif stage == "num":
                    done(nc.scalar.activation(sq[:, :], hh[:, :], ACT.Square))
                elif stage == "b_mean":
                    done(nc.scalar.activation(sq[:, :], hh[:, :], ACT.Square))
                elif stage == "fin":
                    link(nc.scalar.activation(rs[:, :], xp[4][:, 0:T], ACT.Ln, scale=1.0 / P, bias=eps[:, 0:1]))
                    done(nc.scalar.activation(rs[:, :], rs[:, :], ACT.Exp, scale=-0.5))

            def layer_norm(layer, which):
                q = 2 * layer + which
                for m in range(KD):
                    e = KD * q + m
                    act.wait_ge(ln_center, e + 1)
                    if m >= BANKS:
                        act.wait_ge(ln_sqsum, e - BANKS + 1)
                    nc.scalar.activation(tt[:, m % BANKS, :], mix[:, m, :], ACT.Square).then_inc(ln_sq, 1)
                act.wait_ge(ln_sqsum, KD * (q + 1))
                link(nc.scalar.activation(rs[:, :], xp[1][:, 0:T], ACT.Ln, scale=1.0 / DM, bias=eps[:, 0:1]))
                nc.scalar.activation(rs[:, :], rs[:, :], ACT.Exp, scale=-0.5).then_inc(ln_rstd, 1)
                for m in range(KD):
                    act.wait_ge(ln_scaled, KD * q + m + 1)
                    bias = prm[:, layer, PLN + 16 * which + 8 + m:PLN + 16 * which + 9 + m]
                    if q == 2 * DEPTH - 1:
                        nc.scalar.activation(mix[:, m, :], mix[:, m, :], ACT.Identity, bias=bias).then_inc(y_ready, 1)
                    else:
                        nc.scalar.activation(xh[:, m, :], mix[:, m, :], ACT.Identity, bias=bias).then_inc(x_hi, 1)

            for c in range(RING - 1):
                split_hi(c)
            act.wait_ge(setup_dve, 1)
            for layer in range(DEPTH):
                tile = 0
                for item, rows in zip(SCHEDULE, PHASE_TABLE):
                    if item[0] == "slot":
                        slot_i = item[1]
                        split_hi(layer * NSLOT + item[1] + RING - 1)
                        for _ in range(tiles_in(item[1])):
                            evict(layer, tile)
                            tile += 1
                        if ends_norm(item[1]) is not None:
                            layer_norm(layer, ends_norm(item[1]))
                        continue
                    for k, (engine, before, _) in enumerate(rows):
                        if engine != "act":
                            continue
                        follow(act, layer, before)
                        if k == 0:
                            settled(act, layer, tile, slot_i)
                        phase(*item[1:], k, layer, lambda ins: ins.then_inc(mix_done["act"], 1))

        @block.vector
        def _(dve):
            V = nc.vector
            chain = [0]

            def link(ins):
                chain[0] += 1
                ins.then_inc(dve_chain, 1)
                dve.wait_ge(dve_chain, chain[0])

            for k in range(KD):
                dve.wait_ge(x_hi, k + 1)
                V.tensor_tensor(xl[:, k, :], mix[:, k, :], xh[:, k, :].bitcast(F32), ALU.subtract).then_inc(x_lo, 1)
            dve.wait_ge(const_in, 48)
            V.tensor_copy(negb[:, :], ee[:, :])
            V.tensor_copy(idb[:, :], ident)
            V.memset(eps[:, :], EPS)
            V.tensor_tensor(oml[:, 0, :], prm[:, 1, PLB:PLB + H], prm[:, 0, PLB:PLB + H], ALU.subtract).then_inc(setup_lb, 1)
            dve.wait_ge(setup_act, 1)
            link(V.tensor_scalar_add(oml[:, 1, :], oml[:, 1, :], 1.0))
            link(V.reciprocal(oml[:, 1, :], oml[:, 1, :]))
            V.memset(oml[:, 0, :], 1.0)
            V.tensor_scalar(nbg[:, :, :], prm[:, :, PBG:PBG + KF], -1.0, None, ALU.mult).then_inc(setup_dve, 1)
            dve.wait_ge(setup_dve, 1)
            dve.wait_ge(small_in, 64)

            def evict(layer, i):
                g = layer * NTILE + i
                kind, a, b = LTILES[i]
                if frees(LTILES[i]) != "dve":
                    return
                ps = gps[g % BANKS][:, 0:T]
                t = tt[:, g % BANKS, :]
                free = tile_free["dve"]
                if kind in ("br", "out", "down") or a == "xD":
                    dve.wait_ge(slot_done, layer * NSLOT + TILE_SLOT[i] + 1)
                else:
                    halves[0] += 1
                    dve.wait_ge(act_half, halves[0])
                if kind == "up":
                    link(V.tensor_tensor(t, t, t, ALU.mult))
                    link(V.tensor_copy(ah[:, a, :], t))
                    V.tensor_tensor(al[:, a, :], t, ah[:, a, :].bitcast(F32), ALU.subtract).then_inc(free, 1)
                elif kind in ("out", "down"):
                    link(V.scalar_tensor_tensor(out=mix[:, a, :], in0=xh[:, a, :].bitcast(F32), scalar=ALPHA, in1=ps,
                                                op0=ALU.mult, op1=ALU.add))
                    V.scalar_tensor_tensor(out=mix[:, a, :], in0=xl[:, a, :].bitcast(F32), scalar=ALPHA,
                                           in1=mix[:, a, :], op0=ALU.mult, op1=ALU.add).then_inc(free, 1)
                elif kind == "gate":
                    link(V.tensor_scalar_add(t, t, 1.0))
                    V.reciprocal(gt[:, b % 4, :], t).then_inc(free, 1)
                elif kind == "br":
                    if a == "C":
                        V.tensor_tensor(mix[:, b, :], ps, gt[:, b % 4, :], ALU.mult).then_inc(free, 1)
                    else:
                        link(V.tensor_tensor(t, ps, gt[:, b % 4, :], ALU.mult))
                        V.tensor_tensor(mix[:, b, :], mix[:, b, :], t, ALU.add).then_inc(free, 1)
                elif a == "xD":
                    V.memset(ud[:, b, 0:2], 0.0)
                    V.tensor_tensor(ud[:, b, 2:2 + SEQ], ps[:, 0:SEQ], bd[:, b, 0:SEQ], ALU.mult)
                    V.tensor_copy(sample_u(b)[:, :, 0:2], cbs[:, layer, b, :, :])
                    V.tensor_tensor(sample_u(b)[:, :, 2:2 + DS], per_seq(ps[:, SEQ:T]), per_seq(bd[:, b, SEQ:T]),
                                    ALU.mult).then_inc(free, 1)
                else:
                    link(V.tensor_scalar_add(t, t, 1.0))
                    if a == "oA":
                        V.reciprocal(za[:, 2, b, :], t).then_inc(free, 1)
                        return
                    link(V.reciprocal(t, t))
                    if a == "fC":
                        V.tensor_scalar(zc[:, 1, b, :], t, oml[:, layer, b:b + 1], None, ALU.mult).then_inc(free, 1)
                    else:
                        V.tensor_tensor(zc[:, 0 if a == "qC" else 3, b, :], ps, t, ALU.mult).then_inc(free, 1)

            def split_mix():
                for m in range(KD):
                    V.tensor_copy(ah[:, m, :], mix[:, m, :]).then_inc(mix_split, 1)
                    splits[0] += 1
                    dve.wait_ge(mix_split, splits[0])
                    V.tensor_tensor(al[:, m, :], mix[:, m, :], ah[:, m, :].bitcast(F32), ALU.subtract).then_inc(mix_split, 1)
                    splits[0] += 1

            def spans(m):
                return [(0, SEQ)] + ([(SEQ, T)] if m == DS // 2 else [])

            def distances(m):
                for lo, hi in spans(m):
                    b = blocks(zc[:, 2, :, :], lo, hi, m)
                    z = blocks(z12[:, 0, :, :], lo, hi, m)
                    mid = b[:, :, :, 0, m - 1:m].to_broadcast([P, H, (hi - lo) // (2 * m), m])
                    V.tensor_tensor(z[:, :, :, 0, :], mid, b[:, :, :, 0, :], ALU.subtract)
                    last = V.tensor_tensor(z[:, :, :, 1, :], b[:, :, :, 1, :], mid, ALU.subtract)
                return last

            def apply_qk(m):
                for lo, hi in spans(m):
                    z = blocks(z12[:, 0, :, :], lo, hi, m)
                    q = blocks(zc[:, 0, :, :], lo, hi, m)
                    k = blocks(zc[:, 1, :, :], lo, hi, m)
                    V.tensor_tensor(z[:, :, :, 0, :], z[:, :, :, 0, :], k[:, :, :, 0, :], ALU.mult)
                    last = V.tensor_tensor(z[:, :, :, 1, :], z[:, :, :, 1, :], q[:, :, :, 1, :], ALU.mult)
                return last

            def take(name, sample):
                mask = c_(name).bitcast(U32)
                for tile, col in ((0, 0), (1, 256)):
                    V.copy_predicated(pt[:, :, col:col + P], mask.unsqueeze(1).to_broadcast([P, H, P]),
                                      xp[tile][:, :].rearrange("p (h t) -> p h t", h=H))
                if sample:
                    V.copy_predicated(pt[0:NS, :, 384:SP4], mask[0:NS, 0:NS].unsqueeze(1).to_broadcast([NS, H, NS]),
                                      xp[2][0:NS, 0:H * NS].rearrange("p (h t) -> p h t", h=H))

            def phase(stage, n, h, k, layer, done):
                if stage == "c_log" and k == 0:
                    done(V.tensor_scalar(z12[:, 0, :, :], zc[:, 1, :, :], CLAMP, None, ALU.min))
                elif stage == "c_log":
                    for hd in range(H):
                        last = V.tensor_tensor_scan(zc[:, 2, hd, :], c_("scan"), z12[:, 0, hd, :], 0.0, ALU.mult, ALU.add)
                    done(last)
                elif stage == "c_first" and k == 0:
                    b = zc[:, 2, :, :].rearrange("p h (b m) -> p (h b) m", m=4)
                    z = z12[:, 0, :, :].rearrange("p h (b m) -> p (h b) m", m=4)
                    done(V.tensor_tensor(z, b, b[:, :, 0:1].to_broadcast([P, H * T // 4, 4]), ALU.subtract))
                elif stage == "c_first":
                    V.tensor_tensor(z12[:, 0, :, :], z12[:, 0, :, :], zc[:, 0, :, :], ALU.mult)
                    done(V.tensor_tensor(z12[:, 1, :, :], z12[:, 1, :, :], zc[:, 1, :, :], ALU.mult))
                elif stage == "c_level" and k == 1:
                    take("diag" if h == 0 else f"lv{LEVELS[h - 1]}", h <= 1)
                    done(distances((LEVELS + (P,))[h]))
                elif stage == "c_level":
                    done(apply_qk((LEVELS + (P,))[h]))
                elif stage == "c_last" and k == 1:
                    V.tensor_copy(pt[:, :, P:2 * P], xp[0][:, :].rearrange("p (h t) -> p h t", h=H))
                    b = zc[:, 2, :, :]
                    for hd in range(H):
                        V.tensor_tensor(z12[:, 0, hd, 0:SEQ], b[:, hd, SEQ - 1:SEQ].to_broadcast([P, SEQ]),
                                        b[:, hd, 0:SEQ], ALU.subtract)
                        s = per_seq(b[:, hd, SEQ:T])
                        last = V.tensor_tensor(per_seq(z12[:, 0, hd, SEQ:T]), s[:, :, DS - 1:DS].to_broadcast([P, NB, DS]),
                                               s, ALU.subtract)
                    done(last)
                elif stage == "c_last":
                    V.tensor_tensor(z12[:, 0, :, :], z12[:, 0, :, :], zc[:, 1, :, :], ALU.mult)
                    done(V.tensor_tensor(qw[:, :, :], qw[:, :, :], zc[:, 0, :, SEQ:T], ALU.mult))
                elif stage == "a_gate" and k == 1:
                    bias = prm[:, layer, PIF:PIF + 2 * H]
                    V.tensor_tensor(iff[:, 0:2, :], xp[0][:, 0:16].rearrange("p (a c) -> p a c", a=2),
                                    bias.unsqueeze(1).to_broadcast([P, 2, 2 * H]), ALU.add)
                    done(V.tensor_tensor(iff[0:NS, 2, :], xp[0][0:NS, 16:24], bias[0:NS, :], ALU.add))
                elif stage == "a_gate":
                    done(V.scalar_tensor_tensor(out=af[:, :, :], in0=iff[:, :, H:2 * H], scalar=0.0, in1=af[:, :, :],
                                                op0=ALU.min, op1=ALU.subtract))
                elif stage == "a_cum":
                    b = xp[1][:, 0:12].rearrange("p (a c) -> p a c", a=3)
                    V.tensor_tensor(gb[:, :, 0:H], iff[:, :, 0:H], b, ALU.subtract)
                    done(V.tensor_copy(gb[:, :, H:2 * H], b))
                elif stage == "a_row":
                    link(V.tensor_copy(row[:, 0, :], xp[2][0:H, 0:T]))
                    V.tensor_tensor_scan(row[:, 1, 0:SEQ], row[:, 0, 0:SEQ], row[:, 0, 0:SEQ], 0.0, ALU.max, ALU.max)
                    for b in range(NB):
                        s = slice(SEQ + b * DS, SEQ + (b + 1) * DS)
                        last = V.tensor_tensor_scan(row[:, 1, s], row[:, 0, s], row[:, 0, s], m0s[:, layer, b:b + 1],
                                                    ALU.max, ALU.max)
                    link(last)
                    if layer:
                        dve.wait_ge(small_out, 16 * 3 * layer)
                    link(V.tensor_tensor(row[:, 0, :], row[:, 1, :], xp[3][0:H, 0:T], ALU.add))
                    V.tensor_copy(mou[:, 0:1], row[:, 0, SEQ - 1:SEQ])
                    V.tensor_copy(mou[:, 1:1 + NB], row[:, 0, SEQ + DS - 1:T:DS])
                    link(V.tensor_tensor(per_seq(wi[:, :]), m0s[:, layer, :].unsqueeze(2).to_broadcast([H, NB, DS]),
                                         per_seq(row[:, 1, SEQ:T]), ALU.subtract))
                    done(V.tensor_scalar(row[:, 1, :], row[:, 1, :], -1.0, None, ALU.mult))
                elif stage == "a_score":
                    V.tensor_tensor(pt[:, h, 0:384], xp[1][:, 0:384], ee[:, 0:384], ALU.mult)
                    V.tensor_tensor(pt[0:NS, h, 384:SP4], xp[1][0:NS, 384:SP4], ee[0:NS, 384:SP4], ALU.mult)
                    V.tensor_copy(dec[:, h, :], xp[2][:, T + DS - 1:384:DS])
                    link(V.tensor_tensor(qw[:, h, :], xp[2][:, T:384], za[:, 0, h, SEQ:T], ALU.mult))
                    done(V.tensor_tensor(per_seq(qn[:, :]), per_seq(qw[:, h, :]),
                                         n0s[:, layer, h, :].unsqueeze(2).to_broadcast([P, NB, DS]), ALU.mult))
                elif stage == "b_rope":
                    for i in range(2):
                        V.tensor_tensor((sq, rs)[i][:, :], xp[i][:, 0:T], c_("sin"), ALU.mult)
                        last = V.tensor_tensor(zc[:, i, h, :], zc[:, i, h, :], c_("cos"), ALU.mult)
                    link(last)
                    for i in range(2):
                        last = V.tensor_tensor(zc[:, i, h, :], zc[:, i, h, :], (sq, rs)[i][:, :], ALU.add)
                    done(last)
                elif stage == "b_score":
                    d = c_("dtab").rearrange("p (h c) -> p h c", h=H)[:, h, :]
                    V.tensor_tensor(pt[:, h, 0:256], xp[1][:, 0:256], d[:, 0:256], ALU.mult)
                    V.tensor_tensor(pt[:, h, 256:384], xp[1][:, 256:384], d[:, 0:128], ALU.mult)
                    V.tensor_tensor(pt[0:NS, h, 384:SP4], xp[1][0:NS, 384:SP4], d[0:NS, 256:320], ALU.mult)
                    done(V.tensor_tensor(qw[:, h, :], zc[:, 0, h, SEQ:T],
                                         c_("inter")[:, h * NS:(h + 1) * NS], ALU.mult))
                elif stage == "num":
                    if n == "A":
                        link(V.tensor_tensor(rs[:, :], rs[:, :], xp[2][:, 0:T], ALU.max))
                        link(V.reciprocal(rs[:, :], rs[:, :]))
                        link(V.tensor_tensor(hh[:, :], xp[3][:, 0:T], rs[:, :], ALU.mult))
                        ends, mask = (ee[:, 255:256], ee[:, 383:384]), ee[0:NS, 384 + DS - 1:SP4:DS]
                    elif n == "B":
                        toend = c_("toend")[:, 2 * h:2 * h + 2]
                        ends, mask = (toend[:, 0:1], toend[:, 1:2]), c_("vmask", NS)[:, h * NB:(h + 1) * NB]
                    else:
                        ends, mask = None, c_("seqmask", NS)
                    if ends:
                        for i in range(2):
                            V.tensor_scalar(vw[:, i, :], v_of(n, h, i), ends[i], None, ALU.mult)
                    done(V.tensor_tensor(vm[:, :, :], v_of(n, h, 2).unsqueeze(1).to_broadcast([NS, NB, P]),
                                         mask.unsqueeze(2).to_broadcast([NS, NB, P]), ALU.mult))
                elif stage == "b_mean":
                    done(V.tensor_tensor(hh[:, :], hh[:, :], xp[4][:, 0:T], ALU.subtract))
                elif stage == "fin":
                    w_ = prm[:, layer, PN + 4 * "ABC".index(n) + h:PN + 4 * "ABC".index(n) + h + 1]
                    link(V.scalar_tensor_tensor(out=hh[:, :], in0=hh[:, :], scalar=w_, in1=rs[:, :],
                                                op0=ALU.mult, op1=ALU.mult))
                    gate = za[:, 2, h, :] if n == "A" else zc[:, 3, h, :]
                    link(V.tensor_tensor(hh[:, :], hh[:, :], gate, ALU.mult))
                    split_y(n, h, hh[:, :])
                    j = state_of(n, h)
                    V.tensor_copy(pst[:, j % 2, :], xp[0][:, 0:P])
                    if n == "A":
                        V.tensor_copy(nou[:, h, 0:1], xp[0][:, P:P + 1])
                        link(V.tensor_tensor(nou[:, h, 1:1 + NB], n0s[:, layer, h, :], dec[:, h, :], ALU.mult))
                        V.tensor_tensor(nou[:, h, 1:1 + NB], nou[:, h, 1:1 + NB], xp[0][:, P + 1:P + 1 + NB], ALU.add)
                    for b in range(NB):
                        new = xp[1 + b // 4][:, (b % 4) * P:(b % 4 + 1) * P]
                        keep = (1.0 - 2.0 ** (-5 - h)) ** DS if n == "B" else dec[:, h, b:b + 1]
                        last = V.scalar_tensor_tensor(out=s0[:, j % 2, b, :], in0=s0[:, j % 2, b, :], scalar=keep,
                                                      in1=new, op0=ALU.mult, op1=ALU.add)
                    done(last)
                elif stage == "conv":
                    if layer and h == 0:
                        dve.wait_ge(small_out, 16 * 3 * layer)
                    tap = lambda j: prm[:, layer, PCW + 4 * j + h:PCW + 4 * j + h + 1]
                    up, us = ud[:, h, 0:SEQ + 2], sample_u(h)
                    yp, ys = hh[:, 0:SEQ], per_seq(hh[:, SEQ:T])
                    V.tensor_scalar(yp, up[:, 0:SEQ], tap(0), None, ALU.mult)
                    link(V.tensor_scalar(ys, us[:, :, 0:DS], tap(0), None, ALU.mult))
                    for j in (1, 2):
                        V.scalar_tensor_tensor(out=yp, in0=up[:, j:j + SEQ], scalar=tap(j), in1=yp, op0=ALU.mult, op1=ALU.add)
                        link(V.scalar_tensor_tensor(out=ys, in0=us[:, :, j:j + DS], scalar=tap(j), in1=ys,
                                                    op0=ALU.mult, op1=ALU.add))
                    link(V.tensor_tensor(hh[:, :], hh[:, :], bd[:, h, :], ALU.mult))
                    split_y("D", h, hh[:, :])
                    V.tensor_copy(cou[:, h, 0, :], up[:, SEQ:SEQ + 2])
                    done(V.tensor_copy(cou[:, h, 1:1 + NB, :], us[:, :, DS:DS + 2]))

            def split_y(n, h, y):
                pair = Y_PAIR[n]
                link(V.tensor_copy(yh[:, pair, h, :], y))
                V.tensor_tensor(yl[:, pair, h, :], y, yh[:, pair, h, :].bitcast(F32), ALU.subtract)

            def layer_norm(layer, which):
                q = 2 * layer + which
                dve.wait_ge(ln_mean, q + 1)
                for m in range(KD):
                    V.scalar_tensor_tensor(out=mix[:, m, :], in0=xp[0][:, 0:T], scalar=-1.0 / KD, in1=mix[:, m, :],
                                           op0=ALU.mult, op1=ALU.add).then_inc(ln_center, 1)
                dve.wait_ge(ln_rstd, q + 1)
                last = q == 2 * DEPTH - 1
                for m in range(KD):
                    gain = prm[:, layer, PLN + 16 * which + m:PLN + 16 * which + m + 1]
                    V.scalar_tensor_tensor(out=mix[:, m, :], in0=mix[:, m, :], scalar=gain, in1=rs[:, :],
                                           op0=ALU.mult, op1=ALU.mult).then_inc(ln_scaled, 1)
                    if m and not last:
                        low_part(layer, which, q, m - 1)
                if not last:
                    low_part(layer, which, q, KD - 1)

            def low_part(layer, which, q, m):
                bias = prm[:, layer, PLN + 16 * which + 8 + m:PLN + 16 * which + 9 + m]
                dve.wait_ge(x_hi, KD * (q + 1) + m + 1)
                V.scalar_tensor_tensor(out=xl[:, m, :], in0=mix[:, m, :], scalar=bias, in1=xh[:, m, :].bitcast(F32),
                                       op0=ALU.add, op1=ALU.subtract).then_inc(x_lo, 1)

            halves, splits = [0], [0]
            dve.wait_ge(setup_pool, 1)
            for layer in range(DEPTH):
                tile = 0
                for item, rows in zip(SCHEDULE, PHASE_TABLE):
                    if item[0] == "slot":
                        slot_i = item[1]
                        for _ in range(tiles_in(item[1])):
                            if frees(LTILES[tile]) == "dve":
                                n_free = freed("dve", layer * NTILE + tile)
                                if n_free:
                                    dve.wait_ge(tile_free["dve"], n_free)
                            evict(layer, tile)
                            tile += 1
                        if SLOTS[item[1]] == ("br", "D", 6):
                            dve.wait_ge(tile_free["dve"], freed("dve", layer * NTILE + tile))
                            split_mix()
                        if ends_norm(item[1]) is not None:
                            dve.wait_ge(tile_free["dve"], freed("dve", layer * NTILE + tile))
                            layer_norm(layer, ends_norm(item[1]))
                        continue
                    for k, (engine, before, _) in enumerate(rows):
                        if engine != "dve":
                            continue
                        follow(dve, layer, before)
                        if k == 0:
                            settled(dve, layer, tile, slot_i)
                        phase(*item[1:], k, layer, lambda ins: ins.then_inc(mix_done["dve"], 1))

        @block.tensor
        def _(pe):
            M = nc.tensor.matmul

            def dense(out, hi, lo, xhi, xlo, start, stop):
                M(out, hi, xhi, start=start, stop=False)
                M(out, hi, xlo, start=False, stop=False)
                return M(out, lo, xhi, start=False, stop=stop)

            def tile_of(layer, i):
                g = layer * NTILE + i
                if g >= BANKS:
                    e = frees(LTILES[(g - BANKS) % NTILE])
                    pe.wait_ge(tile_free[e], freed(e, g - BANKS + 1))
                return gps[g % BANKS][:, 0:T]

            def slot(layer, i, tile):
                c = layer * NSLOT + i
                pe.wait_ge(lo_done, c + 1)
                kind, a, b = SLOTS[i]
                hi, lo = whi[:, c % RING], wlo[:, c % RING]
                if kind == "br":
                    if b == 0:
                        pe.wait_ge(mix_done["dve"], layer * PHASES_PER_LAYER["dve"] + mixer_end(a))
                    pair = Y_PAIR[a]
                    for j in range(2):
                        out = tile_of(layer, tile + j)
                        for k in range(H):
                            last = dense(out, hi[:, 4 * j + k, :], lo[:, 4 * j + k, :], yh[:, pair, k, :],
                                         yl[:, pair, k, :], k == 0, k == H - 1)
                    last.then_inc(slot_done, 1)
                    return
                if kind == "down":
                    out = tile_of(layer, tile) if b == 0 else gps[(layer * NTILE + tile) % BANKS][:, 0:T]
                else:
                    out = tile_of(layer, tile)
                for k in range(KD):
                    if kind == "down":
                        f = KD * b + k
                        if a == 0:
                            up = LTILES.index(("up", f, 0))
                            pe.wait_ge(tile_free["dve"], freed("dve", layer * NTILE + up + 1))
                        xhi, xlo = ah[:, f, :], al[:, f, :]
                        first, end = f == 0, f == KF - 1
                    elif kind == "out":
                        if a == 0:
                            pe.wait_ge(mix_split, 2 * KD * layer + 2 * k + 2)
                        xhi, xlo = ah[:, k, :], al[:, k, :]
                        first, end = k == 0, k == KD - 1
                    else:
                        if i == 0 or (kind == "up" and a == 0):
                            pe.wait_ge(x_lo, KD * (2 * layer + (kind == "up")) + k + 1)
                        xhi, xlo = xh[:, k, :], xl[:, k, :]
                        first, end = k == 0, k == KD - 1
                    last = dense(out, hi[:, k, :], lo[:, k, :], xhi, xlo, first, end)
                last.then_inc(slot_done, 1)

            def mean_part(layer, which, m):
                kind = "down" if which else "out"
                t = LTILES.index((kind, m, 3 if which else 0))
                pe.wait_ge(tile_free["dve"], freed("dve", layer * NTILE + t + 1))
                return M(xp[0][:, 0:T], ones[:, 1, :], mix[:, m, :], start=m == 0, stop=m == KD - 1)

            def layer_norm(layer, which):
                q = 2 * layer + which
                mean_part(layer, which, KD - 1).then_inc(ln_mean, 1)
                for m in range(KD):
                    pe.wait_ge(ln_sq, KD * q + m + 1)
                    M(xp[1][:, 0:T], ones[:, 0, :], tt[:, m % BANKS, :], start=m == 0, stop=m == KD - 1).then_inc(ln_sqsum, 1)

            def turn(out_bank, src):
                for i, (lo, n) in enumerate(TILES):
                    last = nc.tensor.transpose(out_bank[0:n, i * P:(i + 1) * P], src[:, lo:lo + n], ident)
                return last

            def scores(bank, n, h):
                q, k = q_of(n, h), k_of(n, h)
                M(bank[:, 0:256], k[:, 0:P], q[:, 0:SEQ], start=True, stop=False, skip_group_check=True)
                M(bank[:, 256:384], k[:, P:SEQ], q[:, P:SEQ], start=False, stop=False, skip_group_check=True)
                return M(bank[0:NS, 384:SP4], k[:, SEQ:T], q[:, SEQ:T], start=False, stop=True, skip_group_check=True)

            def weigh(bank, lhs, h):
                M(bank[:, 0:256], lhs(0), pt[:, h, 0:256], start=True, stop=False, skip_group_check=True)
                M(bank[:, P:SEQ], lhs(1), pt[:, h, 256:384], start=False, stop=False, skip_group_check=True)
                return M(bank[:, SEQ:T], lhs(2), pt[0:NS, h, 384:SP4], start=False, stop=False, skip_group_check=True)

            def phase(stage, n, h, layer, done):
                if stage == "vt":
                    done(turn(xp[4], vf[:, h % 2, :]))
                elif stage in ("c_level", "c_last"):
                    if stage == "c_last":
                        for hd in range(H):
                            last = M(xp[0][:, hd * P:(hd + 1) * P], z12[:, 0, hd, 0:P], z12[:, 0, hd, P:SEQ],
                                     start=hd == 0, stop=hd == H - 1, skip_group_check=True)
                        done(last)
                        return
                    left = 1 if h == 0 else 0
                    for i in range(3 if h <= 1 else 2):
                        lo, w_ = TILES[i]
                        for hd in range(H):
                            last = M(xp[i][0:w_, hd * w_:(hd + 1) * w_], z12[:, left, hd, lo:lo + w_],
                                     z12[:, 0, hd, lo:lo + w_], start=hd == 0, stop=hd == H - 1, skip_group_check=True)
                    done(last)
                elif stage == "a_gate":
                    for i, (lo, w_) in enumerate(TILES):
                        for part, xx in enumerate((xh, xl)):
                            for k in range(KD):
                                last = M(xp[0][0:w_, 8 * i:8 * i + 8], xx[:, k, lo:lo + w_].bitcast(F32),
                                         gw[:, layer, k, :], start=i == 0 and part == 0 and k == 0,
                                         stop=part == 1 and k == KD - 1, skip_group_check=True)
                    done(last)
                elif stage == "a_cum":
                    M(xp[1][:, 0:4], c_("tri"), af[:, 0, :], start=True, stop=False, skip_group_check=True)
                    M(xp[1][:, 4:8], ones[:, 0, :], af[:, 0, :], start=False, stop=False, skip_group_check=True)
                    M(xp[1][:, 4:8], c_("tri"), af[:, 1, :], start=False, stop=False, skip_group_check=True)
                    done(M(xp[1][:, 8:12], c_("trib"), af[:, 2, :], start=False, stop=True, skip_group_check=True))
                elif stage == "a_row":
                    for i in range(3):
                        nc.tensor.transpose(xp[2][0:H, i * P:(i + 1) * P], gb[:, i, 0:H], ident)
                        last = nc.tensor.transpose(xp[3][0:H, i * P:(i + 1) * P], gb[:, i, H:2 * H], ident)
                    done(last)
                elif stage == "a_score":
                    sel = c_("sel", H)[:, h * P:(h + 1) * P]
                    for j, (col, src) in enumerate(((slice(0, 256), slice(0, 256)), (slice(256, 384), slice(P, SEQ)),
                                                    (slice(384, SP4), slice(SEQ, T)))):
                        M(xp[0][:, col], sel, row[:, 1, src], start=j == 0, stop=False, skip_group_check=True)
                    M(xp[0][:, 0:SP4], idb[:, :], negb[:, :], start=False, stop=True, skip_group_check=True)
                    scores(xp[1], n, h)
                    M(xp[2][:, 0:T], sel, row[:, 0, :], start=True, stop=False, skip_group_check=True)
                    done(M(xp[2][:, T:384], sel, wi[:, :], start=False, stop=True, skip_group_check=True))
                elif stage == "b_rope":
                    M(xp[0][:, 0:T], c_("perm"), zc[:, 0, h, :], start=True, stop=True)
                    done(M(xp[1][:, 0:T], c_("perm"), zc[:, 1, h, :], start=True, stop=True))
                elif stage == "b_score":
                    done(scores(xp[1], n, h))
                elif stage == "num":
                    j = layer * HEADS_PER_LAYER + state_of(n, h)
                    pe.wait_ge(s_in[j % 2], 16 * (j // 2 + 1))
                    weigh(xp[3], lambda i: v_of(n, h, i), h)
                    for b in range(NB):
                        s = slice(b * DS, (b + 1) * DS)
                        last = M(xp[3][:, SEQ + b * DS:SEQ + (b + 1) * DS], s0[:, j % 2, b, :], qw[:, h, s],
                                 start=False, stop=b == NB - 1, skip_group_check=True)
                    if n == "A":
                        weigh(xp[4], lambda i: ones[0:TILES[i][1], 0, :], h)
                        M(xp[4][:, SEQ:T], ones[:, 0, :], qn[:, :], start=False, stop=True, skip_group_check=True)
                    keys = z12[:, 0, h, :] if n == "C" else k_of(n, h)
                    done(turn(xp[0], keys))
                elif stage == "b_mean":
                    done(M(xp[4][:, 0:T], ones[:, 1, :], hh[:, :], start=True, stop=True))
                elif stage == "fin":
                    M(xp[4][:, 0:T], ones[:, 0, :], sq[:, :], start=True, stop=True)
                    for i in range(2):
                        v = v_of(n, h, i) if n == "C" else vw[:, i, :]
                        M(xp[0][:, 0:P], kt[:, i, :], v, start=i == 0, stop=False, skip_group_check=True)
                    if n == "A":
                        for i in range(2):
                            M(xp[0][:, P:P + 1], kt[:, i, :], ee[:, (255, 383)[i]:(256, 384)[i]], start=False, stop=False,
                              skip_group_check=True)
                        M(xp[0][:, P + 1:P + 1 + NB], kt[0:NS, 2, :], ee[0:NS, 384 + DS - 1:SP4:DS], start=False,
                          stop=True, skip_group_check=True)
                    for i in range(2):
                        last = M(xp[1 + i][:, :], kt[0:NS, 2, :], vm[:, 4 * i:4 * i + 4, :], start=True, stop=True)
                    done(last)

            pe.wait_ge(setup_pool, 1)
            pe.wait_ge(setup_dve, 1)
            for layer in range(DEPTH):
                tile = 0
                for item, rows in zip(SCHEDULE, PHASE_TABLE):
                    if item[0] == "slot":
                        slot_i = i = item[1]
                        kind, a, b = SLOTS[i]
                        slot(layer, i, tile)
                        tile += tiles_in(i)
                        if kind == "out" and a:
                            mean_part(layer, 0, a - 1)
                        if kind == "down" and a and b == 0:
                            mean_part(layer, 1, a - 1)
                        if ends_norm(i) is not None:
                            layer_norm(layer, ends_norm(i))
                        continue
                    for k, (engine, before, _) in enumerate(rows):
                        if engine != "pe":
                            continue
                        follow(pe, layer, before)
                        settled(pe, layer, tile, slot_i)
                        phase(*item[1:], layer, lambda ins: ins.then_inc(mix_done["pe"], 1))


def constants():
    import numpy as np
    f = np.float64
    s, t = np.arange(P)[:, None], np.arange(P)[None, :]
    gamma = 1.0 - 2.0 ** (-5.0 - np.arange(H, dtype=f))
    c = np.zeros((P, NCONST + SP4), np.float32)

    def put(name, value, rows=P):
        off, n = CONST_AT[name]
        c[:rows, off:off + n] = np.asarray(value).reshape(rows, n)

    j, seq = np.arange(NS) % DS, np.arange(NS) // DS
    own = seq[:, None] == seq[None, :]
    see = own & (j[:, None] <= j[None, :])
    put("ident", s == t)
    put("perm", (s + P // 2) % P == t)
    put("tri", s <= t)
    trib = np.zeros((P, P))
    trib[:NS, :NS] = see
    put("trib", trib)
    put("diag", (s // 4 == t // 4) & (s <= t))
    for m in LEVELS:
        put(f"lv{m}", (s // (2 * m) == t // (2 * m)) & (s % (2 * m) < m) & (t % (2 * m) >= m))
    d = np.zeros((P, H, 320))
    for h in range(H):
        d[:, h, 0:P] = np.where(s <= t, gamma[h] ** np.maximum(t - s, 0).astype(f), 0)
        d[:, h, P:2 * P] = gamma[h] ** (t + P - s).astype(f)
        d[:NS, h, 2 * P:] = np.where(see, gamma[h] ** np.maximum(j[None, :] - j[:, None], 0).astype(f), 0)
    put("dtab", d)
    put("inter", np.broadcast_to(gamma[:, None] ** (j + 1.0)[None, :], (P, H, NS)))
    put("toend", np.stack([gamma[None, :] ** (SEQ - 1.0 - P * i - s) for i in range(2)], axis=2))
    in_seq = seq[:, None] == np.arange(NB)[None, :]
    put("seqmask", in_seq, NS)
    put("vmask", in_seq[:, None, :] * (gamma[None, :] ** (DS - 1.0 - j)[:, None])[:, :, None], NS)
    half = P // 2
    inv = np.float32(10000.0) ** (-np.arange(half, dtype=np.float32) / np.float32(half))
    pos = np.concatenate([np.arange(SEQ), 2048 + j]).astype(np.float32)
    ang = (pos[None, :] * inv[:, None]).astype(np.float32).astype(f)
    put("cos", np.concatenate([np.cos(ang), np.cos(ang)]))
    put("sin", np.concatenate([-np.sin(ang), np.sin(ang)]))
    scan = np.ones((P, T))
    scan[:, [0] + list(range(SEQ, T, DS))] = 0
    put("scan", scan)
    put("sel", (np.arange(H)[:, None, None] == np.arange(H)[None, :, None]) & np.ones((1, 1, P), bool), H)
    neg = np.zeros((P, SP4))
    neg[:, 0:P] = np.where(s <= t, 0, NEG)
    neg[:, 256:384] = neg[:, 0:P]
    neg[:NS, 384:] = np.where(see, 0, NEG)
    c[:, NCONST:] = neg
    return c


def kernel(x_prompt, x_sample, state_mlstm_C, state_mlstm_n, state_mlstm_m, state_ret, state_hgrn, state_conv,
           w_in, b_mlstm_gate, norm_a, norm_b, norm_c, lb_c, conv_w, w_branch, w_gate, b_gate, w_out, ln1_g, ln1_b,
           ln2_g, ln2_b, w_up, w_down):
    import concourse.bacc as bacc
    import numpy as np
    from concourse.bass_utils import run_bass_kernel_spmd as run

    a = lambda v: np.asarray(v)
    x_prompt, x_sample = a(x_prompt), a(x_sample)
    w_in, w_gate, w_branch, w_out, w_up, w_down = map(a, (w_in, w_gate, w_branch, w_out, w_up, w_down))

    w = np.empty((DEPTH, NSLOT, P, KD, P), np.float32)
    for layer in range(DEPTH):
        for i, (kind, p, q) in enumerate(SLOTS):
            if kind == "in":
                src = w_in[layer][:, IN_COL[p] + q * P:IN_COL[p] + (q + 1) * P]
            elif kind == "gate":
                col = DM * BRANCH[p] + q * P
                src = w_gate[layer][:, col:col + P]
            elif kind == "br":
                src = w_branch[layer, BRANCH[p]][:, q * P:(q + 2) * P]
                w[layer, i] = src.reshape(H, P, 2, P).transpose(1, 2, 0, 3).reshape(P, KD, P)
                continue
            elif kind == "out":
                src = w_out[layer][:, p * P:(p + 1) * P]
            elif kind == "up":
                src = w_up[layer][:, p * P:(p + 1) * P]
            else:
                src = w_down[layer][q * DM:(q + 1) * DM, p * P:(p + 1) * P]
            w[layer, i] = src.reshape(KD, P, P).transpose(1, 0, 2)

    x = np.concatenate([x_prompt[0], x_sample.reshape(NS, DM)])
    x = np.ascontiguousarray(x.T.reshape(KD, P, T).transpose(1, 0, 2))
    col = lambda v: a(v).reshape(DEPTH, -1, P).transpose(2, 0, 1)
    par = np.concatenate([col(norm_a), col(norm_b), col(norm_c), col(conv_w), col(b_gate), col(ln1_g), col(ln1_b),
                          col(ln2_g), col(ln2_b), col(lb_c),
                          np.broadcast_to(a(b_mlstm_gate)[None], (P, DEPTH, 2 * H))], axis=2)
    ifw = np.ascontiguousarray(w_in[:, :, GATE_COL:GATE_COL + 2 * H].reshape(DEPTH, KD, P, 2 * H).transpose(2, 0, 1, 3))
    st = np.concatenate([a(state_hgrn), a(state_mlstm_C), a(state_ret)], axis=2).transpose(0, 2, 3, 1, 4)
    n0 = a(state_mlstm_n).transpose(3, 0, 2, 1)
    m0 = a(state_mlstm_m).transpose(2, 0, 1)
    cb = a(state_conv).reshape(DEPTH, NB, 2, H, P).transpose(4, 0, 3, 1, 2)

    nc = bacc.Bacc("TRN2", target_bir_lowering=False, num_devices=1)
    arrays, args = {}, []
    for name, v in (("w", w), ("x", x), ("cst", constants()), ("par", par), ("ifw", ifw), ("st", st), ("n0", n0),
                    ("m0", m0), ("cb", cb)):
        v = np.ascontiguousarray(v)
        arrays["in_" + name] = v
        args.append(nc.dram_tensor("in_" + name, v.shape, F32, kind="ExternalInput").ap())
    outs = {"y": (P, KD, T), "sp": (DEPTH, HEADS_PER_LAYER, P, P), "ss": (DEPTH, HEADS_PER_LAYER, P, NB, P),
            "n": (DEPTH, P, H, 1 + NB), "m": (DEPTH, H, 1 + NB), "c": (DEPTH, P, H, 1 + NB, 2)}
    for name, shape in outs.items():
        args.append(nc.dram_tensor("out_" + name, shape, F32, kind="ExternalOutput").ap())
    trunk(nc, *args)
    r = run(nc, [arrays], core_ids=[0]).results[0]
    y, sp, ss, n, m, c = (np.asarray(r["out_" + name]) for name in outs)

    y = y.transpose(2, 1, 0).reshape(T, DM)
    ss = ss.transpose(0, 3, 1, 2, 4)
    sp = sp[:, None]
    n = n.transpose(0, 3, 2, 1)
    m = m.transpose(0, 2, 1)
    c = c.transpose(0, 3, 4, 2, 1).reshape(DEPTH, 1 + NB, 2, H * P)
    copy = np.ascontiguousarray
    return (copy(y[:SEQ][None]), copy(y[SEQ:].reshape(NB, DS, DM)),
            copy(sp[:, :, 4:8]), copy(n[:, :1]), copy(m[:, :1]), copy(sp[:, :, 8:12]), copy(sp[:, :, 0:4]), copy(c[:, :1]),
            copy(ss[:, :, 4:8]), copy(n[:, 1:]), copy(m[:, 1:]), copy(ss[:, :, 8:12]), copy(ss[:, :, 0:4]), copy(c[:, 1:]))
```

```python
from contextlib import ExitStack

import concourse.bass as bass
from concourse import mybir

ALU = mybir.AluOpType
ACT = mybir.ActivationFunctionType
F32 = mybir.dt.float32
F32R = mybir.dt.float32r
BF16 = mybir.dt.bfloat16
U32 = mybir.dt.uint32

P = 128
DEPTH, SEQ, NB, DS = 2, 256, 8, 8
NS = NB * DS
T = SEQ + NS
H = 4
DM = 1024
KD = DM // P
KF = 4 * KD
ALPHA = (2 * DEPTH) ** 0.25
KSCALE = float(P) ** -0.5
EPS = 1e-5
CLAMP = 1.0 - 1e-6
NEG = -1e30
SP4 = 448
TILES = ((0, P), (P, P), (SEQ, NS))
RING = 3
BANKS = 3
LEVELS = (4, 8, 16, 32, 64)

PN, PCW, PBG, PLN, PLB = 0, 12, 24, 56, 88
NPAR = 92


def const_layout():
    at, off = {}, 0
    for name, n in (("ident", P), ("perm", P), ("tri", P), ("trib", P), ("diag", P), ("lv4", P), ("lv8", P),
                    ("lv16", P), ("lv32", P), ("lv64", P), ("dtab", H * 320), ("inter", H * NS),
                    ("toend", H * 2), ("seqmask", NB), ("vmask", H * NB), ("cos", T), ("sin", T),
                    ("scan", T), ("sel", H * P)):
        at[name] = (off, n)
        off += n
    return at, off


CONST_AT, NCONST = const_layout()


def slots_of_layer():
    s = []
    for kind in ("vC", "fC", "qC", "gC", "vA", "qA", "kA", "oA", "ifA", "cD", "xD", "bD"):
        s += [("in", kind, h) for h in range(1 if kind == "ifA" else H)]

    def mixed(n):
        for half in range(2):
            for m in range(4):
                s.append(("gate", n, 4 * half + m))
            for m in range(2):
                s.append(("br", n, 4 * half + 2 * m))

    mixed("C")
    for kind in ("vB", "qB", "kB", "gB"):
        s += [("in", kind, h) for h in range(H)]
    mixed("A")
    mixed("D")
    mixed("B")
    s += [("out", m, 0) for m in range(KD)]
    s += [("up", m, 0) for m in range(KF)]
    s += [("down", m, q) for m in range(KD) for q in range(4)]
    return s


SLOTS = slots_of_layer()
NSLOT = len(SLOTS)
IN_COL = {"ifA": 2048, "qA": 0, "kA": 512, "vA": 1024, "oA": 1536, "qB": 2056, "kB": 2568, "vB": 3080, "gB": 3592,
          "qC": 4104, "fC": 4616, "vC": 5128, "gC": 5640, "xD": 6152, "bD": 6664, "cD": 7176}
BRANCH = {"A": 0, "B": 1, "C": 2, "D": 3}
Y_PAIR = {"C": 0, "A": 1, "B": 0, "D": 1}
MIXERS = "CAB"


def tiles_of_layer():
    t = []
    for i, (kind, a, b) in enumerate(SLOTS):
        if kind == "br":
            t += [("br", a, b), ("br", a, b + 1)]
        elif kind != "down" or b == 3:
            t.append((kind, a, b))
        if turns_values(i):
            t.append(("vt", *SLOTS[i - 1][1:]))
    return t


def turns_values(i):
    return i > 0 and SLOTS[i - 1][0] == "in" and SLOTS[i - 1][1][0] == "v"


def sigmoids(tile):
    return tile[0] == "gate" or tile[0] == "in" and tile[1] in ("fC", "qC", "gC", "oA", "gB")


def frees(tile):
    kind, a, _ = tile
    if kind in ("gate", "vt"):
        return "act"
    return "dve" if kind != "in" or a in ("fC", "qC", "gC", "gB", "xD") else "act"


def hi_engine(c):
    return "dve" if sigmoids(SLOTS[(c - RING + 1) % NSLOT]) and c >= RING - 1 else "act"


LTILES = tiles_of_layer()
NTILE = len(LTILES)


def freed(engine, n):
    full, rest = divmod(n, NTILE)
    per = sum(frees(t) == engine for t in LTILES)
    return full * per + sum(frees(t) == engine for t in LTILES[:rest])


def rounded(engine, n):
    return sum(hi_engine(c) == engine for c in range(n))


BEFORE = "before"
PHASES = {
    "c_log": (("dve", BEFORE), ("act", 0), ("dve", 1)),
    "c_first": (("dve", BEFORE), ("act", 0), ("dve", 1)),
    "c_level": (("pe", BEFORE), ("dve", 0), ("act", 1), ("dve", 0), ("dve", 2)),
    "c_last": (("pe", BEFORE), ("dve", 0), ("act", 1), ("dve", 0), ("dve", 2)),
    "a_gate": (("pe", BEFORE), ("dve", 0), ("act", 1), ("dve", 2)),
    "a_cum": (("pe", BEFORE), ("dve", 0)),
    "a_row": (("pe", BEFORE), ("dve", 0), ("act", 1)),
    "a_score": (("pe", ("fin", -1, 1)), ("dve", 0), ("act", 0), ("dve", 2)),
    "b_rope": (("pe", ("fin", -1, 1)), ("dve", 0)),
    "b_score": (("pe", ("b_rope", 0, 1)), ("dve", 0)),
    "numC": (("pe", ("fin", -1, 1)), ("act", (0, ("fin", -1, 3))), ("dve", 0)),
    "numA": (("pe", (("a_score", 0, 3), ("fin", -1, 2))), ("act", 0), ("dve", 0), ("dve", 1), ("act", 3)),
    "numB": (("pe", (("b_score", 0, 1), ("fin", -1, 2))), ("act", (0, ("fin", -1, 3))), ("dve", 0)),
    "b_mean": (("pe", ("num", 0, 1)), ("dve", 0), ("act", 1)),
    "finC": (("pe", (("num", 0, 1), ("num", 0, 2))), ("dve", 0), ("act", (0, ("fin", -1, 3))), ("dve", 2)),
    "finA": (("pe", ("num", 0, 4)), ("dve", 0), ("act", (0, ("fin", -1, 3))), ("dve", 2)),
    "finB": (("pe", (("b_mean", 0, 2), ("num", 0, 2))), ("dve", 0), ("act", (0, ("fin", -1, 3))), ("dve", 2)),
    "conv": (("dve", BEFORE),),
}
COST = {"c_log": 1.8, "c_first": 2.2, "c_level": 1.4, "c_last": 1.7, "a_gate": 1, "a_cum": 1, "a_row": 1.4,
        "a_score": 1, "b_rope": 1.2, "b_score": 1, "numC": 1, "numA": 1.9, "numB": 1, "b_mean": 1, "finC": 1.1,
        "finA": 1.1, "finB": 1.1}


def phases(stage, n):
    return PHASES[stage if stage in PHASES else stage + n]


def schedule_of_layer():
    index = {s: i for i, s in enumerate(SLOTS)}
    last = lambda kind: index[("in", kind, H - 1)]
    chain = [("c_log", "C", 0, last("fC") + 1), ("c_first", "C", 0, last("qC") + 1)]
    chain += [("c_level", "C", i, 0) for i in range(len(LEVELS) + 1)] + [("c_last", "C", 0, last("gC") + 1)]
    for h in range(H):
        chain += [("num", "C", h, 0), ("fin", "C", h, 0)]
    chain += [("a_gate", "A", 0, index[("in", "ifA", 0)] + 1), ("a_cum", "A", 0, 0), ("a_row", "A", 0, 0)]
    for h in range(H):
        chain += [("a_score", "A", h, 0), ("num", "A", h, 0), ("fin", "A", h, 0)]
    for h in range(H):
        chain += [("b_rope", "B", h, last("kB") + 1), ("b_score", "B", h, 0), ("num", "B", h, 0),
                  ("b_mean", "B", h, 0), ("fin", "B", h, last("gB") + 1)]
    before = {index[("gate", n, 0)]: n for n in "CAB"}
    conv = {index[("gate", "D", c)]: c for c in range(H)}
    out, free_at = [], 0
    for i, slot in enumerate(SLOTS):
        if i in before:
            while any(c[1] == before[i] for c in chain):
                out.append(("mix", *chain.pop(0)[:3]))
        out.append(("slot", i))
        if i in conv:
            out.append(("mix", "conv", "D", conv[i]))
        while chain and chain[0][3] <= i and free_at <= i:
            stage = chain.pop(0)
            out.append(("mix", *stage[:3]))
            name = stage[0] if stage[0] in COST else stage[0] + stage[1]
            free_at = max(free_at, i) + COST[name]
    assert not chain
    return out


SCHEDULE = schedule_of_layer()


def phase_counts():
    done = {"pe": 0, "act": 0, "dve": 0}
    at, table = {}, []
    for item in SCHEDULE:
        if item[0] == "slot":
            table.append(None)
            continue
        _, stage, n, h = item
        before = [(e, v if v else -1) for e, v in done.items()]
        rows = []
        for j, (engine, refs) in enumerate(phases(stage, n)):
            waits = []
            for ref in refs if isinstance(refs, tuple) and not isinstance(refs[0], str) else (refs,):
                if ref == BEFORE:
                    waits += before
                elif isinstance(ref, int):
                    waits.append((rows[ref][0], rows[ref][2]))
                elif (ref[0], n, h + ref[1], ref[2]) in at:
                    waits.append(at[ref[0], n, h + ref[1], ref[2]])
                else:
                    waits += before
            done[engine] += 1
            rows.append((engine, waits, done[engine]))
            at[stage, n, h, j] = (engine, done[engine])
        table.append(rows)
    return table, done


PHASE_TABLE, PHASES_PER_LAYER = phase_counts()


def mixer_end(n):
    return max(rows[-1][2] for item, rows in zip(SCHEDULE, PHASE_TABLE)
               if item[0] == "mix" and item[2] == n and item[1] in ("fin", "conv"))


def tiles_in(i):
    kind, _, b = SLOTS[i]
    return 2 if kind == "br" else int(kind != "down" or b == 3) + turns_values(i)


def slot_of_tile():
    return [i for i in range(NSLOT) for _ in range(tiles_in(i))]


TILE_SLOT = slot_of_tile()


def ends_norm(i):
    return {("out", KD - 1, 0): 0, ("down", KD - 1, 3): 1}.get(SLOTS[i])
HEADS_PER_LAYER = 3 * H


def trunk(nc, w, x, cst, par, ifb, st, n0, m0, cb, y_out, sp_out, ss_out, n_out, m_out, c_out):
    with ExitStack() as ctx:
        def sb(name, shape, dt=F32, where=ctx):
            return where.enter_context(nc.sbuf_tensor(name, shape, dt))

        def sem(name):
            return ctx.enter_context(nc.semaphore(name))

        xh = sb("xh", [P, KD, T], F32R)
        xl = sb("xl", [P, KD, T], F32R)
        raw = sb("raw", [P, RING, KD, P])
        whi = sb("whi", [P, RING, KD, P], F32R)
        wlo = sb("wlo", [P, RING, KD, P], F32R)
        with ExitStack() as early:
            zc = sb("zc", [P, 4, H, T], F32, early)
            vc = sb("vc", [P, H, 3, P], F32, early)
            za = sb("za", [P, 3, H, T], F32, early)
            va = sb("va", [P, H, 3, P], F32, early)
            ud = sb("ud", [P, H, SEQ + 2 + NB * (DS + 2)], F32, early)
            bd = sb("bd", [P, H, T], F32, early)
            yh = sb("yh", [P, 2, H, T], F32R, early)
            yl = sb("yl", [P, 2, H, T], F32R, early)
            vf = sb("vf", [P, 2, T], F32, early)
        ah = sb("ah", [P, KF, T], F32R)
        al = sb("al", [P, KF, T], F32R)
        pt = sb("pt", [P, H, SP4])
        mix = sb("mix", [P, KD, T])
        z12 = mix[:, :, :].rearrange("p (a h) t -> p a h t", a=2)
        gt = zc[:, 2, :, :]
        s0 = sb("s0", [P, 2, NB, P])
        ee = sb("ee", [P, SP4])
        vm = sb("vm", [NS, NB, P])
        kt = sb("kt", [P, 3, P])
        vw = sb("vw", [P, 2, P])
        pst = sb("pst", [P, 2, P])
        hh = sb("hh", [P, T])
        sq = sb("sq", [P, T])
        rs = sb("rs", [P, T])
        tt = sb("tt", [P, BANKS, T])
        qw = sb("qw", [P, H, NS])
        qn = sb("qn", [P, NS])
        dec = sb("dec", [P, H, NB])
        con = sb("con", [P, NCONST])
        ones = sb("ones", [P, 2, P])
        negb = sb("negb", [P, SP4], BF16)
        idb = sb("idb", [P, P], BF16)
        prm = sb("prm", [P, DEPTH, NPAR])
        oml = sb("oml", [P, DEPTH, H])
        bif = sb("bif", [2 * H, DEPTH])
        iff_fm = sb("iff_fm", [2 * H, T])
        n0s = sb("n0s", [P, DEPTH, H, NB])
        nou = sb("nou", [P, H, 1 + NB])
        m0s = sb("m0s", [H, DEPTH, NB])
        row = sb("row", [H, 2, T])
        wi = sb("wi", [H, NS])
        mou = sb("mou", [H, 1 + NB])
        cbs = sb("cbs", [P, DEPTH, H, NB, 2])
        cou = sb("cou", [P, H, 1 + NB, 2])
        iff = sb("iff", [P, 3, 2 * H])
        gb = sb("gb", [P, 3, 2 * H])
        af = sb("af", [P, 3, H])
        eps = sb("eps", [P, 1])
        gps = [ctx.enter_context(nc.psum_tensor(f"gps{i}", [P, 512], F32)) for i in range(BANKS)]
        xp = [ctx.enter_context(nc.psum_tensor(f"xp{i}", [P, 512], F32)) for i in range(5)]

        def c_(name, rows=P):
            off, n = CONST_AT[name]
            return con[0:rows, off:off + n]

        ident = c_("ident")

        const_in, small_in = sem("const_in"), sem("small_in")
        x_in = [sem(f"x_in{i}") for i in range(KD // 2)]
        raw_in = [sem(f"raw_in{i}") for i in range(RING)]
        lo_done, slot_done = sem("lo_done"), sem("slot_done")
        hi_done = {"act": sem("hi_done_act"), "dve": sem("hi_done_dve")}
        tile_free = {"act": sem("tile_free_act"), "dve": sem("tile_free_dve")}
        act_part = sem("act_part")
        dve_part = sem("dve_part")
        mix_done = {e: sem(f"mix_done_{e}") for e in ("pe", "act", "dve")}
        setup_dve, setup_act, setup_lb, setup_pool = sem("setup_dve"), sem("setup_act"), sem("setup_lb"), sem("setup_pool")
        x_hi, x_lo = sem("x_hi"), sem("x_lo")
        dve_chain, act_chain = sem("dve_chain"), sem("act_chain")
        mix_split = sem("mix_split")
        ln_mean, ln_center, ln_sq, ln_sqsum = sem("ln_mean"), sem("ln_center"), sem("ln_sq"), sem("ln_sqsum")
        ln_rstd, ln_scaled, y_ready = sem("ln_rstd"), sem("ln_scaled"), sem("y_ready")
        s_out, small_out, y_sent = sem("s_out"), sem("small_out"), sem("y_sent")
        s_in = [sem("s_in0"), sem("s_in1")]
        block = ctx.enter_context(nc.Block())

        def q_of(n, h):
            return (za if n == "A" else zc)[:, 0, h, :]

        def k_of(n, h):
            return (za if n == "A" else zc)[:, 1, h, :]

        def v_of(n, h, tile):
            rows = TILES[tile][1]
            return (va if n == "A" else vc)[0:rows, h, tile, :]

        def state_of(n, h):
            return H * MIXERS.index(n) + h

        def blocks(ap, lo, hi, m):
            return ap[:, :, lo:hi].rearrange("p h (b two m) -> p h b two m", two=2, m=m)

        def per_seq(ap):
            return ap.rearrange("p (b t) -> p b t", t=DS)

        def sample_u(h):
            return ud[:, h, SEQ + 2:SEQ + 2 + NB * (DS + 2)].rearrange("p (b t) -> p b t", t=DS + 2)

        def follow(eng, layer, waits):
            for e, count in waits:
                count = layer * PHASES_PER_LAYER[e] + max(count, 0)
                if count:
                    eng.wait_ge(mix_done[e], count)

        def settled(eng, layer, tile, i):
            n = layer * NTILE + tile - tiles_in(i)
            for e in ("act", "dve"):
                if freed(e, n):
                    eng.wait_ge(tile_free[e], freed(e, n))

        @block.sync
        def _(sp):
            sp.dma_start(raw[:, 0, :, :], w[0, 0]).then_inc(raw_in[0], 16)
            for i in range(KD // 2):
                sp.dma_start(mix[:, 2 * i:2 * i + 2, :], x[:, 2 * i:2 * i + 2, :]).then_inc(x_in[i], 16)
            sp.dma_start(raw[:, 1, :, :], w[0, 1]).then_inc(raw_in[1], 16)
            sp.dma_start(con[:, :], cst[:, 0:NCONST]).then_inc(const_in, 16)
            sp.dma_start(ee[:, :], cst[:, NCONST:NCONST + SP4]).then_inc(const_in, 16)
            sp.dma_start(prm[:, :, :], par).then_inc(const_in, 16)
            sp.dma_start(raw[:, 2, :, :], w[0, 2]).then_inc(raw_in[2], 16)
            for dst, src in ((bif[:, :], ifb), (n0s[:, :, :, :], n0), (m0s[:, :, :], m0),
                             (cbs[:, :, :, :, :], cb)):
                sp.dma_start(dst, src).then_inc(small_in, 16)
            for j in range(2):
                sp.dma_start(s0[:, j, :, :], st[0, j]).then_inc(s_in[j], 16)
            sent = 0
            for layer in range(DEPTH):
                reload = None
                for item, rows in zip(SCHEDULE, PHASE_TABLE):
                    if item[0] == "slot":
                        c = layer * NSLOT + item[1] + RING
                        if c < DEPTH * NSLOT:
                            sp.wait_ge(lo_done, c - RING + 1)
                            sp.dma_start(raw[:, c % RING, :, :], w[c // NSLOT, c % NSLOT]).then_inc(raw_in[c % RING], 16)
                        if reload is not None:
                            j = layer * HEADS_PER_LAYER + reload
                            reload = None
                            if j < DEPTH * HEADS_PER_LAYER:
                                sp.wait_ge(s_out, 32 * (j - 1))
                                sp.dma_start(s0[:, j % 2, :, :],
                                             st[j // HEADS_PER_LAYER, j % HEADS_PER_LAYER]).then_inc(s_in[j % 2], 16)
                        continue
                    _, stage, n, h = item
                    if stage == "fin":
                        k = layer * PHASES_PER_LAYER["dve"] + rows[1][2]
                        sp.wait_ge(mix_done["dve"], k)
                        j = state_of(n, h)
                        sp.dma_start(ss_out[layer, j], s0[:, j % 2, :, :]).then_inc(s_out, 16)
                        sp.dma_start(sp_out[layer, j], pst[:, j % 2, :]).then_inc(s_out, 16)
                        reload = j + 2
                        if n == "A" and h == H - 1:
                            sp.dma_start(n_out[layer], nou[:, :, :]).then_inc(small_out, 16)
                            sp.dma_start(m_out[layer], mou[:, :]).then_inc(small_out, 16)
                    if stage == "conv" and h == H - 1:
                        sp.wait_ge(mix_done["dve"], layer * PHASES_PER_LAYER["dve"] + rows[-1][2])
                        sp.dma_start(c_out[layer], cou[:, :, :, :]).then_inc(small_out, 16)
            for m in range(KD):
                sp.wait_ge(y_ready, m + 1)
                sp.dma_start(y_out[:, m, :], mix[:, m, :]).then_inc(y_sent, 16)
            sp.wait_ge(y_sent, 16 * KD)
            sp.wait_ge(s_out, 32 * DEPTH * HEADS_PER_LAYER)
            sp.wait_ge(small_out, 16 * 3 * DEPTH)

        @block.gpsimd
        def _(pool):
            nc.gpsimd.memset(ones[:, 0, :], 1.0)
            nc.gpsimd.memset(ones[:, 1, :], 1.0 / P)
            nc.gpsimd.memset(pt[:, :, :], 0.0)
            nc.gpsimd.memset(iff[:, :, :], 0.0).then_inc(setup_pool, 1)
            for c in range(DEPTH * NSLOT):
                pool.wait_ge(hi_done[hi_engine(c)], rounded(hi_engine(c), c + 1))
                nc.gpsimd.tensor_tensor(wlo[:, c % RING, :, :], raw[:, c % RING, :, :],
                                        whi[:, c % RING, :, :].bitcast(F32), ALU.subtract).then_inc(lo_done, 1)

        @block.scalar
        def _(act):
            nc.scalar.preload_act_table_set("natural_log_exp_and_others")
            chain = [0]

            def link(ins):
                chain[0] += 1
                ins.then_inc(act_chain, 1)
                act.wait_ge(act_chain, chain[0])

            def split_hi(c):
                if c >= DEPTH * NSLOT or hi_engine(c) != "act":
                    return
                act.wait_ge(raw_in[c % RING], 16 * (c // RING + 1))
                if c >= RING:
                    act.wait_ge(slot_done, c - RING + 1)
                nc.scalar.activation(whi[:, c % RING, :, :], raw[:, c % RING, :, :],
                                     ACT.Copy).then_inc(hi_done["act"], 1)

            def evict(layer, i):
                g = layer * NTILE + i
                kind, a, b = LTILES[i]
                bank = gps[g % BANKS]
                ps = bank[:, 0:T]
                t = tt[:, g % BANKS, :]
                if kind in ("br", "out", "down") or a == "xD":
                    return
                act.wait_ge(slot_done, layer * NSLOT + TILE_SLOT[i] + 1)
                free = tile_free["act"]
                if kind == "vt":
                    v = va if a == "vA" else vc
                    nc.scalar.activation(v[:, b, 0:2, :], bank[:, 0:2 * P].rearrange("p (a c) -> p a c", a=2), ACT.Copy)
                    nc.scalar.activation(v[0:NS, b, 2, :], bank[0:NS, 2 * P:3 * P], ACT.Copy).then_inc(free, 1)
                elif kind == "up":
                    nc.scalar.activation(t, ps, ACT.Relu).then_inc(act_part, 1)
                elif sigmoids(LTILES[i]):
                    if kind == "gate":
                        j = KD * BRANCH[a] + b
                        link(nc.scalar.activation(t, ps, ACT.Abs, bias=prm[:, layer, PBG + j:PBG + j + 1]))
                    else:
                        link(nc.scalar.activation(t, ps, ACT.Abs))
                    link(nc.scalar.activation(t, t, ACT.Exp, scale=-1.0))
                    nc.scalar.activation(t, t, ACT.Ln, bias=1.0).then_inc(act_part, 1)
                elif a[0] == "v":
                    nc.scalar.activation(vf[:, b % 2, :], ps, ACT.Copy).then_inc(free, 1)
                elif a == "ifA":
                    nc.scalar.activation(iff_fm[:, :], bank[0:2 * H, 0:T], ACT.Identity,
                                         bias=bif[:, layer:layer + 1]).then_inc(free, 1)
                elif a in ("qA", "kA", "qB", "kB"):
                    dst = (q_of if a[0] == "q" else k_of)(a[1], b)
                    nc.scalar.activation(dst, ps, ACT.Copy, scale=KSCALE if a[0] == "k" else 1.0).then_inc(free, 1)
                else:
                    nc.scalar.activation(bd[:, b, :], ps, ACT.Copy).then_inc(free, 1)

            def evict_second(layer, i):
                if not sigmoids(LTILES[i]):
                    return
                g = layer * NTILE + i
                kind, a, b = LTILES[i]
                t = tt[:, g % BANKS, :]
                seconds[0] += 1
                act.wait_ge(dve_part, seconds[0])
                if kind == "gate":
                    nc.scalar.activation(gt[:, b % 4, :], t, ACT.Exp).then_inc(tile_free["act"], 1)
                elif a == "oA":
                    nc.scalar.activation(za[:, 2, b, :], t, ACT.Exp).then_inc(tile_free["act"], 1)
                else:
                    nc.scalar.activation(t, t, ACT.Exp, scale=-1.0 if a == "fC" else 1.0).then_inc(act_part, 1)

            def phase(stage, n, h, k, layer, done):
                if stage == "c_log":
                    done(nc.scalar.activation(z12[:, 0, :, :], z12[:, 0, :, :], ACT.Ln, scale=-1.0, bias=1.0))
                elif stage == "c_first":
                    nc.scalar.activation(z12[:, 1, :, :], z12[:, 0, :, :], ACT.Exp, scale=-1.0)
                    done(nc.scalar.activation(z12[:, 0, :, :], z12[:, 0, :, :], ACT.Exp))
                elif stage == "c_level":
                    hi = T if LEVELS[h:] and LEVELS[h] == DS // 2 else SEQ
                    z = z12[:, (h + 1) % 2, :, 0:hi]
                    done(nc.scalar.activation(z, z, ACT.Exp))
                elif stage == "c_last":
                    nc.scalar.activation(z12[:, 1, :, :], z12[:, 1, :, :], ACT.Exp)
                    nc.scalar.activation(qw[:, :, :], zc[:, 2, :, SEQ:T], ACT.Exp)
                    done(nc.scalar.activation(dec[:, :, :], zc[:, 2, :, SEQ + DS - 1:T:DS], ACT.Exp))
                elif stage == "a_gate":
                    link(nc.scalar.activation(af[:, :, :], iff[:, :, H:2 * H], ACT.Abs))
                    link(nc.scalar.activation(af[:, :, :], af[:, :, :], ACT.Exp, scale=-1.0))
                    done(nc.scalar.activation(af[:, :, :], af[:, :, :], ACT.Ln, bias=1.0))
                elif stage == "a_row":
                    nc.scalar.activation(row[:, 0, :], row[:, 0, :], ACT.Exp, scale=-1.0)
                    done(nc.scalar.activation(wi[:, :], wi[:, :], ACT.Exp))
                elif stage == "a_score":
                    nc.scalar.activation(ee[:, 0:256], xp[0][:, 0:256], ACT.Exp, bias=gb[:, 0, h:h + 1])
                    nc.scalar.activation(ee[:, 256:384], xp[0][:, 256:384], ACT.Exp, bias=gb[:, 1, h:h + 1])
                    done(nc.scalar.activation(ee[0:NS, 384:SP4], xp[0][0:NS, 384:SP4], ACT.Exp, bias=gb[0:NS, 2, h:h + 1]))
                elif stage == "num" and k == 1:
                    nc.scalar.activation(kt[:, 0:2, :], xp[0][:, 0:2 * P].rearrange("p (a c) -> p a c", a=2), ACT.Copy)
                    nc.scalar.activation(kt[0:NS, 2, :], xp[0][0:NS, 2 * P:3 * P], ACT.Copy)
                    if n == "A":
                        done(nc.scalar.activation(sq[:, :], xp[4][:, 0:T], ACT.Abs))
                    elif n == "B":
                        done(nc.scalar.activation(hh[:, :], xp[3][:, 0:T], ACT.Copy))
                    else:
                        nc.scalar.activation(sq[:, :], xp[3][:, 0:T], ACT.Square)
                        done(nc.scalar.activation(hh[:, :], xp[3][:, 0:T], ACT.Copy))
                elif stage == "num":
                    done(nc.scalar.activation(sq[:, :], hh[:, :], ACT.Square))
                elif stage == "b_mean":
                    done(nc.scalar.activation(sq[:, :], hh[:, :], ACT.Square))
                elif stage == "fin":
                    link(nc.scalar.activation(rs[:, :], xp[4][:, 0:T], ACT.Ln, scale=1.0 / P, bias=eps[:, 0:1]))
                    done(nc.scalar.activation(rs[:, :], rs[:, :], ACT.Exp, scale=-0.5))

            def layer_norm(layer, which):
                q = 2 * layer + which
                for m in range(KD):
                    e = KD * q + m
                    act.wait_ge(ln_center, e + 1)
                    if m >= BANKS:
                        act.wait_ge(ln_sqsum, e - BANKS + 1)
                    nc.scalar.activation(tt[:, m % BANKS, :], mix[:, m, :], ACT.Square).then_inc(ln_sq, 1)
                act.wait_ge(ln_sqsum, KD * (q + 1))
                link(nc.scalar.activation(rs[:, :], xp[1][:, 0:T], ACT.Ln, scale=1.0 / DM, bias=eps[:, 0:1]))
                nc.scalar.activation(rs[:, :], rs[:, :], ACT.Exp, scale=-0.5).then_inc(ln_rstd, 1)
                for m in range(KD):
                    act.wait_ge(ln_scaled, KD * q + m + 1)
                    bias = prm[:, layer, PLN + 16 * which + 8 + m:PLN + 16 * which + 9 + m]
                    if q == 2 * DEPTH - 1:
                        nc.scalar.activation(mix[:, m, :], mix[:, m, :], ACT.Identity, bias=bias).then_inc(y_ready, 1)
                    else:
                        nc.scalar.activation(xh[:, m, :], mix[:, m, :], ACT.Identity, bias=bias).then_inc(x_hi, 1)

            split_hi(0)
            for k in range(KD):
                act.wait_ge(x_in[k // 2], 16)
                nc.scalar.activation(xh[:, k, :], mix[:, k, :], ACT.Copy).then_inc(x_hi, 1)
            split_hi(1)
            act.wait_ge(setup_lb, 1)
            nc.scalar.activation(oml[:, 1, :], oml[:, 0, :], ACT.Exp).then_inc(setup_act, 1)

            seconds = [0]
            act.wait_ge(setup_dve, 1)
            for layer in range(DEPTH):
                tile = 0
                for item, rows in zip(SCHEDULE, PHASE_TABLE):
                    if item[0] == "slot":
                        slot_i = item[1]
                        for i in range(tile - tiles_in(slot_i - 1) if slot_i else 0, tile):
                            evict_second(layer, i)
                        split_hi(layer * NSLOT + item[1] + RING - 1)
                        for _ in range(tiles_in(item[1])):
                            evict(layer, tile)
                            tile += 1
                        if ends_norm(item[1]) is not None:
                            layer_norm(layer, ends_norm(item[1]))
                        continue
                    for k, (engine, before, _) in enumerate(rows):
                        if engine != "act":
                            continue
                        follow(act, layer, before)
                        if k == 0:
                            settled(act, layer, tile, slot_i)
                        phase(*item[1:], k, layer, lambda ins: ins.then_inc(mix_done["act"], 1))

        @block.vector
        def _(dve):
            V = nc.vector
            chain = [0]

            def link(ins):
                chain[0] += 1
                ins.then_inc(dve_chain, 1)
                dve.wait_ge(dve_chain, chain[0])

            for k in range(KD):
                dve.wait_ge(x_hi, k + 1)
                V.tensor_tensor(xl[:, k, :], mix[:, k, :], xh[:, k, :].bitcast(F32), ALU.subtract).then_inc(x_lo, 1)
            dve.wait_ge(const_in, 48)
            V.tensor_copy(negb[:, :], ee[:, :])
            V.tensor_copy(idb[:, :], ident)
            V.memset(eps[:, :], EPS)
            V.tensor_tensor(oml[:, 0, :], prm[:, 1, PLB:PLB + H], prm[:, 0, PLB:PLB + H], ALU.subtract).then_inc(setup_lb, 1)
            dve.wait_ge(setup_act, 1)
            link(V.tensor_scalar_add(oml[:, 1, :], oml[:, 1, :], 1.0))
            link(V.reciprocal(oml[:, 1, :], oml[:, 1, :]))
            V.memset(oml[:, 0, :], 1.0).then_inc(setup_dve, 1)
            dve.wait_ge(setup_dve, 1)
            dve.wait_ge(small_in, 64)

            def split_hi(c):
                if c >= DEPTH * NSLOT or hi_engine(c) != "dve":
                    return
                dve.wait_ge(raw_in[c % RING], 16 * (c // RING + 1))
                dve.wait_ge(slot_done, c - RING + 1) if c >= RING else None
                V.tensor_copy(whi[:, c % RING, :, :], raw[:, c % RING, :, :]).then_inc(hi_done["dve"], 1)

            def evict_second(layer, i):
                kind, a, b = LTILES[i]
                if not sigmoids(LTILES[i]) or kind == "gate" or a == "oA":
                    return
                g = layer * NTILE + i
                t = tt[:, g % BANKS, :]
                act_parts[0] += 1
                dve.wait_ge(act_part, act_parts[0])
                if a == "fC":
                    V.tensor_scalar(zc[:, 1, b, :], t, oml[:, layer, b:b + 1], None, ALU.mult).then_inc(tile_free["dve"], 1)
                else:
                    V.tensor_tensor(zc[:, 0 if a == "qC" else 3, b, :], gps[g % BANKS][:, 0:T], t,
                                    ALU.mult).then_inc(tile_free["dve"], 1)

            def evict(layer, i):
                g = layer * NTILE + i
                kind, a, b = LTILES[i]
                if frees(LTILES[i]) != "dve" and not sigmoids(LTILES[i]):
                    return
                ps = gps[g % BANKS][:, 0:T]
                t = tt[:, g % BANKS, :]
                free = tile_free["dve"]
                if kind in ("br", "out", "down") or a == "xD":
                    dve.wait_ge(slot_done, layer * NSLOT + TILE_SLOT[i] + 1)
                else:
                    act_parts[0] += 1
                    dve.wait_ge(act_part, act_parts[0])
                if kind == "up":
                    link(V.tensor_tensor(t, t, t, ALU.mult))
                    link(V.tensor_copy(ah[:, a, :], t))
                    V.tensor_tensor(al[:, a, :], t, ah[:, a, :].bitcast(F32), ALU.subtract).then_inc(free, 1)
                elif kind in ("out", "down"):
                    link(V.scalar_tensor_tensor(out=mix[:, a, :], in0=xh[:, a, :].bitcast(F32), scalar=ALPHA, in1=ps,
                                                op0=ALU.mult, op1=ALU.add))
                    V.scalar_tensor_tensor(out=mix[:, a, :], in0=xl[:, a, :].bitcast(F32), scalar=ALPHA,
                                           in1=mix[:, a, :], op0=ALU.mult, op1=ALU.add).then_inc(free, 1)
                elif kind == "gate":
                    j = KD * BRANCH[a] + b
                    link(V.tensor_scalar(gt[:, b % 4, :], ps, prm[:, layer, PBG + j:PBG + j + 1], 0.0, ALU.add, ALU.min))
                    V.tensor_tensor(t, gt[:, b % 4, :], t, ALU.subtract).then_inc(dve_part, 1)
                elif kind == "br":
                    if a == "C":
                        V.tensor_tensor(mix[:, b, :], ps, gt[:, b % 4, :], ALU.mult).then_inc(free, 1)
                    else:
                        link(V.tensor_tensor(t, ps, gt[:, b % 4, :], ALU.mult))
                        V.tensor_tensor(mix[:, b, :], mix[:, b, :], t, ALU.add).then_inc(free, 1)
                elif a == "xD":
                    V.memset(ud[:, b, 0:2], 0.0)
                    V.tensor_tensor(ud[:, b, 2:2 + SEQ], ps[:, 0:SEQ], bd[:, b, 0:SEQ], ALU.mult)
                    V.tensor_copy(sample_u(b)[:, :, 0:2], cbs[:, layer, b, :, :])
                    V.tensor_tensor(sample_u(b)[:, :, 2:2 + DS], per_seq(ps[:, SEQ:T]), per_seq(bd[:, b, SEQ:T]),
                                    ALU.mult).then_inc(free, 1)
                elif a == "fC":
                    V.scalar_tensor_tensor(out=t, in0=ps, scalar=0.0, in1=t, op0=ALU.max, op1=ALU.add).then_inc(dve_part, 1)
                else:
                    V.scalar_tensor_tensor(out=t, in0=ps, scalar=0.0, in1=t, op0=ALU.min,
                                           op1=ALU.subtract).then_inc(dve_part, 1)

            def split_mix():
                for m in range(KD):
                    V.tensor_copy(ah[:, m, :], mix[:, m, :]).then_inc(mix_split, 1)
                    splits[0] += 1
                    dve.wait_ge(mix_split, splits[0])
                    V.tensor_tensor(al[:, m, :], mix[:, m, :], ah[:, m, :].bitcast(F32), ALU.subtract).then_inc(mix_split, 1)
                    splits[0] += 1

            def spans(m):
                return [(0, SEQ)] + ([(SEQ, T)] if m == DS // 2 else [])

            def distances(m, buf):
                for lo, hi in spans(m):
                    b = blocks(zc[:, 2, :, :], lo, hi, m)
                    z = blocks(z12[:, buf, :, :], lo, hi, m)
                    mid = b[:, :, :, 0, m - 1:m].to_broadcast([P, H, (hi - lo) // (2 * m), m])
                    V.tensor_tensor(z[:, :, :, 0, :], mid, b[:, :, :, 0, :], ALU.subtract)
                    last = V.tensor_tensor(z[:, :, :, 1, :], b[:, :, :, 1, :], mid, ALU.subtract)
                return last

            def apply_qk(m, buf):
                for lo, hi in spans(m):
                    z = blocks(z12[:, buf, :, :], lo, hi, m)
                    q = blocks(zc[:, 0, :, :], lo, hi, m)
                    k = blocks(zc[:, 1, :, :], lo, hi, m)
                    V.tensor_tensor(z[:, :, :, 0, :], z[:, :, :, 0, :], k[:, :, :, 0, :], ALU.mult)
                    last = V.tensor_tensor(z[:, :, :, 1, :], z[:, :, :, 1, :], q[:, :, :, 1, :], ALU.mult)
                return last

            def take(level):
                m = LEVELS[level - 1] if level else P
                mask = c_(f"lv{m}" if level else "diag").bitcast(U32)

                def late(ap, width):
                    if not level:
                        return ap
                    return ap.rearrange("p (b two m) -> p b two m", two=2, m=m)[:, :, 1, :]

                for tile, col in ((0, 0), (1, 256), (2, 384)):
                    rows, w_ = (NS, NS) if tile == 2 else (P, P)
                    if tile == 2 and level > 1:
                        continue
                    if not level:
                        last = V.copy_predicated(pt[0:rows, :, col:col + w_],
                                          mask[0:rows, 0:w_].unsqueeze(1).to_broadcast([rows, H, w_]),
                                          xp[tile][0:rows, 0:H * w_].rearrange("p (h t) -> p h t", h=H))
                        continue
                    nb = w_ // (2 * m)
                    last = V.copy_predicated(blocks(pt[0:rows, :, :], col, col + w_, m)[:, :, :, 1, :],
                                      late(mask[0:rows, 0:w_], w_).unsqueeze(1).to_broadcast([rows, H, nb, m]),
                                      xp[tile][0:rows, 0:H * w_ // 2].rearrange("p (h b m) -> p h b m", h=H, m=m))
                return last

            def phase(stage, n, h, k, layer, done):
                if stage == "c_log" and k == 0:
                    done(V.tensor_scalar(z12[:, 0, :, :], zc[:, 1, :, :], CLAMP, None, ALU.min))
                elif stage == "c_log":
                    for hd in range(H):
                        last = V.tensor_tensor_scan(zc[:, 2, hd, :], c_("scan"), z12[:, 0, hd, :], 0.0, ALU.mult, ALU.add)
                    done(last)
                elif stage == "c_first" and k == 0:
                    b = zc[:, 2, :, :].rearrange("p h (b m) -> p (h b) m", m=4)
                    z = z12[:, 0, :, :].rearrange("p h (b m) -> p (h b) m", m=4)
                    done(V.tensor_tensor(z, b, b[:, :, 0:1].to_broadcast([P, H * T // 4, 4]), ALU.subtract))
                elif stage == "c_first":
                    V.tensor_tensor(z12[:, 0, :, :], z12[:, 0, :, :], zc[:, 0, :, :], ALU.mult)
                    done(V.tensor_tensor(z12[:, 1, :, :], z12[:, 1, :, :], zc[:, 1, :, :], ALU.mult))
                elif stage == "c_level" and k == 1:
                    done(distances((LEVELS + (P,))[h], (h + 1) % 2))
                elif stage == "c_level" and k == 3:
                    done(take(h))
                elif stage == "c_level":
                    done(apply_qk((LEVELS + (P,))[h], (h + 1) % 2))
                elif stage == "c_last" and k == 1:
                    b = zc[:, 2, :, :]
                    V.tensor_tensor(z12[:, 1, :, 0:SEQ], b[:, :, SEQ - 1:SEQ].to_broadcast([P, H, SEQ]),
                                    b[:, :, 0:SEQ], ALU.subtract)
                    s = b[:, :, SEQ:T].rearrange("p h (b t) -> p h b t", t=DS)
                    done(V.tensor_tensor(z12[:, 1, :, SEQ:T].rearrange("p h (b t) -> p h b t", t=DS),
                                         s[:, :, :, DS - 1:DS].to_broadcast([P, H, NB, DS]), s, ALU.subtract))
                elif stage == "c_last" and k == 3:
                    done(V.tensor_copy(pt[:, :, P:2 * P], xp[0][:, :].rearrange("p (h t) -> p h t", h=H)))
                elif stage == "c_last":
                    V.tensor_tensor(z12[:, 1, :, :], z12[:, 1, :, :], zc[:, 1, :, :], ALU.mult)
                    done(V.tensor_tensor(qw[:, :, :], qw[:, :, :], zc[:, 0, :, SEQ:T], ALU.mult))
                elif stage == "a_gate" and k == 1:
                    V.tensor_copy(iff[:, 0:2, :], xp[0][:, 0:16].rearrange("p (a c) -> p a c", a=2))
                    done(V.tensor_copy(iff[0:NS, 2, :], xp[0][0:NS, 16:24]))
                elif stage == "a_gate":
                    done(V.scalar_tensor_tensor(out=af[:, :, :], in0=iff[:, :, H:2 * H], scalar=0.0, in1=af[:, :, :],
                                                op0=ALU.min, op1=ALU.subtract))
                elif stage == "a_cum":
                    b = xp[1][:, 0:12].rearrange("p (a c) -> p a c", a=3)
                    V.tensor_tensor(gb[:, :, 0:H], iff[:, :, 0:H], b, ALU.subtract)
                    done(V.tensor_copy(gb[:, :, H:2 * H], b))
                elif stage == "a_row":
                    link(V.tensor_copy(row[:, 0, :], xp[2][0:H, 0:T]))
                    V.tensor_tensor_scan(row[:, 1, 0:SEQ], row[:, 0, 0:SEQ], row[:, 0, 0:SEQ], 0.0, ALU.max, ALU.max)
                    for b in range(NB):
                        s = slice(SEQ + b * DS, SEQ + (b + 1) * DS)
                        last = V.tensor_tensor_scan(row[:, 1, s], row[:, 0, s], row[:, 0, s], m0s[:, layer, b:b + 1],
                                                    ALU.max, ALU.max)
                    link(last)
                    if layer:
                        dve.wait_ge(small_out, 16 * 3 * layer)
                    link(V.tensor_tensor(row[:, 0, :], row[:, 1, :], xp[3][0:H, 0:T], ALU.add))
                    V.tensor_copy(mou[:, 0:1], row[:, 0, SEQ - 1:SEQ])
                    V.tensor_copy(mou[:, 1:1 + NB], row[:, 0, SEQ + DS - 1:T:DS])
                    link(V.tensor_tensor(per_seq(wi[:, :]), m0s[:, layer, :].unsqueeze(2).to_broadcast([H, NB, DS]),
                                         per_seq(row[:, 1, SEQ:T]), ALU.subtract))
                    done(V.tensor_scalar(row[:, 1, :], row[:, 1, :], -1.0, None, ALU.mult))
                elif stage == "a_score" and k == 3:
                    V.tensor_tensor(pt[:, h, 0:384], xp[1][:, 0:384], ee[:, 0:384], ALU.mult)
                    done(V.tensor_tensor(pt[0:NS, h, 384:SP4], xp[1][0:NS, 384:SP4], ee[0:NS, 384:SP4], ALU.mult))
                elif stage == "a_score":
                    V.tensor_copy(dec[:, h, :], xp[2][:, T + DS - 1:384:DS])
                    link(V.tensor_tensor(qw[:, h, :], xp[2][:, T:384], za[:, 0, h, SEQ:T], ALU.mult))
                    done(V.tensor_tensor(per_seq(qn[:, :]), per_seq(qw[:, h, :]),
                                         n0s[:, layer, h, :].unsqueeze(2).to_broadcast([P, NB, DS]), ALU.mult))
                elif stage == "b_rope":
                    for i in range(2):
                        V.tensor_tensor((sq, rs)[i][:, :], xp[i][:, 0:T], c_("sin"), ALU.mult)
                        last = V.tensor_tensor(zc[:, i, h, :], zc[:, i, h, :], c_("cos"), ALU.mult)
                    link(last)
                    V.tensor_tensor(zc[:, 1, h, :], zc[:, 1, h, :], rs[:, :], ALU.add)
                    link(V.tensor_tensor(zc[:, 0, h, :], zc[:, 0, h, :], sq[:, :], ALU.add))
                    done(V.tensor_tensor(qw[:, h, :], zc[:, 0, h, SEQ:T], c_("inter")[:, h * NS:(h + 1) * NS], ALU.mult))
                elif stage == "b_score":
                    d = c_("dtab").rearrange("p (h c) -> p h c", h=H)[:, h, :]
                    V.tensor_tensor(pt[:, h, 0:256], xp[1][:, 0:256], d[:, 0:256], ALU.mult)
                    V.tensor_tensor(pt[:, h, 256:384], xp[1][:, 256:384], d[:, 0:128], ALU.mult)
                    done(V.tensor_tensor(pt[0:NS, h, 384:SP4], xp[1][0:NS, 384:SP4], d[0:NS, 256:320], ALU.mult))
                elif stage == "num" and k == 3:
                    link(V.tensor_tensor(sq[:, :], sq[:, :], xp[2][:, 0:T], ALU.max))
                    link(V.reciprocal(sq[:, :], sq[:, :]))
                    done(V.tensor_tensor(hh[:, :], xp[3][:, 0:T], sq[:, :], ALU.mult))
                elif stage == "num":
                    if n == "A":
                        ends, mask = (ee[:, 255:256], ee[:, 383:384]), ee[0:NS, 384 + DS - 1:SP4:DS]
                    elif n == "B":
                        toend = c_("toend")[:, 2 * h:2 * h + 2]
                        ends, mask = (toend[:, 0:1], toend[:, 1:2]), c_("vmask", NS)[:, h * NB:(h + 1) * NB]
                    else:
                        ends, mask = None, c_("seqmask", NS)
                    if ends:
                        for i in range(2):
                            V.tensor_scalar(vw[:, i, :], v_of(n, h, i), ends[i], None, ALU.mult)
                    done(V.tensor_tensor(vm[:, :, :], v_of(n, h, 2).unsqueeze(1).to_broadcast([NS, NB, P]),
                                         mask.unsqueeze(2).to_broadcast([NS, NB, P]), ALU.mult))
                elif stage == "b_mean":
                    done(V.tensor_tensor(hh[:, :], hh[:, :], xp[4][:, 0:T], ALU.subtract))
                elif stage == "fin" and k == 3:
                    w_ = prm[:, layer, PN + 4 * "ABC".index(n) + h:PN + 4 * "ABC".index(n) + h + 1]
                    link(V.scalar_tensor_tensor(out=hh[:, :], in0=hh[:, :], scalar=w_, in1=rs[:, :],
                                                op0=ALU.mult, op1=ALU.mult))
                    gate = za[:, 2, h, :] if n == "A" else zc[:, 3, h, :]
                    link(V.tensor_tensor(hh[:, :], hh[:, :], gate, ALU.mult))
                    done(split_y(n, h, hh[:, :]))
                elif stage == "fin":
                    j = state_of(n, h)
                    V.tensor_copy(pst[:, j % 2, :], xp[0][:, 0:P])
                    if n == "A":
                        V.tensor_copy(nou[:, h, 0:1], xp[0][:, P:P + 1])
                        link(V.tensor_tensor(nou[:, h, 1:1 + NB], n0s[:, layer, h, :], dec[:, h, :], ALU.mult))
                        V.tensor_tensor(nou[:, h, 1:1 + NB], nou[:, h, 1:1 + NB], xp[0][:, P + 1:P + 1 + NB], ALU.add)
                    for b in range(NB):
                        new = xp[1 + b // 4][:, (b % 4) * P:(b % 4 + 1) * P]
                        keep = (1.0 - 2.0 ** (-5 - h)) ** DS if n == "B" else dec[:, h, b:b + 1]
                        last = V.scalar_tensor_tensor(out=s0[:, j % 2, b, :], in0=s0[:, j % 2, b, :], scalar=keep,
                                                      in1=new, op0=ALU.mult, op1=ALU.add)
                    done(last)
                elif stage == "conv":
                    if layer and h == 0:
                        dve.wait_ge(small_out, 16 * 3 * layer)
                    tap = lambda j: prm[:, layer, PCW + 4 * j + h:PCW + 4 * j + h + 1]
                    up, us = ud[:, h, 0:SEQ + 2], sample_u(h)
                    y = ee[:, 0:T]
                    yp, ys = y[:, 0:SEQ], per_seq(y[:, SEQ:T])
                    V.tensor_scalar(yp, up[:, 0:SEQ], tap(0), None, ALU.mult)
                    link(V.tensor_scalar(ys, us[:, :, 0:DS], tap(0), None, ALU.mult))
                    for j in (1, 2):
                        V.scalar_tensor_tensor(out=yp, in0=up[:, j:j + SEQ], scalar=tap(j), in1=yp, op0=ALU.mult, op1=ALU.add)
                        link(V.scalar_tensor_tensor(out=ys, in0=us[:, :, j:j + DS], scalar=tap(j), in1=ys,
                                                    op0=ALU.mult, op1=ALU.add))
                    link(V.tensor_tensor(y, y, bd[:, h, :], ALU.mult))
                    split_y("D", h, y)
                    V.tensor_copy(cou[:, h, 0, :], up[:, SEQ:SEQ + 2])
                    done(V.tensor_copy(cou[:, h, 1:1 + NB, :], us[:, :, DS:DS + 2]))

            def split_y(n, h, y):
                pair = Y_PAIR[n]
                link(V.tensor_copy(yh[:, pair, h, :], y))
                return V.tensor_tensor(yl[:, pair, h, :], y, yh[:, pair, h, :].bitcast(F32), ALU.subtract)

            def layer_norm(layer, which):
                q = 2 * layer + which
                dve.wait_ge(ln_mean, q + 1)
                for m in range(KD):
                    V.scalar_tensor_tensor(out=mix[:, m, :], in0=xp[0][:, 0:T], scalar=-1.0 / KD, in1=mix[:, m, :],
                                           op0=ALU.mult, op1=ALU.add).then_inc(ln_center, 1)
                dve.wait_ge(ln_rstd, q + 1)
                last = q == 2 * DEPTH - 1
                for m in range(KD):
                    gain = prm[:, layer, PLN + 16 * which + m:PLN + 16 * which + m + 1]
                    V.scalar_tensor_tensor(out=mix[:, m, :], in0=mix[:, m, :], scalar=gain, in1=rs[:, :],
                                           op0=ALU.mult, op1=ALU.mult).then_inc(ln_scaled, 1)
                    if m and not last:
                        low_part(layer, which, q, m - 1)
                if not last:
                    low_part(layer, which, q, KD - 1)

            def low_part(layer, which, q, m):
                bias = prm[:, layer, PLN + 16 * which + 8 + m:PLN + 16 * which + 9 + m]
                dve.wait_ge(x_hi, KD * (q + 1) + m + 1)
                V.scalar_tensor_tensor(out=xl[:, m, :], in0=mix[:, m, :], scalar=bias, in1=xh[:, m, :].bitcast(F32),
                                       op0=ALU.add, op1=ALU.subtract).then_inc(x_lo, 1)

            act_parts, splits = [0], [0]
            dve.wait_ge(setup_pool, 1)
            for layer in range(DEPTH):
                tile = 0
                for item, rows in zip(SCHEDULE, PHASE_TABLE):
                    if item[0] == "slot":
                        slot_i = item[1]
                        for i in range(tile - tiles_in(slot_i - 1) if slot_i else 0, tile):
                            evict_second(layer, i)
                        split_hi(layer * NSLOT + slot_i + RING - 1)
                        for _ in range(tiles_in(item[1])):
                            if frees(LTILES[tile]) == "dve":
                                n_free = freed("dve", layer * NTILE + tile - (sigmoids(LTILES[tile - 1]) if tile else 0))
                                if n_free:
                                    dve.wait_ge(tile_free["dve"], n_free)
                                if LTILES[tile][0] == "br":
                                    dve.wait_ge(tile_free["act"], freed("act", layer * NTILE + tile))
                            evict(layer, tile)
                            tile += 1
                        if SLOTS[item[1]] == ("br", "B", 6):
                            dve.wait_ge(tile_free["dve"], freed("dve", layer * NTILE + tile))
                            split_mix()
                        if ends_norm(item[1]) is not None:
                            dve.wait_ge(tile_free["dve"], freed("dve", layer * NTILE + tile))
                            layer_norm(layer, ends_norm(item[1]))
                        continue
                    for k, (engine, before, _) in enumerate(rows):
                        if engine != "dve":
                            continue
                        follow(dve, layer, before)
                        if k == 0:
                            settled(dve, layer, tile, slot_i)
                        phase(*item[1:], k, layer, lambda ins: ins.then_inc(mix_done["dve"], 1))

        @block.tensor
        def _(pe):
            M = nc.tensor.matmul

            def dense(out, hi, lo, xhi, xlo, start, stop):
                M(out, hi, xhi, start=start, stop=False)
                M(out, hi, xlo, start=False, stop=False)
                return M(out, lo, xhi, start=False, stop=stop)

            def tile_bank(layer, i):
                g = layer * NTILE + i
                if g >= BANKS:
                    e = frees(LTILES[(g - BANKS) % NTILE])
                    pe.wait_ge(tile_free[e], freed(e, g - BANKS + 1))
                return gps[g % BANKS]

            def slot(layer, i, tile):
                c = layer * NSLOT + i
                pe.wait_ge(lo_done, c + 1)
                kind, a, b = SLOTS[i]
                hi, lo = whi[:, c % RING], wlo[:, c % RING]
                if kind == "br":
                    if b == 0:
                        pe.wait_ge(mix_done["dve"], layer * PHASES_PER_LAYER["dve"] + mixer_end(a))
                    pair = Y_PAIR[a]
                    for j in range(2):
                        out = tile_bank(layer, tile + j)[:, 0:T]
                        for k in range(H):
                            last = dense(out, hi[:, 4 * j + k, :], lo[:, 4 * j + k, :], yh[:, pair, k, :],
                                         yl[:, pair, k, :], k == 0, k == H - 1)
                    last.then_inc(slot_done, 1)
                    return
                if kind == "down":
                    out = tile_bank(layer, tile)[:, 0:T] if b == 0 else gps[(layer * NTILE + tile) % BANKS][:, 0:T]
                else:
                    out = tile_bank(layer, tile)[:, 0:T]
                for k in range(KD):
                    if kind == "down":
                        f = KD * b + k
                        if a == 0:
                            up = LTILES.index(("up", f, 0))
                            pe.wait_ge(tile_free["dve"], freed("dve", layer * NTILE + up + 1))
                        xhi, xlo = ah[:, f, :], al[:, f, :]
                        first, end = f == 0, f == KF - 1
                    elif kind == "out":
                        if a == 0:
                            pe.wait_ge(mix_split, 2 * KD * layer + 2 * k + 2)
                        xhi, xlo = ah[:, k, :], al[:, k, :]
                        first, end = k == 0, k == KD - 1
                    else:
                        if i == 0 or (kind == "up" and a == 0):
                            pe.wait_ge(x_lo, KD * (2 * layer + (kind == "up")) + k + 1)
                        xhi, xlo = xh[:, k, :], xl[:, k, :]
                        first, end = k == 0, k == KD - 1
                    last = dense(out, hi[:, k, :], lo[:, k, :], xhi, xlo, first, end)
                if turns_values(i):
                    bank = tile_bank(layer, tile + 1)
                    pe.wait_ge(tile_free["act"], freed("act", layer * NTILE + tile))
                    last = turn(bank, vf[:, SLOTS[i - 1][2] % 2, :])
                last.then_inc(slot_done, 1)

            def mean_part(layer, which, m):
                kind = "down" if which else "out"
                t = LTILES.index((kind, m, 3 if which else 0))
                pe.wait_ge(tile_free["dve"], freed("dve", layer * NTILE + t + 1))
                return M(xp[0][:, 0:T], ones[:, 1, :], mix[:, m, :], start=m == 0, stop=m == KD - 1)

            def layer_norm(layer, which):
                q = 2 * layer + which
                mean_part(layer, which, KD - 1).then_inc(ln_mean, 1)
                for m in range(KD):
                    pe.wait_ge(ln_sq, KD * q + m + 1)
                    M(xp[1][:, 0:T], ones[:, 0, :], tt[:, m % BANKS, :], start=m == 0, stop=m == KD - 1).then_inc(ln_sqsum, 1)

            def turn(out_bank, src):
                for i, (lo, n) in enumerate(TILES):
                    last = nc.tensor.transpose(out_bank[0:n, i * P:(i + 1) * P], src[:, lo:lo + n], ident)
                return last

            def scores(bank, n, h):
                q, k = q_of(n, h), k_of(n, h)
                M(bank[:, 0:256], k[:, 0:P], q[:, 0:SEQ], start=True, stop=False, skip_group_check=True)
                M(bank[:, 256:384], k[:, P:SEQ], q[:, P:SEQ], start=False, stop=False, skip_group_check=True)
                return M(bank[0:NS, 384:SP4], k[:, SEQ:T], q[:, SEQ:T], start=False, stop=True, skip_group_check=True)

            def weigh(bank, lhs, h):
                M(bank[:, 0:256], lhs(0), pt[:, h, 0:256], start=True, stop=False, skip_group_check=True)
                M(bank[:, P:SEQ], lhs(1), pt[:, h, 256:384], start=False, stop=False, skip_group_check=True)
                return M(bank[:, SEQ:T], lhs(2), pt[0:NS, h, 384:SP4], start=False, stop=False, skip_group_check=True)

            def phase(stage, n, h, layer, done):
                if stage in ("c_level", "c_last"):
                    if stage == "c_last":
                        for hd in range(H):
                            last = M(xp[0][:, hd * P:(hd + 1) * P], z12[:, 0, hd, 0:P], z12[:, 0, hd, P:SEQ],
                                     start=hd == 0, stop=hd == H - 1, skip_group_check=True)
                        done(last)
                        return
                    for i in range(3 if h <= 1 else 2):
                        lo, w_ = TILES[i]
                        for hd in range(H):
                            if h == 0:
                                last = M(xp[i][0:w_, hd * w_:(hd + 1) * w_], z12[:, 1, hd, lo:lo + w_],
                                         z12[:, 0, hd, lo:lo + w_], start=hd == 0, stop=hd == H - 1, skip_group_check=True)
                                continue
                            m = LEVELS[h - 1]
                            z = z12[:, h % 2, hd, lo:lo + w_]
                            out = xp[i][0:w_, hd * w_ // 2:(hd + 1) * w_ // 2].rearrange("p (b m) -> p b m", m=m)
                            last = M(out, z, z.rearrange("p (b two m) -> p b two m", two=2, m=m)[:, :, 1, :],
                                     start=hd == 0, stop=hd == H - 1, skip_group_check=True)
                    done(last)
                elif stage == "a_gate":
                    for i, (lo, w_) in enumerate(TILES):
                        last = nc.tensor.transpose(xp[0][0:w_, 8 * i:8 * i + 8], iff_fm[:, lo:lo + w_], ident[0:8, 0:8])
                    done(last)
                elif stage == "a_cum":
                    M(xp[1][:, 0:4], c_("tri"), af[:, 0, :], start=True, stop=False, skip_group_check=True)
                    M(xp[1][:, 4:8], ones[:, 0, :], af[:, 0, :], start=False, stop=False, skip_group_check=True)
                    M(xp[1][:, 4:8], c_("tri"), af[:, 1, :], start=False, stop=False, skip_group_check=True)
                    done(M(xp[1][:, 8:12], c_("trib"), af[:, 2, :], start=False, stop=True, skip_group_check=True))
                elif stage == "a_row":
                    for i in range(3):
                        nc.tensor.transpose(xp[2][0:H, i * P:(i + 1) * P], gb[:, i, 0:H], ident)
                        last = nc.tensor.transpose(xp[3][0:H, i * P:(i + 1) * P], gb[:, i, H:2 * H], ident)
                    done(last)
                elif stage == "a_score":
                    sel = c_("sel", H)[:, h * P:(h + 1) * P]
                    for j, (col, src) in enumerate(((slice(0, 256), slice(0, 256)), (slice(256, 384), slice(P, SEQ)),
                                                    (slice(384, SP4), slice(SEQ, T)))):
                        M(xp[0][:, col], sel, row[:, 1, src], start=j == 0, stop=False, skip_group_check=True)
                    M(xp[0][:, 0:SP4], idb[:, :], negb[:, :], start=False, stop=True, skip_group_check=True)
                    scores(xp[1], n, h)
                    M(xp[2][:, 0:T], sel, row[:, 0, :], start=True, stop=False, skip_group_check=True)
                    done(M(xp[2][:, T:384], sel, wi[:, :], start=False, stop=True, skip_group_check=True))
                elif stage == "b_rope":
                    M(xp[0][:, 0:T], c_("perm"), zc[:, 0, h, :], start=True, stop=True)
                    done(M(xp[1][:, 0:T], c_("perm"), zc[:, 1, h, :], start=True, stop=True))
                elif stage == "b_score":
                    done(scores(xp[1], n, h))
                elif stage == "num":
                    j = layer * HEADS_PER_LAYER + state_of(n, h)
                    turn(xp[0], z12[:, 1, h, :] if n == "C" else k_of(n, h))
                    pe.wait_ge(s_in[j % 2], 16 * (j // 2 + 1))
                    weigh(xp[3], lambda i: v_of(n, h, i), h)
                    for b in range(NB):
                        s = slice(b * DS, (b + 1) * DS)
                        last = M(xp[3][:, SEQ + b * DS:SEQ + (b + 1) * DS], s0[:, j % 2, b, :], qw[:, h, s],
                                 start=False, stop=b == NB - 1, skip_group_check=True)
                    if n == "A":
                        weigh(xp[4], lambda i: ones[0:TILES[i][1], 0, :], h)
                        last = M(xp[4][:, SEQ:T], ones[:, 0, :], qn[:, :], start=False, stop=True, skip_group_check=True)
                    done(last)
                elif stage == "b_mean":
                    done(M(xp[4][:, 0:T], ones[:, 1, :], hh[:, :], start=True, stop=True))
                elif stage == "fin":
                    for i in range(2):
                        v = v_of(n, h, i) if n == "C" else vw[:, i, :]
                        M(xp[0][:, 0:P], kt[:, i, :], v, start=i == 0, stop=False, skip_group_check=True)
                    if n == "A":
                        for i in range(2):
                            M(xp[0][:, P:P + 1], kt[:, i, :], ee[:, (255, 383)[i]:(256, 384)[i]], start=False, stop=False,
                              skip_group_check=True)
                        M(xp[0][:, P + 1:P + 1 + NB], kt[0:NS, 2, :], ee[0:NS, 384 + DS - 1:SP4:DS], start=False,
                          stop=True, skip_group_check=True)
                    for i in range(2):
                        M(xp[1 + i][:, :], kt[0:NS, 2, :], vm[:, 4 * i:4 * i + 4, :], start=True, stop=True)
                    done(M(xp[4][:, 0:T], ones[:, 0, :], sq[:, :], start=True, stop=True))

            stages = 0
            for layer in range(DEPTH):
                tile = 0
                for item, rows in zip(SCHEDULE, PHASE_TABLE):
                    if item[0] == "slot":
                        slot_i = i = item[1]
                        kind, a, b = SLOTS[i]
                        if layer == 0 and turns_values(i):
                            pe.wait_ge(const_in, 48)
                        slot(layer, i, tile)
                        tile += tiles_in(i)
                        if kind == "out" and a:
                            mean_part(layer, 0, a - 1)
                        if kind == "down" and a and b == 0:
                            mean_part(layer, 1, a - 1)
                        if ends_norm(i) is not None:
                            layer_norm(layer, ends_norm(i))
                        continue
                    for k, (engine, before, _) in enumerate(rows):
                        if engine != "pe":
                            continue
                        if stages == 0:
                            pe.wait_ge(setup_pool, 1)
                            pe.wait_ge(setup_dve, 1)
                        stages += 1
                        follow(pe, layer, before)
                        settled(pe, layer, tile, slot_i)
                        phase(*item[1:], layer, lambda ins: ins.then_inc(mix_done["pe"], 1))


def constants():
    import numpy as np
    f = np.float64
    s, t = np.arange(P)[:, None], np.arange(P)[None, :]
    gamma = 1.0 - 2.0 ** (-5.0 - np.arange(H, dtype=f))
    c = np.zeros((P, NCONST + SP4), np.float32)

    def put(name, value, rows=P):
        off, n = CONST_AT[name]
        c[:rows, off:off + n] = np.asarray(value).reshape(rows, n)

    j, seq = np.arange(NS) % DS, np.arange(NS) // DS
    own = seq[:, None] == seq[None, :]
    see = own & (j[:, None] <= j[None, :])
    put("ident", s == t)
    put("perm", (s + P // 2) % P == t)
    put("tri", s <= t)
    trib = np.zeros((P, P))
    trib[:NS, :NS] = see
    put("trib", trib)
    put("diag", (s // 4 == t // 4) & (s <= t))
    for m in LEVELS:
        put(f"lv{m}", (s // (2 * m) == t // (2 * m)) & (s % (2 * m) < m) & (t % (2 * m) >= m))
    d = np.zeros((P, H, 320))
    for h in range(H):
        d[:, h, 0:P] = np.where(s <= t, gamma[h] ** np.maximum(t - s, 0).astype(f), 0)
        d[:, h, P:2 * P] = gamma[h] ** (t + P - s).astype(f)
        d[:NS, h, 2 * P:] = np.where(see, gamma[h] ** np.maximum(j[None, :] - j[:, None], 0).astype(f), 0)
    put("dtab", d)
    put("inter", np.broadcast_to(gamma[:, None] ** (j + 1.0)[None, :], (P, H, NS)))
    put("toend", np.stack([gamma[None, :] ** (SEQ - 1.0 - P * i - s) for i in range(2)], axis=2))
    in_seq = seq[:, None] == np.arange(NB)[None, :]
    put("seqmask", in_seq, NS)
    put("vmask", in_seq[:, None, :] * (gamma[None, :] ** (DS - 1.0 - j)[:, None])[:, :, None], NS)
    half = P // 2
    inv = np.float32(10000.0) ** (-np.arange(half, dtype=np.float32) / np.float32(half))
    pos = np.concatenate([np.arange(SEQ), 2048 + j]).astype(np.float32)
    ang = (pos[None, :] * inv[:, None]).astype(np.float32).astype(f)
    put("cos", np.concatenate([np.cos(ang), np.cos(ang)]))
    put("sin", np.concatenate([-np.sin(ang), np.sin(ang)]))
    scan = np.ones((P, T))
    scan[:, [0] + list(range(SEQ, T, DS))] = 0
    put("scan", scan)
    put("sel", (np.arange(H)[:, None, None] == np.arange(H)[None, :, None]) & np.ones((1, 1, P), bool), H)
    neg = np.zeros((P, SP4))
    neg[:, 0:P] = np.where(s <= t, 0, NEG)
    neg[:, 256:384] = neg[:, 0:P]
    neg[:NS, 384:] = np.where(see, 0, NEG)
    c[:, NCONST:] = neg
    return c


def kernel(x_prompt, x_sample, state_mlstm_C, state_mlstm_n, state_mlstm_m, state_ret, state_hgrn, state_conv,
           w_in, b_mlstm_gate, norm_a, norm_b, norm_c, lb_c, conv_w, w_branch, w_gate, b_gate, w_out, ln1_g, ln1_b,
           ln2_g, ln2_b, w_up, w_down):
    import concourse.bacc as bacc
    import numpy as np
    from concourse.bass_utils import run_bass_kernel_spmd as run

    a = lambda v: np.asarray(v)
    x_prompt, x_sample = a(x_prompt), a(x_sample)
    w_in, w_gate, w_branch, w_out, w_up, w_down = map(a, (w_in, w_gate, w_branch, w_out, w_up, w_down))

    w = np.empty((DEPTH, NSLOT, P, KD, P), np.float32)
    for layer in range(DEPTH):
        for i, (kind, p, q) in enumerate(SLOTS):
            if p == "ifA":
                src = np.zeros((DM, P), np.float32)
                src[:, 0:2 * H] = w_in[layer][:, IN_COL[p]:IN_COL[p] + 2 * H]
            elif kind == "in":
                src = w_in[layer][:, IN_COL[p] + q * P:IN_COL[p] + (q + 1) * P]
            elif kind == "gate":
                col = DM * BRANCH[p] + q * P
                src = w_gate[layer][:, col:col + P]
            elif kind == "br":
                src = w_branch[layer, BRANCH[p]][:, q * P:(q + 2) * P]
                w[layer, i] = src.reshape(H, P, 2, P).transpose(1, 2, 0, 3).reshape(P, KD, P)
                continue
            elif kind == "out":
                src = w_out[layer][:, p * P:(p + 1) * P]
            elif kind == "up":
                src = w_up[layer][:, p * P:(p + 1) * P]
            else:
                src = w_down[layer][q * DM:(q + 1) * DM, p * P:(p + 1) * P]
            w[layer, i] = src.reshape(KD, P, P).transpose(1, 0, 2)

    x = np.concatenate([x_prompt[0], x_sample.reshape(NS, DM)])
    x = np.ascontiguousarray(x.T.reshape(KD, P, T).transpose(1, 0, 2))
    col = lambda v: a(v).reshape(DEPTH, -1, P).transpose(2, 0, 1)
    par = np.concatenate([col(norm_a), col(norm_b), col(norm_c), col(conv_w), col(b_gate), col(ln1_g), col(ln1_b),
                          col(ln2_g), col(ln2_b), col(lb_c)], axis=2)
    ifb = a(b_mlstm_gate).T
    st = np.concatenate([a(state_hgrn), a(state_mlstm_C), a(state_ret)], axis=2).transpose(0, 2, 3, 1, 4)
    n0 = a(state_mlstm_n).transpose(3, 0, 2, 1)
    m0 = a(state_mlstm_m).transpose(2, 0, 1)
    cb = a(state_conv).reshape(DEPTH, NB, 2, H, P).transpose(4, 0, 3, 1, 2)

    nc = bacc.Bacc("TRN2", target_bir_lowering=False, num_devices=1)
    arrays, args = {}, []
    for name, v in (("w", w), ("x", x), ("cst", constants()), ("par", par), ("ifb", ifb), ("st", st), ("n0", n0),
                    ("m0", m0), ("cb", cb)):
        v = np.ascontiguousarray(v)
        arrays["in_" + name] = v
        args.append(nc.dram_tensor("in_" + name, v.shape, F32, kind="ExternalInput").ap())
    outs = {"y": (P, KD, T), "sp": (DEPTH, HEADS_PER_LAYER, P, P), "ss": (DEPTH, HEADS_PER_LAYER, P, NB, P),
            "n": (DEPTH, P, H, 1 + NB), "m": (DEPTH, H, 1 + NB), "c": (DEPTH, P, H, 1 + NB, 2)}
    for name, shape in outs.items():
        args.append(nc.dram_tensor("out_" + name, shape, F32, kind="ExternalOutput").ap())
    trunk(nc, *args)
    r = run(nc, [arrays], core_ids=[0]).results[0]
    y, sp, ss, n, m, c = (np.asarray(r["out_" + name]) for name in outs)

    y = y.transpose(2, 1, 0).reshape(T, DM)
    ss = ss.transpose(0, 3, 1, 2, 4)
    sp = sp[:, None]
    n = n.transpose(0, 3, 2, 1)
    m = m.transpose(0, 2, 1)
    c = c.transpose(0, 3, 4, 2, 1).reshape(DEPTH, 1 + NB, 2, H * P)
    copy = np.ascontiguousarray
    return (copy(y[:SEQ][None]), copy(y[SEQ:].reshape(NB, DS, DM)),
            copy(sp[:, :, 4:8]), copy(n[:, :1]), copy(m[:, :1]), copy(sp[:, :, 8:12]), copy(sp[:, :, 0:4]), copy(c[:, :1]),
            copy(ss[:, :, 4:8]), copy(n[:, 1:]), copy(m[:, 1:]), copy(ss[:, :, 8:12]), copy(ss[:, :, 0:4]), copy(c[:, 1:]))
```

```python
from contextlib import ExitStack

import concourse.bass as bass
from concourse import mybir

ALU = mybir.AluOpType
ACT = mybir.ActivationFunctionType
F32 = mybir.dt.float32
F32R = mybir.dt.float32r
BF16 = mybir.dt.bfloat16
U32 = mybir.dt.uint32

P = 128
DEPTH, SEQ, NB, DS = 2, 256, 8, 8
NS = NB * DS
T = SEQ + NS
H = 4
DM = 1024
KD = DM // P
KF = 4 * KD
ALPHA = (2 * DEPTH) ** 0.25
KSCALE = float(P) ** -0.5
EPS = 1e-5
CLAMP = 1.0 - 1e-6
NEG = -1e30
SP4 = 448
TILES = ((0, P), (P, P), (SEQ, NS))
RING = 3
PARTS = 4
BANKS = 3
LEVELS = (4, 8, 16, 32, 64)

PN, PCW, PBG, PLN, PLB = 0, 12, 24, 56, 88
NPAR = 92


def const_layout():
    at, off = {}, 0
    for name, n in (("ident", P), ("perm", P), ("tri", P), ("trib", P), ("diag", P), ("lv4", P), ("lv8", P),
                    ("lv16", P), ("lv32", P), ("lv64", P), ("dtab", H * 320), ("inter", H * NS),
                    ("toend", H * 2), ("seqmask", NB), ("vmask", H * NB), ("cos", T), ("sin", T),
                    ("scan", T), ("sel", H * P)):
        at[name] = (off, n)
        off += n
    return at, off


CONST_AT, NCONST = const_layout()


def slots_of_layer():
    s = []
    for kind in ("vC", "fC", "qC", "gC", "cD", "xD", "bD", "vA", "qA", "kA", "oA", "ifA"):
        s += [("in", kind, h) for h in range(1 if kind == "ifA" else H)]

    def mixed(n):
        for half in range(2):
            for m in range(4):
                s.append(("gate", n, 4 * half + m))
            for m in range(2):
                s.append(("br", n, 4 * half + 2 * m))

    mixed("C")
    for kind in ("vB", "qB", "kB", "gB"):
        s += [("in", kind, h) for h in range(H)]
    mixed("A")
    mixed("D")
    mixed("B")
    s += [("out", m, 0) for m in range(KD)]
    s += [("up", m, 0) for m in range(KF)]
    s += [("down", m, q) for m in range(KD) for q in range(4)]
    return s


SLOTS = slots_of_layer()
NSLOT = len(SLOTS)
IN_COL = {"ifA": 2048, "qA": 0, "kA": 512, "vA": 1024, "oA": 1536, "qB": 2056, "kB": 2568, "vB": 3080, "gB": 3592,
          "qC": 4104, "fC": 4616, "vC": 5128, "gC": 5640, "xD": 6152, "bD": 6664, "cD": 7176}
BRANCH = {"A": 0, "B": 1, "C": 2, "D": 3}
Y_PAIR = {"C": 0, "A": 1, "B": 0, "D": 1}
MIXERS = "CAB"


def tiles_of_layer():
    t = []
    for i, (kind, a, b) in enumerate(SLOTS):
        if kind == "br":
            t += [("br", a, b), ("br", a, b + 1)]
        elif kind != "down" or b == 3:
            t.append((kind, a, b))
        if turns_values(i):
            t.append(("vt", *SLOTS[i - 1][1:]))
    return t


def turns_values(i):
    return i > 0 and SLOTS[i - 1][0] == "in" and SLOTS[i - 1][1][0] == "v"


def sigmoids(tile):
    return tile[0] == "gate" or tile[0] == "in" and tile[1] in ("fC", "qC", "gC", "oA", "gB")


def crossed(i):
    return i > 0 and SLOTS[i][0] == SLOTS[i - 1][0] == "gate"


def frees(tile):
    kind, a, _ = tile
    if kind in ("gate", "vt"):
        return "act"
    return "dve" if kind != "in" or a in ("fC", "qC", "gC", "gB", "xD") else "act"


def hi_engine(c):
    return "dve" if c >= RING and sigmoids(SLOTS[(c - RING) % NSLOT]) else "act"


LTILES = tiles_of_layer()
NTILE = len(LTILES)


def freed(engine, n):
    full, rest = divmod(n, NTILE)
    per = sum(frees(t) == engine for t in LTILES)
    return full * per + sum(frees(t) == engine for t in LTILES[:rest])


def rounded(engine, n):
    return sum(hi_engine(c) == engine for c in range(n))


BEFORE = "before"
PHASES = {
    "c_log": (("dve", BEFORE), ("act", 0), ("dve", 1)),
    "c_first": (("dve", BEFORE), ("act", 0), ("dve", 1)),
    "c_level": (("pe", BEFORE), ("dve", 0), ("act", 1), ("dve", 0), ("dve", 2)),
    "c_last": (("pe", BEFORE), ("dve", 0), ("act", 1), ("dve", 0), ("dve", 2)),
    "a_gate": (("pe", BEFORE), ("dve", 0), ("act", 1), ("dve", 2)),
    "a_cum": (("pe", BEFORE), ("dve", 0)),
    "a_row": (("pe", BEFORE), ("dve", 0)),
    "a_exp": (("act", BEFORE),),
    "a_score": (("pe", ("fin", -1, 1)), ("dve", 0), ("act", 0), ("dve", 2)),
    "b_rope": (("pe", ("fin", -1, 1)), ("dve", 0)),
    "b_score": (("pe", ("b_rope", 0, 1)), ("dve", 0)),
    "numC": (("pe", ("fin", -1, 1)), ("act", (0, ("fin", -1, 3))), ("dve", 0)),
    "numA": (("pe", (("a_score", 0, 3), ("fin", -1, 2))), ("act", 0), ("dve", 1)),
    "a_sq": (("act", ("num", 0, 2)), ("dve", ("num", 0, 0))),
    "numB": (("pe", (("b_score", 0, 1), ("fin", -1, 2))), ("act", (0, ("fin", -1, 3))), ("dve", 0)),
    "b_mean": (("pe", ("num", 0, 1)), ("dve", 0), ("act", 1)),
    "finC": (("pe", (("num", 0, 1), ("num", 0, 2))), ("dve", 0), ("act", (0, ("fin", -1, 3))), ("dve", 2)),
    "finA": (("pe", (("a_sq", 0, 0), ("a_sq", 0, 1))), ("dve", 0), ("act", (0, ("fin", -1, 3))), ("dve", 2)),
    "finB": (("pe", (("b_mean", 0, 2), ("num", 0, 2))), ("dve", 0), ("act", (0, ("fin", -1, 3))), ("dve", 2)),
    "conv": (("dve", BEFORE),),
    "d_split": (("dve", BEFORE),),
}
COST = {"c_log": 1, "c_first": 1, "c_level": 2, "c_last": 4, "a_gate": 1, "a_cum": 1, "a_row": 2, "a_exp": 1,
        "a_score": 2, "b_rope": 2, "b_score": 1, "numC": 1, "numA": 2, "a_sq": 1, "numB": 1, "b_mean": 1,
        "finC": 2, "finA": 1, "finB": 1}


def phases(stage, n):
    return PHASES[stage if stage in PHASES else stage + n]


def schedule_of_layer():
    index = {s: i for i, s in enumerate(SLOTS)}
    last = lambda kind: index[("in", kind, H - 1)]
    chain = [("c_log", "C", h, last("fC") + 1) for h in range(2)]
    chain += [("c_first", "C", h, last("qC") + 1) for h in range(H)]
    chain += [("c_level", "C", i, last("gC") + 2) for i in range(len(LEVELS) + 1)] + [("c_last", "C", 0, last("gC") + 1)]
    for h in range(H):
        chain += [("num", "C", h, 0), ("fin", "C", h, 0)]
    chain += [("a_gate", "A", 0, index[("in", "ifA", 0)] + 1), ("a_cum", "A", 0, 0), ("a_row", "A", 0, 0), ("a_exp", "A", 0, 0)]
    for h in range(H):
        chain += [("a_score", "A", h, 0), ("num", "A", h, 0), ("a_sq", "A", h, 0), ("fin", "A", h, 0)]
    for h in range(H):
        chain += [("b_rope", "B", h, last("gB") + 3), ("b_score", "B", h, 0), ("num", "B", h, 0),
                  ("b_mean", "B", h, 0), ("fin", "B", h, last("gB") + 1)]
    before = {index[("gate", "C", 0)]: "C", index[("br", "A", 0)]: "A", index[("br", "B", 0)]: "B"}
    beside = {index[("in", "kA", 0)] + 3 * h - 1: ("mix", "conv", "D", h) for h in range(H)}
    beside.update({index[("gate", "D", h)]: ("mix", "d_split", "D", h) for h in range(2)})
    out, free_at = [], 0
    for i, slot in enumerate(SLOTS):
        if i in before:
            while any(c[1] == before[i] for c in chain):
                out.append(("mix", *chain.pop(0)[:3]))
        out.append(("slot", i))
        while chain and chain[0][3] <= i and free_at <= i:
            stage = chain.pop(0)
            out.append(("mix", *stage[:3]))
            name = stage[0] if stage[0] in COST else stage[0] + stage[1]
            free_at = max(free_at, i) + COST[name]
        if i in beside:
            out.append(beside[i])
    assert not chain
    return out


SCHEDULE = schedule_of_layer()


def phase_counts():
    done = {"pe": 0, "act": 0, "dve": 0}
    chain_done = {e: -1 for e in done}
    at, table = {}, []
    for item in SCHEDULE:
        if item[0] == "slot":
            table.append(None)
            continue
        _, stage, n, h = item
        if n == "D":
            before = [("dve", done["dve"] or -1)]
        else:
            before = list(chain_done.items())
        rows = []
        for j, (engine, refs) in enumerate(phases(stage, n)):
            waits = []
            for ref in refs if isinstance(refs, tuple) and not isinstance(refs[0], str) else (refs,):
                if ref == BEFORE:
                    waits += before
                elif isinstance(ref, int):
                    waits.append((rows[ref][0], rows[ref][2]))
                elif (ref[0], n, h + ref[1], ref[2]) in at:
                    waits.append(at[ref[0], n, h + ref[1], ref[2]])
                else:
                    waits += before
            done[engine] += 1
            rows.append((engine, waits, done[engine]))
            at[stage, n, h, j] = (engine, done[engine])
        if n != "D":
            chain_done = dict(done)
        table.append(rows)
    return table, done


PHASE_TABLE, PHASES_PER_LAYER = phase_counts()


def stages_behind(i):
    found, at = [], None
    for item, rows in zip(SCHEDULE, PHASE_TABLE):
        if item[0] == "slot":
            at = item[1]
        elif at == i:
            found.append((*item[1:], rows))
    return found


def mixer_end(n):
    return max(rows[-1][2] for item, rows in zip(SCHEDULE, PHASE_TABLE)
               if item[0] == "mix" and item[2] == n and item[1] in ("fin", "d_split"))


def tiles_in(i):
    kind, _, b = SLOTS[i]
    return 2 if kind == "br" else int(kind != "down" or b == 3) + turns_values(i)


def slot_of_tile():
    return [i for i in range(NSLOT) for _ in range(tiles_in(i))]


TILE_SLOT = slot_of_tile()


def ends_norm(i):
    return {("out", KD - 1, 0): 0, ("down", KD - 1, 3): 1}.get(SLOTS[i])


def norm_input(i):
    kind, a, b = SLOTS[i]
    if kind == "out":
        return a, 0
    return (a, 1) if kind == "down" and b == 3 else (None, None)


def paired(i):
    return i == 1 or SLOTS[i] in (("out", 1, 0), ("up", 1, 0))


HALF = KD // 2
SHIFT_DVE = 3
HEADS_PER_LAYER = 3 * H


def trunk(nc, w, x, cst, par, ifb, st, n0, m0, cb, y_out, sp_out, ss_out, n_out, m_out, c_out):
    with ExitStack() as ctx:
        def sb(name, shape, dt=F32, where=ctx):
            return where.enter_context(nc.sbuf_tensor(name, shape, dt))

        def sem(name):
            return ctx.enter_context(nc.semaphore(name))

        xh = sb("xh", [P, KD, T], F32R)
        xl = sb("xl", [P, KD, T], F32R)
        raw = sb("raw", [P, RING, KD, P])
        whi = sb("whi", [P, RING, KD, P], F32R)
        wlo = sb("wlo", [P, RING, KD, P], F32R)
        with ExitStack() as early:
            zc = sb("zc", [P, 4, H, T], F32, early)
            vc = sb("vc", [P, H, 3, P], F32, early)
            za = sb("za", [P, 3, H, T], F32, early)
            va = sb("va", [P, H, 3, P], F32, early)
            ud = sb("ud", [P, H, SEQ + 2 + NB * (DS + 2)], F32, early)
            bd = sb("bd", [P, H, T], F32, early)
            yh = sb("yh", [P, 2, H, T], F32R, early)
            yl = sb("yl", [P, 2, H, T], F32R, early)
            vf = sb("vf", [P, 2, T], F32, early)
        ah = sb("ah", [P, KF, T], F32R)
        al = sb("al", [P, KF, T], F32R)
        pt = sb("pt", [P, H, SP4])
        mix = sb("mix", [P, KD, T])
        z12 = mix[:, :, :].rearrange("p (a h) t -> p a h t", a=2)
        gt = zc[:, 2, :, :]
        s0 = sb("s0", [P, 2, NB, P])
        ee = sb("ee", [P, SP4])
        vm = sb("vm", [NS, NB, P])
        kt = sb("kt", [P, 3, P])
        vw = sb("vw", [P, 2, P])
        pst = sb("pst", [P, 2, P])
        hh = sb("hh", [P, T])
        sq = sb("sq", [P, T])
        rs = sb("rs", [P, T])
        tt = sb("tt", [P, BANKS, T])
        qw = sb("qw", [P, H, NS])
        qn = sb("qn", [P, NS])
        dec = sb("dec", [P, H, NB])
        con = sb("con", [P, NCONST])
        ones = sb("ones", [P, 2, P])
        negb = sb("negb", [P, SP4], BF16)
        idb = sb("idb", [P, P], BF16)
        prm = sb("prm", [P, DEPTH, NPAR])
        oml = sb("oml", [P, DEPTH, H])
        bif = sb("bif", [2 * H, DEPTH])
        iff_fm = sb("iff_fm", [2 * H, T])
        n0s = sb("n0s", [P, DEPTH, H, NB])
        nou = sb("nou", [P, H, 1 + NB])
        m0s = sb("m0s", [H, DEPTH, NB])
        row = sb("row", [H, 2, T])
        wi = sb("wi", [H, NS])
        mou = sb("mou", [H, 1 + NB])
        cbs = sb("cbs", [P, DEPTH, H, NB, 2])
        cou = sb("cou", [P, H, 1 + NB, 2])
        iff = sb("iff", [P, 3, 2 * H])
        gb = sb("gb", [P, 3, 2 * H])
        af = sb("af", [P, 3, H])
        eps = sb("eps", [P, 1])
        gps = [ctx.enter_context(nc.psum_tensor(f"gps{i}", [P, 512], F32)) for i in range(BANKS)]
        xp = [ctx.enter_context(nc.psum_tensor(f"xp{i}", [P, 512], F32)) for i in range(5)]

        def c_(name, rows=P):
            off, n = CONST_AT[name]
            return con[0:rows, off:off + n]

        ident = c_("ident")

        first_in, const_in, small_in = sem("first_in"), sem("const_in"), sem("small_in")
        x_in = [sem(f"x_in{i}") for i in range(KD // 2)]
        raw_in = [sem(f"raw_in{i}") for i in range(RING)]
        lo_done, slot_done = sem("lo_done"), sem("slot_done")
        hi_done = {"act": sem("hi_done_act"), "dve": sem("hi_done_dve")}
        tile_free = {"act": sem("tile_free_act"), "dve": sem("tile_free_dve")}
        act_part = sem("act_part")
        dve_part = sem("dve_part")
        mix_done = {e: sem(f"mix_done_{e}") for e in ("pe", "act", "dve")}
        setup_dve, setup_act, setup_lb, setup_pool = sem("setup_dve"), sem("setup_act"), sem("setup_lb"), sem("setup_pool")
        x_hi, x_lo = sem("x_hi"), sem("x_lo")
        dve_chain, act_chain = sem("dve_chain"), sem("act_chain")
        mix_split = sem("mix_split")
        ln_half, ln_center, ln_sq, ln_sqsum = sem("ln_half"), sem("ln_center"), sem("ln_sq"), sem("ln_sqsum")
        ln_sum, ln_added = sem("ln_sum"), sem("ln_added")
        ln_mean, ln_shift, ln_shifted = sem("ln_mean"), sem("ln_shift"), sem("ln_shifted")
        ln_var, ln_rstd, ln_scaled, y_ready = sem("ln_var"), sem("ln_rstd"), sem("ln_scaled"), sem("y_ready")
        s_out, small_out, y_sent = sem("s_out"), sem("small_out"), sem("y_sent")
        s_in = [sem("s_in0"), sem("s_in1")]
        block = ctx.enter_context(nc.Block())

        def q_of(n, h):
            return (za if n == "A" else zc)[:, 0, h, :]

        def k_of(n, h):
            return (za if n == "A" else zc)[:, 1, h, :]

        def v_of(n, h, tile):
            rows = TILES[tile][1]
            return (va if n == "A" else vc)[0:rows, h, tile, :]

        def state_of(n, h):
            return H * MIXERS.index(n) + h if n in MIXERS else None

        def blocks(ap, lo, hi, m):
            return ap[:, :, lo:hi].rearrange("p h (b two m) -> p h b two m", two=2, m=m)

        def per_seq(ap):
            return ap.rearrange("p (b t) -> p b t", t=DS)

        def sample_u(h):
            return ud[:, h, SEQ + 2:SEQ + 2 + NB * (DS + 2)].rearrange("p (b t) -> p b t", t=DS + 2)

        def follow(eng, layer, waits):
            for e, count in waits:
                count = layer * PHASES_PER_LAYER[e] + max(count, 0)
                if count:
                    eng.wait_ge(mix_done[e], count)

        def centered(eng, layer, which, m):
            if m <= HALF:
                eng.wait_ge(ln_center, (HALF + 2) * (2 * layer + which) + m + 1)
            else:
                t = LTILES.index(("down", m, 3) if which else ("out", m, 0))
                eng.wait_ge(tile_free["dve"], freed("dve", layer * NTILE + t + 1))

        def settled(eng, layer, tile, i):
            n = layer * NTILE + tile - tiles_in(i) - crossed(i)
            for e in ("act", "dve"):
                if freed(e, n):
                    eng.wait_ge(tile_free[e], freed(e, n))

        @block.sync
        def _(sp):
            sp.dma_start(raw[:, 0, :, :], w[0, 0]).then_inc(raw_in[0], 16)
            for i in range(KD // 2):
                sp.dma_start(mix[:, 2 * i:2 * i + 2, :], x[:, 2 * i:2 * i + 2, :]).then_inc(x_in[i], 16)
            for c in range(1, RING):
                sp.dma_start(raw[:, c, :, :], w[0, c]).then_inc(raw_in[c], 16)
            sp.dma_start(ident, cst[:, 0:P]).then_inc(first_in, 16)
            sp.dma_start(prm[:, :, :], par).then_inc(first_in, 16)
            for layer in range(DEPTH):
                for i in range(NSLOT):
                    c = layer * NSLOT + i + RING
                    if c < DEPTH * NSLOT:
                        sp.wait_ge(lo_done, c - RING + 1)
                        sp.dma_start(raw[:, c % RING, :, :], w[c // NSLOT, c % NSLOT]).then_inc(raw_in[c % RING], 16)
                    if layer == 0 and 1 <= i < 1 + PARTS:
                        part = slice(P + (i - 1) * (NCONST - P) // PARTS, P + i * (NCONST - P) // PARTS)
                        sp.dma_start(con[:, part], cst[:, part]).then_inc(const_in, 16)
                    if layer == 0 and i == 1 + PARTS:
                        sp.dma_start(ee[:, :], cst[:, NCONST:NCONST + SP4]).then_inc(const_in, 16)
                        for dst, src in ((bif[:, :], ifb), (n0s[:, :, :, :], n0), (m0s[:, :, :], m0),
                                         (cbs[:, :, :, :, :], cb)):
                            sp.dma_start(dst, src).then_inc(small_in, 16)
                    if layer == 0 and i in (6, 7):
                        sp.dma_start(s0[:, i - 6, :, :], st[0, i - 6]).then_inc(s_in[i - 6], 16)
                    for stage, n, h, rows in stages_behind(i - 1):
                        if stage == "fin":
                            sp.wait_ge(mix_done["dve"], layer * PHASES_PER_LAYER["dve"] + rows[1][2])
                            j = state_of(n, h)
                            sp.dma_start(ss_out[layer, j], s0[:, j % 2, :, :]).then_inc(s_out, 16)
                            sp.dma_start(sp_out[layer, j], pst[:, j % 2, :]).then_inc(s_out, 16)
                            if n == "A" and h == H - 1:
                                sp.dma_start(n_out[layer], nou[:, :, :]).then_inc(small_out, 16)
                                sp.dma_start(m_out[layer], mou[:, :]).then_inc(small_out, 16)
                        if stage == "conv" and h == H - 1:
                            sp.wait_ge(mix_done["dve"], layer * PHASES_PER_LAYER["dve"] + rows[-1][2])
                            sp.dma_start(c_out[layer], cou[:, :, :, :]).then_inc(small_out, 16)
                    for stage, n, h, _ in stages_behind(i - 2):
                        j = layer * HEADS_PER_LAYER + state_of(n, h) + 2 if stage == "fin" else DEPTH * HEADS_PER_LAYER
                        if j < DEPTH * HEADS_PER_LAYER:
                            sp.wait_ge(s_out, 32 * (j - 1))
                            sp.dma_start(s0[:, j % 2, :, :],
                                         st[j // HEADS_PER_LAYER, j % HEADS_PER_LAYER]).then_inc(s_in[j % 2], 16)
            for m in range(KD):
                sp.wait_ge(y_ready, m + 1)
                sp.dma_start(y_out[:, m, :], mix[:, m, :]).then_inc(y_sent, 16)
            sp.wait_ge(y_sent, 16 * KD)
            sp.wait_ge(s_out, 32 * DEPTH * HEADS_PER_LAYER)
            sp.wait_ge(small_out, 16 * 3 * DEPTH)

        @block.gpsimd
        def _(pool):
            nc.gpsimd.memset(ones[:, 0, :], 1.0)
            nc.gpsimd.memset(ones[:, 1, :], 1.0 / P)
            nc.gpsimd.memset(pt[:, :, :], 0.0)
            nc.gpsimd.memset(iff[:, :, :], 0.0).then_inc(setup_pool, 1)

            def shift(q):
                pool.wait_ge(ln_shift, 2 * q + 1)
                for m in range(SHIFT_DVE, KD):
                    pool.wait_ge(ln_sq, KD * q + m + 1)
                    nc.gpsimd.tensor_tensor(mix[:, m, :], mix[:, m, :], sq[:, :], ALU.subtract).then_inc(ln_shifted, 1)

            for c in range(DEPTH * NSLOT):
                if c >= RING and ends_norm((c - RING) % NSLOT) is not None:
                    shift(2 * ((c - RING) // NSLOT) + ends_norm((c - RING) % NSLOT))
                pool.wait_ge(hi_done[hi_engine(c)], rounded(hi_engine(c), c + 1))
                nc.gpsimd.tensor_tensor(wlo[:, c % RING, :, :], raw[:, c % RING, :, :],
                                        whi[:, c % RING, :, :].bitcast(F32), ALU.subtract).then_inc(lo_done, 1)
            shift(2 * DEPTH - 1)

        @block.scalar
        def _(act):
            nc.scalar.preload_act_table_set("natural_log_exp_and_others")
            chain = [0]

            def link(ins):
                chain[0] += 1
                ins.then_inc(act_chain, 1)
                act.wait_ge(act_chain, chain[0])

            def split_hi(c):
                if c >= DEPTH * NSLOT or hi_engine(c) != "act":
                    return
                act.wait_ge(raw_in[c % RING], 16 * (c // RING + 1))
                if c >= RING:
                    act.wait_ge(slot_done, c - RING + 1)
                nc.scalar.activation(whi[:, c % RING, :, :], raw[:, c % RING, :, :],
                                     ACT.Copy).then_inc(hi_done["act"], 1)

            def evict(layer, i):
                g = layer * NTILE + i
                kind, a, b = LTILES[i]
                bank = gps[g % BANKS]
                ps = bank[:, 0:T]
                t = tt[:, g % BANKS, :]
                if kind in ("br", "out", "down") or a == "xD":
                    return
                act.wait_ge(slot_done, layer * NSLOT + TILE_SLOT[i] + 1)
                free = tile_free["act"]
                if kind == "vt":
                    v = va if a == "vA" else vc
                    nc.scalar.activation(v[:, b, 0:2, :], bank[:, 0:2 * P].rearrange("p (a c) -> p a c", a=2), ACT.Copy)
                    nc.scalar.activation(v[0:NS, b, 2, :], bank[0:NS, 2 * P:3 * P], ACT.Copy).then_inc(free, 1)
                elif kind == "up":
                    nc.scalar.activation(t, ps, ACT.Relu).then_inc(act_part, 1)
                elif sigmoids(LTILES[i]):
                    if kind == "gate":
                        j = KD * BRANCH[a] + b
                        link(nc.scalar.activation(t, ps, ACT.Abs, bias=prm[:, layer, PBG + j:PBG + j + 1]))
                    else:
                        link(nc.scalar.activation(t, ps, ACT.Abs))
                    link(nc.scalar.activation(t, t, ACT.Exp, scale=-1.0))
                    nc.scalar.activation(t, t, ACT.Ln, bias=1.0).then_inc(act_part, 1)
                elif a[0] == "v":
                    nc.scalar.activation(vf[:, b % 2, :], ps, ACT.Copy).then_inc(free, 1)
                elif a == "ifA":
                    nc.scalar.activation(iff_fm[:, :], bank[0:2 * H, 0:T], ACT.Identity,
                                         bias=bif[:, layer:layer + 1]).then_inc(free, 1)
                elif a in ("qA", "kA", "qB", "kB"):
                    dst = (q_of if a[0] == "q" else k_of)(a[1], b)
                    nc.scalar.activation(dst, ps, ACT.Copy, scale=KSCALE if a[0] == "k" else 1.0).then_inc(free, 1)
                else:
                    nc.scalar.activation(bd[:, b, :], ps, ACT.Copy).then_inc(free, 1)

            def evict_second(layer, i):
                if not sigmoids(LTILES[i]):
                    return
                g = layer * NTILE + i
                kind, a, b = LTILES[i]
                t = tt[:, g % BANKS, :]
                seconds[0] += 1
                act.wait_ge(dve_part, seconds[0])
                if kind == "gate":
                    nc.scalar.activation(gt[:, b % 4, :], t, ACT.Exp).then_inc(tile_free["act"], 1)
                elif a == "oA":
                    nc.scalar.activation(za[:, 2, b, :], t, ACT.Exp).then_inc(tile_free["act"], 1)
                else:
                    nc.scalar.activation(t, t, ACT.Exp, scale=-1.0 if a == "fC" else 1.0).then_inc(act_part, 1)

            def phase(stage, n, h, k, layer, done):
                if stage == "c_log":
                    z = z12[:, 0, 2 * h:2 * h + 2, :]
                    done(nc.scalar.activation(z, z, ACT.Ln, scale=-1.0, bias=1.0))
                elif stage == "c_first":
                    nc.scalar.activation(z12[:, 1, h, :], z12[:, 0, h, :], ACT.Exp, scale=-1.0)
                    done(nc.scalar.activation(z12[:, 0, h, :], z12[:, 0, h, :], ACT.Exp))
                elif stage == "c_level":
                    hi = T if LEVELS[h:] and LEVELS[h] == DS // 2 else SEQ
                    z = z12[:, (h + 1) % 2, :, 0:hi]
                    done(nc.scalar.activation(z, z, ACT.Exp))
                elif stage == "c_last":
                    nc.scalar.activation(z12[:, 1, :, :], z12[:, 1, :, :], ACT.Exp)
                    nc.scalar.activation(qw[:, :, :], zc[:, 2, :, SEQ:T], ACT.Exp)
                    done(nc.scalar.activation(dec[:, :, :], zc[:, 2, :, SEQ + DS - 1:T:DS], ACT.Exp))
                elif stage == "a_gate":
                    link(nc.scalar.activation(af[:, :, :], iff[:, :, H:2 * H], ACT.Abs))
                    link(nc.scalar.activation(af[:, :, :], af[:, :, :], ACT.Exp, scale=-1.0))
                    done(nc.scalar.activation(af[:, :, :], af[:, :, :], ACT.Ln, bias=1.0))
                elif stage == "a_exp":
                    nc.scalar.activation(row[:, 0, :], row[:, 0, :], ACT.Exp, scale=-1.0)
                    done(nc.scalar.activation(wi[:, :], wi[:, :], ACT.Exp))
                elif stage == "a_score":
                    nc.scalar.activation(ee[:, 0:256], xp[0][:, 0:256], ACT.Exp, bias=gb[:, 0, h:h + 1])
                    nc.scalar.activation(ee[:, 256:384], xp[0][:, 256:384], ACT.Exp, bias=gb[:, 1, h:h + 1])
                    done(nc.scalar.activation(ee[0:NS, 384:SP4], xp[0][0:NS, 384:SP4], ACT.Exp, bias=gb[0:NS, 2, h:h + 1]))
                elif stage == "num" and k == 1:
                    nc.scalar.activation(kt[:, 0:2, :], xp[0][:, 0:2 * P].rearrange("p (a c) -> p a c", a=2), ACT.Copy)
                    nc.scalar.activation(kt[0:NS, 2, :], xp[0][0:NS, 2 * P:3 * P], ACT.Copy)
                    if n == "A":
                        done(nc.scalar.activation(sq[:, :], xp[4][:, 0:T], ACT.Abs))
                    elif n == "B":
                        done(nc.scalar.activation(hh[:, :], xp[3][:, 0:T], ACT.Copy))
                    else:
                        nc.scalar.activation(sq[:, :], xp[3][:, 0:T], ACT.Square)
                        done(nc.scalar.activation(hh[:, :], xp[3][:, 0:T], ACT.Copy))
                elif stage in ("a_sq", "b_mean"):
                    done(nc.scalar.activation(sq[:, :], hh[:, :], ACT.Square))
                elif stage == "fin":
                    link(nc.scalar.activation(rs[:, :], xp[4][:, 0:T], ACT.Ln, scale=1.0 / P, bias=eps[:, 0:1]))
                    done(nc.scalar.activation(rs[:, :], rs[:, :], ACT.Exp, scale=-0.5))

            def squares(layer, which, m):
                for j in {HALF: range(3), HALF + 1: range(3, HALF + 2)}.get(m, range(m, m + 1) if m > HALF else ()):
                    e = KD * (2 * layer + which) + j
                    centered(act, layer, which, j)
                    if j >= BANKS:
                        act.wait_ge(ln_added, (KD - 2) * (2 * layer + which) + max(j - BANKS, 1))
                    nc.scalar.activation(tt[:, j % BANKS, :], mix[:, j, :], ACT.Square).then_inc(ln_sq, 1)

            def layer_norm(layer, which):
                q = 2 * layer + which
                act.wait_ge(ln_mean, q + 1)
                nc.scalar.activation(sq[:, :], xp[1][:, 0:T], ACT.Copy, scale=1.0 / KD).then_inc(ln_shift, 1)
                nc.scalar.activation(hh[:, :], xp[1][:, 0:T], ACT.Square, scale=1.0 / KD).then_inc(ln_shift, 1)
                act.wait_ge(ln_var, q + 1)
                link(nc.scalar.activation(rs[:, :], rs[:, :], ACT.Ln, bias=eps[:, 0:1]))
                nc.scalar.activation(rs[:, :], rs[:, :], ACT.Exp, scale=-0.5).then_inc(ln_rstd, 1)
                for m in range(KD):
                    act.wait_ge(ln_scaled, KD * q + m + 1)
                    bias = prm[:, layer, PLN + 16 * which + 8 + m:PLN + 16 * which + 9 + m]
                    if q == 2 * DEPTH - 1:
                        nc.scalar.activation(mix[:, m, :], mix[:, m, :], ACT.Identity, bias=bias).then_inc(y_ready, 1)
                    else:
                        nc.scalar.activation(xh[:, m, :], mix[:, m, :], ACT.Identity, bias=bias).then_inc(x_hi, 1)

            split_hi(0)
            for k in range(KD):
                act.wait_ge(x_in[k // 2], 16)
                nc.scalar.activation(xh[:, k, :], mix[:, k, :], ACT.Copy).then_inc(x_hi, 1)
            split_hi(1)
            split_hi(2)

            seconds = [0]
            for layer in range(DEPTH):
                tile = 0
                for item, rows in zip(SCHEDULE, PHASE_TABLE):
                    if item[0] == "slot":
                        slot_i = item[1]
                        earlier = range(tile - tiles_in(slot_i - 1) if slot_i else 0, tile)
                        if not crossed(slot_i):
                            for i in earlier:
                                evict_second(layer, i)
                        split_hi(layer * NSLOT + slot_i + RING)
                        for _ in range(tiles_in(item[1])):
                            evict(layer, tile)
                            tile += 1
                        if crossed(slot_i):
                            for i in earlier:
                                evict_second(layer, i)
                        if layer == 0 and slot_i == H - 1:
                            act.wait_ge(setup_lb, 1)
                            nc.scalar.activation(oml[:, 1, :], oml[:, 0, :], ACT.Exp).then_inc(setup_act, 1)
                            act.wait_ge(setup_dve, 1)
                        if layer == 0 and slot_i == 3 * H - 1:
                            act.wait_ge(setup_dve, 2)
                        m, which = norm_input(slot_i)
                        if m is not None:
                            squares(layer, which, m)
                        if ends_norm(item[1]) is not None:
                            layer_norm(layer, ends_norm(item[1]))
                        continue
                    for k, (engine, before, _) in enumerate(rows):
                        if engine != "act":
                            continue
                        follow(act, layer, before)
                        if k == 0:
                            settled(act, layer, tile, slot_i)
                        phase(*item[1:], k, layer, lambda ins: ins.then_inc(mix_done["act"], 1))

        @block.vector
        def _(dve):
            V = nc.vector
            chain = [0]

            def link(ins):
                chain[0] += 1
                ins.then_inc(dve_chain, 1)
                dve.wait_ge(dve_chain, chain[0])

            for k in range(KD):
                dve.wait_ge(x_hi, k + 1)
                V.tensor_tensor(xl[:, k, :], mix[:, k, :], xh[:, k, :].bitcast(F32), ALU.subtract).then_inc(x_lo, 1)
            dve.wait_ge(first_in, 32)
            V.tensor_copy(idb[:, :], ident)
            V.memset(eps[:, :], EPS)
            V.tensor_tensor(oml[:, 0, :], prm[:, 1, PLB:PLB + H], prm[:, 0, PLB:PLB + H], ALU.subtract).then_inc(setup_lb, 1)
            dve.wait_ge(setup_act, 1)
            link(V.tensor_scalar_add(oml[:, 1, :], oml[:, 1, :], 1.0))
            link(V.reciprocal(oml[:, 1, :], oml[:, 1, :]))
            V.memset(oml[:, 0, :], 1.0).then_inc(setup_dve, 1)
            dve.wait_ge(setup_dve, 1)

            def split_hi(c):
                if c >= DEPTH * NSLOT or hi_engine(c) != "dve":
                    return
                dve.wait_ge(raw_in[c % RING], 16 * (c // RING + 1))
                dve.wait_ge(slot_done, c - RING + 1) if c >= RING else None
                V.tensor_copy(whi[:, c % RING, :, :], raw[:, c % RING, :, :]).then_inc(hi_done["dve"], 1)

            def evict_second(layer, i):
                kind, a, b = LTILES[i]
                if not sigmoids(LTILES[i]) or kind == "gate" or a == "oA":
                    return
                g = layer * NTILE + i
                t = tt[:, g % BANKS, :]
                act_parts[0] += 1
                dve.wait_ge(act_part, act_parts[0])
                if a == "fC":
                    V.tensor_scalar(zc[:, 1, b, :], t, oml[:, layer, b:b + 1], None, ALU.mult).then_inc(tile_free["dve"], 1)
                else:
                    V.tensor_tensor(zc[:, 0 if a == "qC" else 3, b, :], gps[g % BANKS][:, 0:T], t,
                                    ALU.mult).then_inc(tile_free["dve"], 1)

            def evict(layer, i):
                g = layer * NTILE + i
                kind, a, b = LTILES[i]
                if frees(LTILES[i]) != "dve" and not sigmoids(LTILES[i]):
                    return
                ps = gps[g % BANKS][:, 0:T]
                t = tt[:, g % BANKS, :]
                free = tile_free["dve"]
                if kind in ("out", "down"):
                    link(V.tensor_tensor(mix[:, a, :], xh[:, a, :].bitcast(F32), xl[:, a, :].bitcast(F32), ALU.add))
                    if a > HALF:
                        link(V.scalar_tensor_tensor(out=mix[:, a, :], in0=mix[:, a, :], scalar=ALPHA, in1=hh[:, :],
                                                    op0=ALU.mult, op1=ALU.subtract))
                    else:
                        link(V.tensor_scalar(mix[:, a, :], mix[:, a, :], ALPHA, None, ALU.mult))
                if kind in ("br", "out", "down") or a == "xD":
                    dve.wait_ge(slot_done, layer * NSLOT + TILE_SLOT[i] + 1)
                else:
                    act_parts[0] += 1
                    dve.wait_ge(act_part, act_parts[0])
                if kind == "up":
                    link(V.tensor_tensor(t, t, t, ALU.mult))
                    link(V.tensor_copy(ah[:, a, :], t))
                    V.tensor_tensor(al[:, a, :], t, ah[:, a, :].bitcast(F32), ALU.subtract).then_inc(free, 1)
                elif kind in ("out", "down"):
                    V.tensor_tensor(mix[:, a, :], mix[:, a, :], ps, ALU.add).then_inc(free, 1)
                elif kind == "gate":
                    j = KD * BRANCH[a] + b
                    link(V.tensor_scalar(gt[:, b % 4, :], ps, prm[:, layer, PBG + j:PBG + j + 1], 0.0, ALU.add, ALU.min))
                    V.tensor_tensor(t, gt[:, b % 4, :], t, ALU.subtract).then_inc(dve_part, 1)
                elif kind == "br":
                    if a == "C":
                        V.tensor_tensor(mix[:, b, :], ps, gt[:, b % 4, :], ALU.mult).then_inc(free, 1)
                    else:
                        link(V.tensor_tensor(t, ps, gt[:, b % 4, :], ALU.mult))
                        V.tensor_tensor(mix[:, b, :], mix[:, b, :], t, ALU.add).then_inc(free, 1)
                elif a == "xD":
                    V.memset(ud[:, b, 0:2], 0.0)
                    V.tensor_tensor(ud[:, b, 2:2 + SEQ], ps[:, 0:SEQ], bd[:, b, 0:SEQ], ALU.mult)
                    V.tensor_copy(sample_u(b)[:, :, 0:2], cbs[:, layer, b, :, :])
                    V.tensor_tensor(sample_u(b)[:, :, 2:2 + DS], per_seq(ps[:, SEQ:T]), per_seq(bd[:, b, SEQ:T]),
                                    ALU.mult).then_inc(free, 1)
                elif a == "fC":
                    V.scalar_tensor_tensor(out=t, in0=ps, scalar=0.0, in1=t, op0=ALU.max, op1=ALU.add).then_inc(dve_part, 1)
                else:
                    V.scalar_tensor_tensor(out=t, in0=ps, scalar=0.0, in1=t, op0=ALU.min,
                                           op1=ALU.subtract).then_inc(dve_part, 1)

            def split_mix(m):
                V.tensor_copy(ah[:, m, :], mix[:, m, :]).then_inc(mix_split, 1)
                splits[0] += 1
                dve.wait_ge(mix_split, splits[0])
                V.tensor_tensor(al[:, m, :], mix[:, m, :], ah[:, m, :].bitcast(F32), ALU.subtract).then_inc(mix_split, 1)
                splits[0] += 1

            def spans(m):
                return [(0, SEQ)] + ([(SEQ, T)] if m == DS // 2 else [])

            def distances(m, buf):
                for lo, hi in spans(m):
                    b = blocks(zc[:, 2, :, :], lo, hi, m)
                    z = blocks(z12[:, buf, :, :], lo, hi, m)
                    mid = b[:, :, :, 0, m - 1:m].to_broadcast([P, H, (hi - lo) // (2 * m), m])
                    V.tensor_tensor(z[:, :, :, 0, :], mid, b[:, :, :, 0, :], ALU.subtract)
                    last = V.tensor_tensor(z[:, :, :, 1, :], b[:, :, :, 1, :], mid, ALU.subtract)
                return last

            def apply_qk(m, buf):
                for lo, hi in spans(m):
                    z = blocks(z12[:, buf, :, :], lo, hi, m)
                    q = blocks(zc[:, 0, :, :], lo, hi, m)
                    k = blocks(zc[:, 1, :, :], lo, hi, m)
                    V.tensor_tensor(z[:, :, :, 0, :], z[:, :, :, 0, :], k[:, :, :, 0, :], ALU.mult)
                    last = V.tensor_tensor(z[:, :, :, 1, :], z[:, :, :, 1, :], q[:, :, :, 1, :], ALU.mult)
                return last

            def take(level):
                m = LEVELS[level - 1] if level else P
                mask = c_(f"lv{m}" if level else "diag").bitcast(U32)

                def late(ap, width):
                    if not level:
                        return ap
                    return ap.rearrange("p (b two m) -> p b two m", two=2, m=m)[:, :, 1, :]

                for tile, col in ((0, 0), (1, 256), (2, 384)):
                    rows, w_ = (NS, NS) if tile == 2 else (P, P)
                    if tile == 2 and level > 1:
                        continue
                    if not level:
                        last = V.copy_predicated(pt[0:rows, :, col:col + w_],
                                          mask[0:rows, 0:w_].unsqueeze(1).to_broadcast([rows, H, w_]),
                                          xp[tile][0:rows, 0:H * w_].rearrange("p (h t) -> p h t", h=H))
                        continue
                    nb = w_ // (2 * m)
                    last = V.copy_predicated(blocks(pt[0:rows, :, :], col, col + w_, m)[:, :, :, 1, :],
                                      late(mask[0:rows, 0:w_], w_).unsqueeze(1).to_broadcast([rows, H, nb, m]),
                                      xp[tile][0:rows, 0:H * w_ // 2].rearrange("p (h b m) -> p h b m", h=H, m=m))
                return last

            def phase(stage, n, h, k, layer, done):
                if stage == "c_log" and k == 0:
                    done(V.tensor_scalar(z12[:, 0, 2 * h:2 * h + 2, :], zc[:, 1, 2 * h:2 * h + 2, :], CLAMP, None, ALU.min))
                elif stage == "c_log":
                    for hd in (2 * h, 2 * h + 1):
                        last = V.tensor_tensor_scan(zc[:, 2, hd, :], c_("scan"), z12[:, 0, hd, :], 0.0, ALU.mult, ALU.add)
                    done(last)
                elif stage == "c_first" and k == 0:
                    b = zc[:, 2, h, :].rearrange("p (b m) -> p b m", m=4)
                    z = z12[:, 0, h, :].rearrange("p (b m) -> p b m", m=4)
                    done(V.tensor_tensor(z, b, b[:, :, 0:1].to_broadcast([P, T // 4, 4]), ALU.subtract))
                elif stage == "c_first":
                    V.tensor_tensor(z12[:, 0, h, :], z12[:, 0, h, :], zc[:, 0, h, :], ALU.mult)
                    done(V.tensor_tensor(z12[:, 1, h, :], z12[:, 1, h, :], zc[:, 1, h, :], ALU.mult))
                elif stage == "c_level" and k == 1:
                    done(distances((LEVELS + (P,))[h], (h + 1) % 2))
                elif stage == "c_level" and k == 3:
                    done(take(h))
                elif stage == "c_level":
                    done(apply_qk((LEVELS + (P,))[h], (h + 1) % 2))
                elif stage == "c_last" and k == 1:
                    b = zc[:, 2, :, :]
                    V.tensor_tensor(z12[:, 1, :, 0:SEQ], b[:, :, SEQ - 1:SEQ].to_broadcast([P, H, SEQ]),
                                    b[:, :, 0:SEQ], ALU.subtract)
                    s = b[:, :, SEQ:T].rearrange("p h (b t) -> p h b t", t=DS)
                    done(V.tensor_tensor(z12[:, 1, :, SEQ:T].rearrange("p h (b t) -> p h b t", t=DS),
                                         s[:, :, :, DS - 1:DS].to_broadcast([P, H, NB, DS]), s, ALU.subtract))
                elif stage == "c_last" and k == 3:
                    done(V.tensor_copy(pt[:, :, P:2 * P], xp[0][:, :].rearrange("p (h t) -> p h t", h=H)))
                elif stage == "c_last":
                    V.tensor_tensor(z12[:, 1, :, :], z12[:, 1, :, :], zc[:, 1, :, :], ALU.mult)
                    done(V.tensor_tensor(qw[:, :, :], qw[:, :, :], zc[:, 0, :, SEQ:T], ALU.mult))
                elif stage == "a_gate" and k == 1:
                    V.tensor_copy(iff[:, 0:2, :], xp[0][:, 0:16].rearrange("p (a c) -> p a c", a=2))
                    done(V.tensor_copy(iff[0:NS, 2, :], xp[0][0:NS, 16:24]))
                elif stage == "a_gate":
                    done(V.scalar_tensor_tensor(out=af[:, :, :], in0=iff[:, :, H:2 * H], scalar=0.0, in1=af[:, :, :],
                                                op0=ALU.min, op1=ALU.subtract))
                elif stage == "a_cum":
                    b = xp[1][:, 0:12].rearrange("p (a c) -> p a c", a=3)
                    V.tensor_tensor(gb[:, :, 0:H], iff[:, :, 0:H], b, ALU.subtract)
                    done(V.tensor_copy(gb[:, :, H:2 * H], b))
                elif stage == "a_row":
                    link(V.tensor_copy(row[:, 0, :], xp[2][0:H, 0:T]))
                    V.tensor_tensor_scan(row[:, 1, 0:SEQ], row[:, 0, 0:SEQ], row[:, 0, 0:SEQ], 0.0, ALU.max, ALU.max)
                    for b in range(NB):
                        s = slice(SEQ + b * DS, SEQ + (b + 1) * DS)
                        last = V.tensor_tensor_scan(row[:, 1, s], row[:, 0, s], row[:, 0, s], m0s[:, layer, b:b + 1],
                                                    ALU.max, ALU.max)
                    link(last)
                    if layer:
                        dve.wait_ge(small_out, 16 * 3 * layer)
                    link(V.tensor_tensor(row[:, 0, :], row[:, 1, :], xp[3][0:H, 0:T], ALU.add))
                    V.tensor_copy(mou[:, 0:1], row[:, 0, SEQ - 1:SEQ])
                    V.tensor_copy(mou[:, 1:1 + NB], row[:, 0, SEQ + DS - 1:T:DS])
                    link(V.tensor_tensor(per_seq(wi[:, :]), m0s[:, layer, :].unsqueeze(2).to_broadcast([H, NB, DS]),
                                         per_seq(row[:, 1, SEQ:T]), ALU.subtract))
                    done(V.tensor_scalar(row[:, 1, :], row[:, 1, :], -1.0, None, ALU.mult))
                elif stage == "a_score" and k == 3:
                    V.tensor_tensor(pt[:, h, 0:384], xp[1][:, 0:384], ee[:, 0:384], ALU.mult)
                    done(V.tensor_tensor(pt[0:NS, h, 384:SP4], xp[1][0:NS, 384:SP4], ee[0:NS, 384:SP4], ALU.mult))
                elif stage == "a_score":
                    V.tensor_copy(dec[:, h, :], xp[2][:, T + DS - 1:384:DS])
                    link(V.tensor_tensor(qw[:, h, :], xp[2][:, T:384], za[:, 0, h, SEQ:T], ALU.mult))
                    done(V.tensor_tensor(per_seq(qn[:, :]), per_seq(qw[:, h, :]),
                                         n0s[:, layer, h, :].unsqueeze(2).to_broadcast([P, NB, DS]), ALU.mult))
                elif stage == "b_rope":
                    for i in range(2):
                        V.tensor_tensor((sq, rs)[i][:, :], xp[i][:, 0:T], c_("sin"), ALU.mult)
                        last = V.tensor_tensor(zc[:, i, h, :], zc[:, i, h, :], c_("cos"), ALU.mult)
                    link(last)
                    V.tensor_tensor(zc[:, 1, h, :], zc[:, 1, h, :], rs[:, :], ALU.add)
                    link(V.tensor_tensor(zc[:, 0, h, :], zc[:, 0, h, :], sq[:, :], ALU.add))
                    done(V.tensor_tensor(qw[:, h, :], zc[:, 0, h, SEQ:T], c_("inter")[:, h * NS:(h + 1) * NS], ALU.mult))
                elif stage == "b_score":
                    d = c_("dtab").rearrange("p (h c) -> p h c", h=H)[:, h, :]
                    V.tensor_tensor(pt[:, h, 0:256], xp[1][:, 0:256], d[:, 0:256], ALU.mult)
                    V.tensor_tensor(pt[:, h, 256:384], xp[1][:, 256:384], d[:, 0:128], ALU.mult)
                    done(V.tensor_tensor(pt[0:NS, h, 384:SP4], xp[1][0:NS, 384:SP4], d[0:NS, 256:320], ALU.mult))
                elif stage == "num" and n == "A":
                    link(V.tensor_tensor(sq[:, :], sq[:, :], xp[2][:, 0:T], ALU.max))
                    link(V.reciprocal(sq[:, :], sq[:, :]))
                    done(V.tensor_tensor(hh[:, :], xp[3][:, 0:T], sq[:, :], ALU.mult))
                elif stage in ("num", "a_sq"):
                    if n == "A":
                        ends, mask = (ee[:, 255:256], ee[:, 383:384]), ee[0:NS, 384 + DS - 1:SP4:DS]
                    elif n == "B":
                        toend = c_("toend")[:, 2 * h:2 * h + 2]
                        ends, mask = (toend[:, 0:1], toend[:, 1:2]), c_("vmask", NS)[:, h * NB:(h + 1) * NB]
                    else:
                        ends, mask = None, c_("seqmask", NS)
                    if ends:
                        for i in range(2):
                            V.tensor_scalar(vw[:, i, :], v_of(n, h, i), ends[i], None, ALU.mult)
                    done(V.tensor_tensor(vm[:, :, :], v_of(n, h, 2).unsqueeze(1).to_broadcast([NS, NB, P]),
                                         mask.unsqueeze(2).to_broadcast([NS, NB, P]), ALU.mult))
                elif stage == "b_mean":
                    done(V.tensor_tensor(hh[:, :], hh[:, :], xp[4][:, 0:T], ALU.subtract))
                elif stage == "fin" and k == 3:
                    w_ = prm[:, layer, PN + 4 * "ABC".index(n) + h:PN + 4 * "ABC".index(n) + h + 1]
                    link(V.scalar_tensor_tensor(out=hh[:, :], in0=hh[:, :], scalar=w_, in1=rs[:, :],
                                                op0=ALU.mult, op1=ALU.mult))
                    gate = za[:, 2, h, :] if n == "A" else zc[:, 3, h, :]
                    link(V.tensor_tensor(hh[:, :], hh[:, :], gate, ALU.mult))
                    done(split_y(n, h, hh[:, :]))
                elif stage == "fin":
                    j = state_of(n, h)
                    V.tensor_copy(pst[:, j % 2, :], xp[0][:, 0:P])
                    if n == "A":
                        V.tensor_copy(nou[:, h, 0:1], xp[0][:, P:P + 1])
                        link(V.tensor_tensor(nou[:, h, 1:1 + NB], n0s[:, layer, h, :], dec[:, h, :], ALU.mult))
                        V.tensor_tensor(nou[:, h, 1:1 + NB], nou[:, h, 1:1 + NB], xp[0][:, P + 1:P + 1 + NB], ALU.add)
                    for b in range(NB):
                        new = xp[1 + b // 4][:, (b % 4) * P:(b % 4 + 1) * P]
                        keep = (1.0 - 2.0 ** (-5 - h)) ** DS if n == "B" else dec[:, h, b:b + 1]
                        last = V.scalar_tensor_tensor(out=s0[:, j % 2, b, :], in0=s0[:, j % 2, b, :], scalar=keep,
                                                      in1=new, op0=ALU.mult, op1=ALU.add)
                    done(last)
                elif stage == "conv":
                    if layer and h == 0:
                        dve.wait_ge(small_out, 16 * 3 * layer)
                    tap = lambda j: prm[:, layer, PCW + 4 * j + h:PCW + 4 * j + h + 1]
                    up, us = ud[:, h, 0:SEQ + 2], sample_u(h)
                    y = ee[:, 0:T]
                    yp, ys = y[:, 0:SEQ], per_seq(y[:, SEQ:T])
                    V.tensor_scalar(yp, up[:, 0:SEQ], tap(0), None, ALU.mult)
                    link(V.tensor_scalar(ys, us[:, :, 0:DS], tap(0), None, ALU.mult))
                    for j in (1, 2):
                        V.scalar_tensor_tensor(out=yp, in0=up[:, j:j + SEQ], scalar=tap(j), in1=yp, op0=ALU.mult, op1=ALU.add)
                        link(V.scalar_tensor_tensor(out=ys, in0=us[:, :, j:j + DS], scalar=tap(j), in1=ys,
                                                    op0=ALU.mult, op1=ALU.add))
                    V.tensor_tensor(bd[:, h, :], y, bd[:, h, :], ALU.mult)
                    V.tensor_copy(cou[:, h, 0, :], up[:, SEQ:SEQ + 2])
                    done(V.tensor_copy(cou[:, h, 1:1 + NB, :], us[:, :, DS:DS + 2]))
                elif stage == "d_split":
                    z = slice(2 * h, 2 * h + 2)
                    link(V.tensor_copy(yh[:, Y_PAIR["D"], z, :], bd[:, z, :]))
                    done(V.tensor_tensor(yl[:, Y_PAIR["D"], z, :], bd[:, z, :], yh[:, Y_PAIR["D"], z, :].bitcast(F32),
                                         ALU.subtract))

            def split_y(n, h, y):
                pair = Y_PAIR[n]
                link(V.tensor_copy(yh[:, pair, h, :], y))
                return V.tensor_tensor(yl[:, pair, h, :], y, yh[:, pair, h, :].bitcast(F32), ALU.subtract)

            def add_block(layer, which, m):
                total = hh if m < HALF else sq
                first = m in (1, HALF + 1)
                ins = V.tensor_tensor(total[:, :], mix[:, m - 1, :] if first else total[:, :], mix[:, m, :], ALU.add)
                if m in (HALF - 1, KD - 2):
                    ins.then_inc(ln_sum, 1)
                else:
                    link(ins)

            def add_squares(layer, which, blocks_):
                q = 2 * layer + which
                for j in blocks_:
                    dve.wait_ge(ln_sq, KD * q + j + 1)
                    if j > 1:
                        dve.wait_ge(ln_added, (KD - 2) * q + j - 1)
                    V.tensor_tensor(rs[:, :], tt[:, 0, :] if j == 1 else rs[:, :], tt[:, j % BANKS, :],
                                    ALU.add).then_inc(ln_added, 1)

            def center(layer, which, m):
                q = 2 * layer + which
                if m == HALF:
                    dve.wait_ge(ln_half, q + 1)
                    for j in range(HALF + 1):
                        V.scalar_tensor_tensor(out=mix[:, j, :], in0=xp[0][:, 0:T], scalar=-1.0 / HALF, in1=mix[:, j, :],
                                               op0=ALU.mult, op1=ALU.add).then_inc(ln_center, 1)
                    V.tensor_scalar(hh[:, :], xp[0][:, 0:T], 1.0 / HALF, None, ALU.mult).then_inc(ln_center, 1)
                    dve.wait_ge(ln_center, (HALF + 2) * (q + 1))
                elif m < KD - 1:
                    add_block(layer, which, m)
                    add_squares(layer, which, (1, 2) if m == HALF + 1 else (3, 4, 5))
                else:
                    add_squares(layer, which, (6,))

            def layer_norm(layer, which):
                q = 2 * layer + which
                dve.wait_ge(ln_shift, 2 * (q + 1))
                dve.wait_ge(ln_sqsum, q + 1)
                V.scalar_tensor_tensor(out=rs[:, :], in0=xp[2][:, 0:T], scalar=1.0 / DM, in1=hh[:, :],
                                       op0=ALU.mult, op1=ALU.subtract).then_inc(ln_var, 1)
                for m in range(SHIFT_DVE):
                    last = V.tensor_tensor(mix[:, m, :], mix[:, m, :], sq[:, :], ALU.subtract)
                link(last)
                dve.wait_ge(ln_rstd, q + 1)
                last = q == 2 * DEPTH - 1
                for m in range(KD):
                    if m >= SHIFT_DVE:
                        dve.wait_ge(ln_shifted, (KD - SHIFT_DVE) * q + m - SHIFT_DVE + 1)
                    gain = prm[:, layer, PLN + 16 * which + m:PLN + 16 * which + m + 1]
                    V.scalar_tensor_tensor(out=mix[:, m, :], in0=mix[:, m, :], scalar=gain, in1=rs[:, :],
                                           op0=ALU.mult, op1=ALU.mult).then_inc(ln_scaled, 1)
                    if m and not last:
                        low_part(layer, which, q, m - 1)
                if not last:
                    low_part(layer, which, q, KD - 1)

            def low_part(layer, which, q, m):
                bias = prm[:, layer, PLN + 16 * which + 8 + m:PLN + 16 * which + 9 + m]
                dve.wait_ge(x_hi, KD * (q + 1) + m + 1)
                V.scalar_tensor_tensor(out=xl[:, m, :], in0=mix[:, m, :], scalar=bias, in1=xh[:, m, :].bitcast(F32),
                                       op0=ALU.add, op1=ALU.subtract).then_inc(x_lo, 1)

            act_parts, splits = [0], [0]
            dve.wait_ge(setup_pool, 1)
            for layer in range(DEPTH):
                tile = 0
                for item, rows in zip(SCHEDULE, PHASE_TABLE):
                    if item[0] == "slot":
                        slot_i = item[1]
                        earlier = range(tile - tiles_in(slot_i - 1) if slot_i else 0, tile)
                        if not crossed(slot_i):
                            for i in earlier:
                                evict_second(layer, i)
                        split_hi(layer * NSLOT + slot_i + RING)
                        for _ in range(tiles_in(item[1])):
                            if frees(LTILES[tile]) == "dve":
                                n_free = freed("dve", layer * NTILE + tile - (tiles_in(slot_i - 1) if crossed(slot_i) else 0))
                                if n_free:
                                    dve.wait_ge(tile_free["dve"], n_free)
                                if LTILES[tile][0] == "br":
                                    dve.wait_ge(tile_free["act"], freed("act", layer * NTILE + tile))
                            evict(layer, tile)
                            tile += 1
                            if LTILES[tile - 1][0:2] == ("br", "B"):
                                dve.wait_ge(tile_free["dve"], freed("dve", layer * NTILE + tile))
                                split_mix(LTILES[tile - 1][2])
                        if crossed(slot_i):
                            for i in earlier:
                                evict_second(layer, i)
                        if layer == 0 and slot_i == 2 * H - 1:
                            dve.wait_ge(const_in, 16 * (PARTS + 1))
                            dve.wait_ge(small_in, 64)
                            V.tensor_copy(negb[:, :], ee[:, :]).then_inc(setup_dve, 1)
                            dve.wait_ge(setup_dve, 2)
                        m, which = norm_input(slot_i)
                        if m is not None and m:
                            dve.wait_ge(tile_free["dve"], freed("dve", layer * NTILE + tile))
                            if m < HALF:
                                add_block(layer, which, m)
                            else:
                                center(layer, which, m)
                        if ends_norm(item[1]) is not None:
                            layer_norm(layer, ends_norm(item[1]))
                        continue
                    for k, (engine, before, _) in enumerate(rows):
                        if engine != "dve":
                            continue
                        follow(dve, layer, before)
                        if k == 0:
                            settled(dve, layer, tile, slot_i)
                        phase(*item[1:], k, layer, lambda ins: ins.then_inc(mix_done["dve"], 1))

        @block.tensor
        def _(pe):
            M = nc.tensor.matmul

            def dense(out, hi, lo, xhi, xlo, start, stop):
                M(out, hi, xhi, start=start, stop=False)
                M(out, hi, xlo, start=False, stop=False)
                return M(out, lo, xhi, start=False, stop=stop)

            def tile_bank(layer, i):
                g = layer * NTILE + i
                if g >= BANKS:
                    e = frees(LTILES[(g - BANKS) % NTILE])
                    pe.wait_ge(tile_free[e], freed(e, g - BANKS + 1))
                return gps[g % BANKS]

            def pair(layer, i, tile):
                c = layer * NSLOT + i
                pe.wait_ge(lo_done, c + 1)
                out = [None, None]
                step = HALF if SLOTS[i][0] == "out" else 1
                for k0 in range(0, KD, step):
                    for j in range(2):
                        if k0 == 0:
                            out[j] = tile_bank(layer, tile - 1 + j)[:, 0:T]
                        hi, lo = whi[:, (c - 1 + j) % RING], wlo[:, (c - 1 + j) % RING]
                        for k in range(k0, k0 + step):
                            if SLOTS[i][0] == "out":
                                pe.wait_ge(mix_split, 2 * KD * layer + 2 * k + 2)
                                xhi, xlo = ah[:, k, :], al[:, k, :]
                            else:
                                pe.wait_ge(x_lo, KD * (2 * layer + (i > 1)) + k + 1)
                                xhi, xlo = xh[:, k, :], xl[:, k, :]
                            last = dense(out[j], hi[:, k, :], lo[:, k, :], xhi, xlo, k == 0, k == KD - 1)
                        if k == KD - 1 and j == 0:
                            last.then_inc(slot_done, 1)
                if turns_values(i):
                    last = turn_values(layer, i, tile)
                last.then_inc(slot_done, 1)

            def turn_values(layer, i, tile):
                bank = tile_bank(layer, tile + 1)
                if layer == 0 and i == 1:
                    pe.wait_ge(first_in, 32)
                pe.wait_ge(tile_free["act"], freed("act", layer * NTILE + tile))
                return turn(bank, vf[:, SLOTS[i - 1][2] % 2, :])

            def slot(layer, i, tile):
                c = layer * NSLOT + i
                pe.wait_ge(lo_done, c + 1)
                kind, a, b = SLOTS[i]
                hi, lo = whi[:, c % RING], wlo[:, c % RING]
                if kind == "br":
                    if b == 0:
                        pe.wait_ge(mix_done["dve"], layer * PHASES_PER_LAYER["dve"] + mixer_end(a))
                    pair = Y_PAIR[a]
                    for j in range(2):
                        out = tile_bank(layer, tile + j)[:, 0:T]
                        for k in range(H):
                            last = dense(out, hi[:, 4 * j + k, :], lo[:, 4 * j + k, :], yh[:, pair, k, :],
                                         yl[:, pair, k, :], k == 0, k == H - 1)
                    last.then_inc(slot_done, 1)
                    return
                if kind == "down":
                    out = tile_bank(layer, tile)[:, 0:T] if b == 0 else gps[(layer * NTILE + tile) % BANKS][:, 0:T]
                else:
                    out = tile_bank(layer, tile)[:, 0:T]
                for k in range(KD):
                    if kind == "down":
                        f = KD * b + k
                        if a == 0:
                            up = LTILES.index(("up", f, 0))
                            pe.wait_ge(tile_free["dve"], freed("dve", layer * NTILE + up + 1))
                        xhi, xlo = ah[:, f, :], al[:, f, :]
                        first, end = f == 0, f == KF - 1
                    elif kind == "out":
                        xhi, xlo = ah[:, k, :], al[:, k, :]
                        first, end = k == 0, k == KD - 1
                    else:
                        if layer == 0 and i == 0:
                            pe.wait_ge(x_lo, k + 1)
                        xhi, xlo = xh[:, k, :], xl[:, k, :]
                        first, end = k == 0, k == KD - 1
                    last = dense(out, hi[:, k, :], lo[:, k, :], xhi, xlo, first, end)
                if turns_values(i):
                    last = turn_values(layer, i, tile)
                last.then_inc(slot_done, 1)

            def half_mean(layer, which):
                q = 2 * layer + which
                pe.wait_ge(ln_sum, 2 * q + 1)
                M(xp[0][:, 0:T], ones[:, 1, :], hh[:, :], start=True, stop=True).then_inc(ln_half, 1)

            def layer_norm(layer, which):
                q = 2 * layer + which
                pe.wait_ge(ln_sum, 2 * q + 2)
                M(xp[1][:, 0:T], ones[:, 1, :], sq[:, :], start=True, stop=False)
                centered(pe, layer, which, KD - 1)
                M(xp[1][:, 0:T], ones[:, 1, :], mix[:, KD - 1, :], start=False, stop=True).then_inc(ln_mean, 1)
                pe.wait_ge(ln_added, (KD - 2) * (q + 1))
                M(xp[2][:, 0:T], ones[:, 0, :], rs[:, :], start=True, stop=False)
                pe.wait_ge(ln_sq, KD * (q + 1))
                M(xp[2][:, 0:T], ones[:, 0, :], tt[:, (KD - 1) % BANKS, :], start=False, stop=True).then_inc(ln_sqsum, 1)

            def turn(out_bank, src):
                for i, (lo, n) in enumerate(TILES):
                    last = nc.tensor.transpose(out_bank[0:n, i * P:(i + 1) * P], src[:, lo:lo + n], ident)
                return last

            def scores(bank, n, h):
                q, k = q_of(n, h), k_of(n, h)
                M(bank[:, 0:256], k[:, 0:P], q[:, 0:SEQ], start=True, stop=False, skip_group_check=True)
                M(bank[:, 256:384], k[:, P:SEQ], q[:, P:SEQ], start=False, stop=False, skip_group_check=True)
                return M(bank[0:NS, 384:SP4], k[:, SEQ:T], q[:, SEQ:T], start=False, stop=True, skip_group_check=True)

            def weigh(bank, lhs, h):
                M(bank[:, 0:256], lhs(0), pt[:, h, 0:256], start=True, stop=False, skip_group_check=True)
                M(bank[:, P:SEQ], lhs(1), pt[:, h, 256:384], start=False, stop=False, skip_group_check=True)
                return M(bank[:, SEQ:T], lhs(2), pt[0:NS, h, 384:SP4], start=False, stop=False, skip_group_check=True)

            def phase(stage, n, h, layer, done):
                if stage in ("c_level", "c_last"):
                    if stage == "c_last":
                        for hd in range(H):
                            last = M(xp[0][:, hd * P:(hd + 1) * P], z12[:, 0, hd, 0:P], z12[:, 0, hd, P:SEQ],
                                     start=hd == 0, stop=hd == H - 1, skip_group_check=True)
                        done(last)
                        return
                    for i in range(3 if h <= 1 else 2):
                        lo, w_ = TILES[i]
                        for hd in range(H):
                            if h == 0:
                                last = M(xp[i][0:w_, hd * w_:(hd + 1) * w_], z12[:, 1, hd, lo:lo + w_],
                                         z12[:, 0, hd, lo:lo + w_], start=hd == 0, stop=hd == H - 1, skip_group_check=True)
                                continue
                            m = LEVELS[h - 1]
                            z = z12[:, h % 2, hd, lo:lo + w_]
                            out = xp[i][0:w_, hd * w_ // 2:(hd + 1) * w_ // 2].rearrange("p (b m) -> p b m", m=m)
                            last = M(out, z, z.rearrange("p (b two m) -> p b two m", two=2, m=m)[:, :, 1, :],
                                     start=hd == 0, stop=hd == H - 1, skip_group_check=True)
                    done(last)
                elif stage == "a_gate":
                    for i, (lo, w_) in enumerate(TILES):
                        last = nc.tensor.transpose(xp[0][0:w_, 8 * i:8 * i + 8], iff_fm[:, lo:lo + w_], ident[0:8, 0:8])
                    done(last)
                elif stage == "a_cum":
                    M(xp[1][:, 0:4], c_("tri"), af[:, 0, :], start=True, stop=False, skip_group_check=True)
                    M(xp[1][:, 4:8], ones[:, 0, :], af[:, 0, :], start=False, stop=False, skip_group_check=True)
                    M(xp[1][:, 4:8], c_("tri"), af[:, 1, :], start=False, stop=False, skip_group_check=True)
                    done(M(xp[1][:, 8:12], c_("trib"), af[:, 2, :], start=False, stop=True, skip_group_check=True))
                elif stage == "a_row":
                    for i in range(3):
                        nc.tensor.transpose(xp[2][0:H, i * P:(i + 1) * P], gb[:, i, 0:H], ident)
                        last = nc.tensor.transpose(xp[3][0:H, i * P:(i + 1) * P], gb[:, i, H:2 * H], ident)
                    done(last)
                elif stage == "a_score":
                    sel = c_("sel", H)[:, h * P:(h + 1) * P]
                    for j, (col, src) in enumerate(((slice(0, 256), slice(0, 256)), (slice(256, 384), slice(P, SEQ)),
                                                    (slice(384, SP4), slice(SEQ, T)))):
                        M(xp[0][:, col], sel, row[:, 1, src], start=j == 0, stop=False, skip_group_check=True)
                    M(xp[0][:, 0:SP4], idb[:, :], negb[:, :], start=False, stop=True, skip_group_check=True)
                    scores(xp[1], n, h)
                    M(xp[2][:, 0:T], sel, row[:, 0, :], start=True, stop=False, skip_group_check=True)
                    done(M(xp[2][:, T:384], sel, wi[:, :], start=False, stop=True, skip_group_check=True))
                elif stage == "b_rope":
                    M(xp[0][:, 0:T], c_("perm"), zc[:, 0, h, :], start=True, stop=True)
                    done(M(xp[1][:, 0:T], c_("perm"), zc[:, 1, h, :], start=True, stop=True))
                elif stage == "b_score":
                    done(scores(xp[1], n, h))
                elif stage == "num":
                    j = layer * HEADS_PER_LAYER + state_of(n, h)
                    turn(xp[0], z12[:, 1, h, :] if n == "C" else k_of(n, h))
                    pe.wait_ge(s_in[j % 2], 16 * (j // 2 + 1))
                    weigh(xp[3], lambda i: v_of(n, h, i), h)
                    for b in range(NB):
                        s = slice(b * DS, (b + 1) * DS)
                        last = M(xp[3][:, SEQ + b * DS:SEQ + (b + 1) * DS], s0[:, j % 2, b, :], qw[:, h, s],
                                 start=False, stop=b == NB - 1, skip_group_check=True)
                    if n == "A":
                        weigh(xp[4], lambda i: ones[0:TILES[i][1], 0, :], h)
                        last = M(xp[4][:, SEQ:T], ones[:, 0, :], qn[:, :], start=False, stop=True, skip_group_check=True)
                    done(last)
                elif stage == "b_mean":
                    done(M(xp[4][:, 0:T], ones[:, 1, :], hh[:, :], start=True, stop=True))
                elif stage == "fin":
                    for i in range(2):
                        v = v_of(n, h, i) if n == "C" else vw[:, i, :]
                        M(xp[0][:, 0:P], kt[:, i, :], v, start=i == 0, stop=False, skip_group_check=True)
                    if n == "A":
                        for i in range(2):
                            M(xp[0][:, P:P + 1], kt[:, i, :], ee[:, (255, 383)[i]:(256, 384)[i]], start=False, stop=False,
                              skip_group_check=True)
                        M(xp[0][:, P + 1:P + 1 + NB], kt[0:NS, 2, :], ee[0:NS, 384 + DS - 1:SP4:DS], start=False,
                          stop=True, skip_group_check=True)
                    for i in range(2):
                        M(xp[1 + i][:, :], kt[0:NS, 2, :], vm[:, 4 * i:4 * i + 4, :], start=True, stop=True)
                    done(M(xp[4][:, 0:T], ones[:, 0, :], sq[:, :], start=True, stop=True))

            stages = 0
            for layer in range(DEPTH):
                tile = 0
                for item, rows in zip(SCHEDULE, PHASE_TABLE):
                    if item[0] == "slot":
                        slot_i = i = item[1]
                        kind, a, b = SLOTS[i]
                        if paired(i) and (layer or i > 1):
                            pair(layer, i, tile)
                        elif not (i + 1 < NSLOT and paired(i + 1)) or layer == 0 and i == 0:
                            slot(layer, i, tile)
                        tile += tiles_in(i)
                        if kind in ("out", "down") and (a, b) == (HALF, 0):
                            half_mean(layer, int(kind == "down"))
                        if ends_norm(i) is not None:
                            layer_norm(layer, ends_norm(i))
                        continue
                    for k, (engine, before, _) in enumerate(rows):
                        if engine != "pe":
                            continue
                        if stages == 0:
                            pe.wait_ge(setup_pool, 1)
                            pe.wait_ge(setup_dve, 2)
                        stages += 1
                        follow(pe, layer, before)
                        settled(pe, layer, tile, slot_i)
                        phase(*item[1:], layer, lambda ins: ins.then_inc(mix_done["pe"], 1))


def constants():
    import numpy as np
    f = np.float64
    s, t = np.arange(P)[:, None], np.arange(P)[None, :]
    gamma = 1.0 - 2.0 ** (-5.0 - np.arange(H, dtype=f))
    c = np.zeros((P, NCONST + SP4), np.float32)

    def put(name, value, rows=P):
        off, n = CONST_AT[name]
        c[:rows, off:off + n] = np.asarray(value).reshape(rows, n)

    j, seq = np.arange(NS) % DS, np.arange(NS) // DS
    own = seq[:, None] == seq[None, :]
    see = own & (j[:, None] <= j[None, :])
    put("ident", s == t)
    put("perm", (s + P // 2) % P == t)
    put("tri", s <= t)
    trib = np.zeros((P, P))
    trib[:NS, :NS] = see
    put("trib", trib)
    put("diag", (s // 4 == t // 4) & (s <= t))
    for m in LEVELS:
        put(f"lv{m}", (s // (2 * m) == t // (2 * m)) & (s % (2 * m) < m) & (t % (2 * m) >= m))
    d = np.zeros((P, H, 320))
    for h in range(H):
        d[:, h, 0:P] = np.where(s <= t, gamma[h] ** np.maximum(t - s, 0).astype(f), 0)
        d[:, h, P:2 * P] = gamma[h] ** (t + P - s).astype(f)
        d[:NS, h, 2 * P:] = np.where(see, gamma[h] ** np.maximum(j[None, :] - j[:, None], 0).astype(f), 0)
    put("dtab", d)
    put("inter", np.broadcast_to(gamma[:, None] ** (j + 1.0)[None, :], (P, H, NS)))
    put("toend", np.stack([gamma[None, :] ** (SEQ - 1.0 - P * i - s) for i in range(2)], axis=2))
    in_seq = seq[:, None] == np.arange(NB)[None, :]
    put("seqmask", in_seq, NS)
    put("vmask", in_seq[:, None, :] * (gamma[None, :] ** (DS - 1.0 - j)[:, None])[:, :, None], NS)
    half = P // 2
    inv = np.float32(10000.0) ** (-np.arange(half, dtype=np.float32) / np.float32(half))
    pos = np.concatenate([np.arange(SEQ), 2048 + j]).astype(np.float32)
    ang = (pos[None, :] * inv[:, None]).astype(np.float32).astype(f)
    put("cos", np.concatenate([np.cos(ang), np.cos(ang)]))
    put("sin", np.concatenate([-np.sin(ang), np.sin(ang)]))
    scan = np.ones((P, T))
    scan[:, [0] + list(range(SEQ, T, DS))] = 0
    put("scan", scan)
    put("sel", (np.arange(H)[:, None, None] == np.arange(H)[None, :, None]) & np.ones((1, 1, P), bool), H)
    neg = np.zeros((P, SP4))
    neg[:, 0:P] = np.where(s <= t, 0, NEG)
    neg[:, 256:384] = neg[:, 0:P]
    neg[:NS, 384:] = np.where(see, 0, NEG)
    c[:, NCONST:] = neg
    return c


def kernel(x_prompt, x_sample, state_mlstm_C, state_mlstm_n, state_mlstm_m, state_ret, state_hgrn, state_conv,
           w_in, b_mlstm_gate, norm_a, norm_b, norm_c, lb_c, conv_w, w_branch, w_gate, b_gate, w_out, ln1_g, ln1_b,
           ln2_g, ln2_b, w_up, w_down):
    import concourse.bacc as bacc
    import numpy as np
    from concourse.bass_utils import run_bass_kernel_spmd as run

    a = lambda v: np.asarray(v)
    x_prompt, x_sample = a(x_prompt), a(x_sample)
    w_in, w_gate, w_branch, w_out, w_up, w_down = map(a, (w_in, w_gate, w_branch, w_out, w_up, w_down))

    w = np.empty((DEPTH, NSLOT, P, KD, P), np.float32)
    for layer in range(DEPTH):
        for i, (kind, p, q) in enumerate(SLOTS):
            if p == "ifA":
                src = np.zeros((DM, P), np.float32)
                src[:, 0:2 * H] = w_in[layer][:, IN_COL[p]:IN_COL[p] + 2 * H]
            elif kind == "in":
                src = w_in[layer][:, IN_COL[p] + q * P:IN_COL[p] + (q + 1) * P]
            elif kind == "gate":
                col = DM * BRANCH[p] + q * P
                src = w_gate[layer][:, col:col + P]
            elif kind == "br":
                src = w_branch[layer, BRANCH[p]][:, q * P:(q + 2) * P]
                w[layer, i] = src.reshape(H, P, 2, P).transpose(1, 2, 0, 3).reshape(P, KD, P)
                continue
            elif kind == "out":
                src = w_out[layer][:, p * P:(p + 1) * P]
            elif kind == "up":
                src = w_up[layer][:, p * P:(p + 1) * P]
            else:
                src = w_down[layer][q * DM:(q + 1) * DM, p * P:(p + 1) * P]
            w[layer, i] = src.reshape(KD, P, P).transpose(1, 0, 2)

    x = np.concatenate([x_prompt[0], x_sample.reshape(NS, DM)])
    x = np.ascontiguousarray(x.T.reshape(KD, P, T).transpose(1, 0, 2))
    col = lambda v: a(v).reshape(DEPTH, -1, P).transpose(2, 0, 1)
    par = np.concatenate([col(norm_a), col(norm_b), col(norm_c), col(conv_w), col(b_gate), col(ln1_g), col(ln1_b),
                          col(ln2_g), col(ln2_b), col(lb_c)], axis=2)
    ifb = a(b_mlstm_gate).T
    st = np.concatenate([a(state_hgrn), a(state_mlstm_C), a(state_ret)], axis=2).transpose(0, 2, 3, 1, 4)
    n0 = a(state_mlstm_n).transpose(3, 0, 2, 1)
    m0 = a(state_mlstm_m).transpose(2, 0, 1)
    cb = a(state_conv).reshape(DEPTH, NB, 2, H, P).transpose(4, 0, 3, 1, 2)

    nc = bacc.Bacc("TRN2", target_bir_lowering=False, num_devices=1)
    arrays, args = {}, []
    for name, v in (("w", w), ("x", x), ("cst", constants()), ("par", par), ("ifb", ifb), ("st", st), ("n0", n0),
                    ("m0", m0), ("cb", cb)):
        v = np.ascontiguousarray(v)
        arrays["in_" + name] = v
        args.append(nc.dram_tensor("in_" + name, v.shape, F32, kind="ExternalInput").ap())
    outs = {"y": (P, KD, T), "sp": (DEPTH, HEADS_PER_LAYER, P, P), "ss": (DEPTH, HEADS_PER_LAYER, P, NB, P),
            "n": (DEPTH, P, H, 1 + NB), "m": (DEPTH, H, 1 + NB), "c": (DEPTH, P, H, 1 + NB, 2)}
    for name, shape in outs.items():
        args.append(nc.dram_tensor("out_" + name, shape, F32, kind="ExternalOutput").ap())
    trunk(nc, *args)
    r = run(nc, [arrays], core_ids=[0]).results[0]
    y, sp, ss, n, m, c = (np.asarray(r["out_" + name]) for name in outs)

    y = y.transpose(2, 1, 0).reshape(T, DM)
    ss = ss.transpose(0, 3, 1, 2, 4)
    sp = sp[:, None]
    n = n.transpose(0, 3, 2, 1)
    m = m.transpose(0, 2, 1)
    c = c.transpose(0, 3, 4, 2, 1).reshape(DEPTH, 1 + NB, 2, H * P)
    copy = np.ascontiguousarray
    return (copy(y[:SEQ][None]), copy(y[SEQ:].reshape(NB, DS, DM)),
            copy(sp[:, :, 4:8]), copy(n[:, :1]), copy(m[:, :1]), copy(sp[:, :, 8:12]), copy(sp[:, :, 0:4]), copy(c[:, :1]),
            copy(ss[:, :, 4:8]), copy(n[:, 1:]), copy(m[:, 1:]), copy(ss[:, :, 8:12]), copy(ss[:, :, 0:4]), copy(c[:, 1:]))
```
